# Optimizing a Trainium2 kernel written in Bass

```python
import math
import jax, jax.numpy as jnp
from jax import lax
import numpy as np

D_MODEL = 1024
BATCH = 1
SEQ = 512
DEPTH = 2

N_MIXERS = 2
N_NSA_LAYERS = (DEPTH + N_MIXERS - 1) // N_MIXERS
N_DIFF_LAYERS = DEPTH // N_MIXERS

REL_BUCKETS = 32
REL_MAX_DIST = 128
N_BIAS_MAPS = 16

NSA_HEADS = 16
NSA_GROUPS = 4
NSA_HPG = NSA_HEADS // NSA_GROUPS
NSA_HEAD_DIM = D_MODEL // NSA_HEADS
NSA_WIDTH = NSA_HEADS * NSA_HEAD_DIM
NSA_KV = NSA_GROUPS * NSA_HEAD_DIM
CMP_BLOCK = 32
CMP_STRIDE = 16
CMP_HIDDEN = 2 * NSA_HEAD_DIM
SEL_BLOCK = 64
SEL_TOPK = 8
WINDOW = 512
NSA_QBLOCK = 64
NSA_SPLIT_SIZES = [NSA_WIDTH] + [NSA_KV] * 6 + [3 * NSA_HEADS, NSA_WIDTH]
NSA_IN = sum(NSA_SPLIT_SIZES)

DIFF_HEADS = 8
DIFF_HALF = D_MODEL // (2 * DIFF_HEADS)
DIFF_VDIM = 2 * DIFF_HALF
DIFF_WIDTH = DIFF_HEADS * DIFF_VDIM
DIFF_IN = 4 * DIFF_WIDTH
DIFF_QBLOCK = 128

NEG = -1e30
BIG = 1e9
EPS = 1e-6


def rmsnorm(x, g):
    xf = x.astype(jnp.float32)
    y = xf * lax.rsqrt(jnp.mean(xf * xf, axis=-1, keepdims=True) + EPS)
    return (y * g.astype(jnp.float32)).astype(x.dtype)

def rel_bucket(dist):
    n = jnp.maximum(dist, 0)
    max_exact = REL_BUCKETS // 2
    nf = jnp.maximum(n, 1).astype(jnp.float32)
    large = max_exact + (jnp.log(nf / max_exact) / math.log(REL_MAX_DIST / max_exact)
                         * (REL_BUCKETS - max_exact)).astype(jnp.int32)
    large = jnp.minimum(large, REL_BUCKETS - 1)
    return jnp.where(n < max_exact, n, large)

def compress(kv, pe, w1, w2):
    b, s, g, dh = kv.shape
    nc = (s - CMP_BLOCK) // CMP_STRIDE + 1
    idx = jnp.arange(nc)[:, None] * CMP_STRIDE + jnp.arange(CMP_BLOCK)[None, :]
    blocks = kv[:, idx] + pe[None, None, :, None, :]
    flat = jnp.moveaxis(blocks, 3, 2).reshape(b, nc, g, CMP_BLOCK * dh)
    return jax.nn.silu(flat @ w1) @ w2

def nsa_mixer(u, table, w_in, pe_k, w1_k, w2_k, pe_v, w1_v, w2_v, w_out):
    b, s, _ = u.shape
    G, J, dh = NSA_GROUPS, NSA_HPG, NSA_HEAD_DIM
    points = np.cumsum(NSA_SPLIT_SIZES)[:-1].tolist()
    q, kc, vc, ks, vs, kw, vw, gate, z = jnp.split(u @ w_in, points, axis=-1)
    q = q.reshape(b, s, G, J, dh) * (dh ** -0.5)
    kc, vc, ks, vs, kw, vw = [t.reshape(b, s, G, dh) for t in (kc, vc, ks, vs, kw, vw)]
    gate = jax.nn.sigmoid(gate.astype(jnp.float32)).reshape(b, s, G, J, 3)

    k_cmp = compress(kc, pe_k, w1_k, w2_k)
    v_cmp = compress(vc, pe_v, w1_v, w2_v)
    nc = k_cmp.shape[1]
    cmp_lo = jnp.arange(nc) * CMP_STRIDE
    cmp_end = cmp_lo + CMP_BLOCK - 1
    n_sel = s // SEL_BLOCK
    topk = min(SEL_TOPK, n_sel)
    sel_lo = jnp.arange(n_sel) * SEL_BLOCK
    overlap = jnp.clip(jnp.minimum(cmp_lo[:, None] + CMP_BLOCK, sel_lo[None, :] + SEL_BLOCK)
                       - jnp.maximum(cmp_lo[:, None], sel_lo[None, :]), 0).astype(jnp.float32) / CMP_BLOCK

    table_g = table.reshape(REL_BUCKETS, G, J)
    table_gt = jnp.transpose(table_g, (1, 0, 2))
    ks_t = jnp.transpose(ks, (0, 2, 1, 3))
    vs_t = jnp.transpose(vs, (0, 2, 1, 3))
    kw_pad = jnp.pad(kw, ((0, 0), (WINDOW, 0), (0, 0), (0, 0)))
    vw_pad = jnp.pad(vw, ((0, 0), (WINDOW, 0), (0, 0), (0, 0)))
    bi = jnp.arange(b)[:, None, None, None]
    gi = jnp.arange(G)[None, :, None, None]
    blk_n = jnp.arange(n_sel)

    def block(qb):
        start = qb * NSA_QBLOCK
        t = start + jnp.arange(NSA_QBLOCK)
        qblk = lax.dynamic_slice_in_dim(q, start, NSA_QBLOCK, axis=1)

        dist_c = t[:, None] - cmp_end[None, :]
        m_c = dist_c >= 0
        bias_c = jnp.transpose(table_g[rel_bucket(dist_c)], (2, 3, 0, 1))
        s_c = jnp.einsum('bqgjd,bcgd->bgjqc', qblk, k_cmp).astype(jnp.float32) + bias_c
        p_c = jax.nn.softmax(jnp.where(m_c, s_c, NEG), axis=-1) * jnp.any(m_c, axis=-1)[:, None]
        o_c = jnp.einsum('bgjqc,bcgd->bqgjd', p_c.astype(v_cmp.dtype), v_cmp)

        imp = jnp.einsum('bgjqc,cn->bgqn', p_c, overlap)
        cur = t // SEL_BLOCK
        forced = (blk_n[None, :] == 0) | (blk_n[None, :] == cur[:, None]) | (blk_n[None, :] == cur[:, None] - 1)
        future = blk_n[None, :] > cur[:, None]
        imp = jnp.where(forced, BIG, jnp.where(future, -BIG, imp))
        _, sel = lax.top_k(imp, topk)
        pos = (sel[..., None] * SEL_BLOCK + jnp.arange(SEL_BLOCK)).reshape(b, G, NSA_QBLOCK, topk * SEL_BLOCK)
        k_g = ks_t[bi, gi, pos]
        v_g = vs_t[bi, gi, pos]
        dist_s = t[None, None, :, None] - pos
        bias_s = jnp.moveaxis(table_gt[gi, rel_bucket(dist_s)], -1, 2)
        s_s = jnp.einsum('bqgjd,bgqkd->bgjqk', qblk, k_g).astype(jnp.float32) + bias_s
        p_s = jax.nn.softmax(jnp.where((dist_s >= 0)[:, :, None], s_s, NEG), axis=-1)
        o_s = jnp.einsum('bgjqk,bgqkd->bqgjd', p_s.astype(v_g.dtype), v_g)

        k_win = lax.dynamic_slice_in_dim(kw_pad, start, NSA_QBLOCK + WINDOW, axis=1)
        v_win = lax.dynamic_slice_in_dim(vw_pad, start, NSA_QBLOCK + WINDOW, axis=1)
        pos_w = start - WINDOW + jnp.arange(NSA_QBLOCK + WINDOW)
        dist_w = t[:, None] - pos_w[None, :]
        m_w = (dist_w >= 0) & (dist_w < WINDOW) & (pos_w[None, :] >= 0)
        bias_w = jnp.transpose(table_g[rel_bucket(dist_w)], (2, 3, 0, 1))
        s_w = jnp.einsum('bqgjd,bkgd->bgjqk', qblk, k_win).astype(jnp.float32) + bias_w
        p_w = jax.nn.softmax(jnp.where(m_w, s_w, NEG), axis=-1)
        o_w = jnp.einsum('bgjqk,bkgd->bqgjd', p_w.astype(v_win.dtype), v_win)
        return o_c, o_s, o_w

    o_c, o_s, o_w = lax.map(block, jnp.arange(s // NSA_QBLOCK))
    o_c, o_s, o_w = [jnp.moveaxis(o, 0, 1).reshape(b, s, G, J, dh) for o in (o_c, o_s, o_w)]
    o = gate[..., 0:1] * o_c + gate[..., 1:2] * o_s + gate[..., 2:3] * o_w
    o = o.astype(u.dtype).reshape(b, s, NSA_WIDTH) * jax.nn.silu(z)
    return o @ w_out

def diff_mixer(u, table, w_in, lq1, lk1, lq2, lk2, subln, w_out, lambda_init):
    b, s, _ = u.shape
    H, d, dv = DIFF_HEADS, DIFF_HALF, DIFF_VDIM
    q, k, v, z = jnp.split(u @ w_in, 4, axis=-1)
    q = q.reshape(b, s, H, 2, d) * (d ** -0.5)
    k = k.reshape(b, s, H, 2, d)
    v = v.reshape(b, s, H, dv)
    lam = (jnp.exp(jnp.sum(lq1.astype(jnp.float32) * lk1.astype(jnp.float32)))
           - jnp.exp(jnp.sum(lq2.astype(jnp.float32) * lk2.astype(jnp.float32))) + lambda_init)
    table_h = table.reshape(REL_BUCKETS, H, 2)
    kpos = jnp.arange(s)

    def block(qb):
        start = qb * DIFF_QBLOCK
        t = start + jnp.arange(DIFF_QBLOCK)
        qblk = lax.dynamic_slice_in_dim(q, start, DIFF_QBLOCK, axis=1)
        dist = t[:, None] - kpos[None, :]
        bias = jnp.transpose(table_h[rel_bucket(dist)], (2, 3, 0, 1))
        sc = jnp.einsum('bqhmd,bkhmd->bhmqk', qblk, k).astype(jnp.float32) + bias
        p = jax.nn.softmax(jnp.where(dist >= 0, sc, NEG), axis=-1)
        a = p[:, :, 0] - lam * p[:, :, 1]
        return jnp.einsum('bhqk,bkhe->bqhe', a.astype(v.dtype), v)

    o = lax.map(block, jnp.arange(s // DIFF_QBLOCK))
    o = jnp.moveaxis(o, 0, 1).reshape(b, s, H, dv)
    o = rmsnorm(o, subln.reshape(H, dv)) * (1.0 - lambda_init)
    o = o.reshape(b, s, DIFF_WIDTH) * jax.nn.silu(z)
    return o @ w_out

def first_inputs(seed: int = 0) -> dict:
    key = jax.random.key(seed)
    ks = jax.random.split(key, 20)
    nrm = jax.random.normal
    f32 = jnp.float32
    A, Bn = N_NSA_LAYERS, N_DIFF_LAYERS
    ld = CMP_BLOCK * NSA_HEAD_DIM
    return {
        "x": nrm(ks[0], (BATCH, SEQ, D_MODEL), f32),
        "rel_bias_table": 0.3 * nrm(ks[1], (REL_BUCKETS, N_BIAS_MAPS), f32),
        "norm_pre": 1.0 + 0.05 * nrm(ks[2], (DEPTH, D_MODEL), f32),
        "norm_post": 1.0 + 0.05 * nrm(ks[3], (DEPTH, D_MODEL), f32),
        "nsa_w_in": nrm(ks[4], (A, D_MODEL, NSA_IN), f32) * D_MODEL ** -0.5,
        "nsa_cmp_pe_k": 0.5 * nrm(ks[5], (A, CMP_BLOCK, NSA_HEAD_DIM), f32),
        "nsa_cmp_w1_k": nrm(ks[6], (A, ld, CMP_HIDDEN), f32) * ld ** -0.5,
        "nsa_cmp_w2_k": nrm(ks[7], (A, CMP_HIDDEN, NSA_HEAD_DIM), f32) * CMP_HIDDEN ** -0.5,
        "nsa_cmp_pe_v": 0.5 * nrm(ks[8], (A, CMP_BLOCK, NSA_HEAD_DIM), f32),
        "nsa_cmp_w1_v": nrm(ks[9], (A, ld, CMP_HIDDEN), f32) * ld ** -0.5,
        "nsa_cmp_w2_v": nrm(ks[10], (A, CMP_HIDDEN, NSA_HEAD_DIM), f32) * CMP_HIDDEN ** -0.5,
        "nsa_w_out": nrm(ks[11], (A, NSA_WIDTH, D_MODEL), f32) * NSA_WIDTH ** -0.5,
        "diff_w_in": nrm(ks[12], (Bn, D_MODEL, DIFF_IN), f32) * D_MODEL ** -0.5,
        "diff_lambda_q1": 0.1 * nrm(ks[13], (Bn, DIFF_HALF), f32),
        "diff_lambda_k1": 0.1 * nrm(ks[14], (Bn, DIFF_HALF), f32),
        "diff_lambda_q2": 0.1 * nrm(ks[15], (Bn, DIFF_HALF), f32),
        "diff_lambda_k2": 0.1 * nrm(ks[16], (Bn, DIFF_HALF), f32),
        "diff_subln": 1.0 + 0.05 * nrm(ks[17], (Bn, DIFF_WIDTH), f32),
        "diff_w_out": nrm(ks[18], (Bn, DIFF_WIDTH, D_MODEL), f32) * DIFF_WIDTH ** -0.5,
    }

def first_block(x, rel_bias_table, norm_pre, norm_post, nsa_w_in, nsa_cmp_pe_k, nsa_cmp_w1_k,
              nsa_cmp_w2_k, nsa_cmp_pe_v, nsa_cmp_w1_v, nsa_cmp_w2_v, nsa_w_out, diff_w_in,
              diff_lambda_q1, diff_lambda_k1, diff_lambda_q2, diff_lambda_k2, diff_subln, diff_w_out):
    for i in range(DEPTH):
        u = rmsnorm(x, norm_pre[i])
        j = i // N_MIXERS
        if i % N_MIXERS == 0:
            y = nsa_mixer(u, rel_bias_table, nsa_w_in[j], nsa_cmp_pe_k[j], nsa_cmp_w1_k[j],
                          nsa_cmp_w2_k[j], nsa_cmp_pe_v[j], nsa_cmp_w1_v[j], nsa_cmp_w2_v[j],
                          nsa_w_out[j])
        else:
            lambda_init = 0.8 - 0.6 * math.exp(-0.3 * i)
            y = diff_mixer(u, rel_bias_table, diff_w_in[j], diff_lambda_q1[j], diff_lambda_k1[j],
                           diff_lambda_q2[j], diff_lambda_k2[j], diff_subln[j], diff_w_out[j],
                           lambda_init)
        x = x + rmsnorm(y, norm_post[i])
    return x


GRID_W = 64
NA_WIN_ROWS = 8
NA_WIN_COLS = 16
NA_HEADS = 16
NA_HEAD_DIM = D_MODEL // NA_HEADS
MLA_HEADS = 16
MLA_Q_RANK = 384
MLA_KV_RANK = 256
MLA_NOPE = 64
MLA_ROPE = 32
MLA_V = 64
ROPE_BASE = 10000.0
Q_BLOCK = 128
PLE_DIM = 256
N_A = (DEPTH + 1) // 2
N_B = DEPTH // 2


def rmsnorm_2(x, g):
    xf = x.astype(jnp.float32)
    y = xf * lax.rsqrt(jnp.mean(xf * xf, axis=-1, keepdims=True) + EPS)
    return (y * g.astype(jnp.float32)).astype(x.dtype)

def rope_tables(seq, dim):
    inv = 1.0 / (ROPE_BASE ** (jnp.arange(0, dim, 2, dtype=jnp.float32) / dim))
    ang = jnp.arange(seq, dtype=jnp.float32)[:, None] * inv[None, :]
    return jnp.cos(ang), jnp.sin(ang)

def apply_rope(x, cos, sin):
    x1, x2 = jnp.split(x, 2, axis=-1)
    c = cos[None, :, None, :].astype(x.dtype)
    s = sin[None, :, None, :].astype(x.dtype)
    return jnp.concatenate([x1 * c - x2 * s, x1 * s + x2 * c], axis=-1)

def neighbourhood_attention(q, k, v, rpb):
    B, S, H, dh = q.shape
    rows = S // GRID_W
    kr = min(NA_WIN_ROWS, rows)
    kc = NA_WIN_COLS
    qg = q.reshape(B, rows, GRID_W, H, dh)
    kg = k.reshape(B, rows, GRID_W, H, dh)
    vg = v.reshape(B, rows, GRID_W, H, dh)
    cols = jnp.arange(GRID_W)
    col_start = jnp.clip(cols - kc // 2, 0, GRID_W - kc)
    col_idx = col_start[:, None] + jnp.arange(kc)[None, :]
    col_off = col_idx - cols[:, None] + (NA_WIN_COLS - 1)
    scale = dh ** -0.5

    def row_block(r):
        rs = jnp.clip(r - kr // 2, 0, rows - kr)
        q_r = lax.dynamic_index_in_dim(qg, r, axis=1, keepdims=False)
        k_band = lax.dynamic_slice_in_dim(kg, rs, kr, axis=1)
        v_band = lax.dynamic_slice_in_dim(vg, rs, kr, axis=1)
        k_win = k_band[:, :, col_idx]
        v_win = v_band[:, :, col_idx]
        row_off = rs + jnp.arange(kr) - r + (NA_WIN_ROWS - 1)
        bias = rpb[:, row_off[:, None, None], col_off[None, :, :]]
        bias = bias.transpose(0, 2, 1, 3).astype(jnp.float32)
        s = jnp.einsum('bwhd,biwjhd->bhwij', q_r, k_win).astype(jnp.float32) * scale
        s = (s + bias[None]).reshape(B, H, GRID_W, kr * kc)
        pr = jax.nn.softmax(s, axis=-1).reshape(B, H, GRID_W, kr, kc).astype(v.dtype)
        return jnp.einsum('bhwij,biwjhd->bwhd', pr, v_win)

    o = lax.map(row_block, jnp.arange(rows))
    return o.transpose(1, 0, 2, 3, 4).reshape(B, S, H, dh)

def block_attention(q, k, v):
    B, S, H, dqk = q.shape
    nb = S // Q_BLOCK
    qb = q.reshape(B, nb, Q_BLOCK, H, dqk).transpose(1, 0, 2, 3, 4)
    scale = dqk ** -0.5

    def one(qblk):
        s = jnp.einsum('bqhd,bkhd->bhqk', qblk, k).astype(jnp.float32) * scale
        pr = jax.nn.softmax(s, axis=-1).astype(v.dtype)
        return jnp.einsum('bhqk,bkhd->bqhd', pr, v)

    o = lax.map(one, qb)
    return o.transpose(1, 0, 2, 3, 4).reshape(B, S, H, v.shape[-1])

def mixer_na(xn, w_in, rpb, w_out):
    B, S, _ = xn.shape
    hd = NA_HEADS * NA_HEAD_DIM
    q, k, v, z = jnp.split(xn @ w_in, 4, axis=-1)
    shp = (B, S, NA_HEADS, NA_HEAD_DIM)
    o = neighbourhood_attention(q.reshape(shp), k.reshape(shp), v.reshape(shp), rpb)
    return (o.reshape(B, S, hd) * jax.nn.silu(z)) @ w_out

def mixer_mla(xn, w_in, q_norm, w_qb, kv_norm, w_kvb, w_out):
    B, S, _ = xn.shape
    H = MLA_HEADS
    c_q, c_kv, k_rope, z = jnp.split(
        xn @ w_in, [MLA_Q_RANK, MLA_Q_RANK + MLA_KV_RANK, MLA_Q_RANK + MLA_KV_RANK + MLA_ROPE], axis=-1)
    cos, sin = rope_tables(S, MLA_ROPE)
    q = (rmsnorm_2(c_q, q_norm) @ w_qb).reshape(B, S, H, MLA_NOPE + MLA_ROPE)
    q_nope, q_pe = jnp.split(q, [MLA_NOPE], axis=-1)
    q_pe = apply_rope(q_pe, cos, sin)
    kv = (rmsnorm_2(c_kv, kv_norm) @ w_kvb).reshape(B, S, H, MLA_NOPE + MLA_V)
    k_nope, v = jnp.split(kv, [MLA_NOPE], axis=-1)
    k_pe = apply_rope(k_rope[:, :, None, :], cos, sin)
    k = jnp.concatenate([k_nope, jnp.broadcast_to(k_pe, (B, S, H, MLA_ROPE))], axis=-1)
    q = jnp.concatenate([q_nope, q_pe], axis=-1)
    o = block_attention(q, k, v)
    return (o.reshape(B, S, H * MLA_V) * jax.nn.silu(z)) @ w_out

def second_inputs(seed: int = 0) -> dict:
    key = jax.random.key(seed)
    ks = jax.random.split(key, 20)
    f32 = jnp.float32

    def w(k, shape, fan_in):
        return jax.random.normal(k, shape, f32) * fan_in ** -0.5

    def gain(k, shape):
        return 1.0 + 0.05 * jax.random.normal(k, shape, f32)

    na_in = 4 * NA_HEADS * NA_HEAD_DIM
    mla_in = MLA_Q_RANK + MLA_KV_RANK + MLA_ROPE + MLA_HEADS * MLA_V
    return {
        "x": jax.random.normal(ks[0], (BATCH, SEQ, D_MODEL), f32),
        "p": jax.random.normal(ks[1], (DEPTH, BATCH, SEQ, PLE_DIM), f32),
        "norm_g": gain(ks[2], (DEPTH, D_MODEL)),
        "na_w_in": w(ks[3], (N_A, D_MODEL, na_in), D_MODEL),
        "na_rpb": 0.1 * jax.random.normal(ks[4], (N_A, NA_HEADS, 2 * NA_WIN_ROWS - 1, 2 * NA_WIN_COLS - 1), f32),
        "na_w_out": w(ks[5], (N_A, NA_HEADS * NA_HEAD_DIM, D_MODEL), NA_HEADS * NA_HEAD_DIM),
        "mla_w_in": w(ks[6], (N_B, D_MODEL, mla_in), D_MODEL),
        "mla_q_norm": gain(ks[7], (N_B, MLA_Q_RANK)),
        "mla_w_qb": w(ks[8], (N_B, MLA_Q_RANK, MLA_HEADS * (MLA_NOPE + MLA_ROPE)), MLA_Q_RANK),
        "mla_kv_norm": gain(ks[9], (N_B, MLA_KV_RANK)),
        "mla_w_kvb": w(ks[10], (N_B, MLA_KV_RANK, MLA_HEADS * (MLA_NOPE + MLA_V)), MLA_KV_RANK),
        "mla_w_out": w(ks[11], (N_B, MLA_HEADS * MLA_V, D_MODEL), MLA_HEADS * MLA_V),
        "ple_norm": gain(ks[12], (DEPTH, D_MODEL)),
        "ple_w_gate": w(ks[13], (DEPTH, D_MODEL, D_MODEL), D_MODEL),
        "ple_w_proj": w(ks[14], (DEPTH, PLE_DIM, D_MODEL), PLE_DIM),
        "final_norm": gain(ks[15], (D_MODEL,)),
    }

def second_block(x, p, norm_g, na_w_in, na_rpb, na_w_out, mla_w_in, mla_q_norm, mla_w_qb,
              mla_kv_norm, mla_w_kvb, mla_w_out, ple_norm, ple_w_gate, ple_w_proj, final_norm):
    for i in range(DEPTH):
        xn = rmsnorm_2(x, norm_g[i])
        j = i // N_MIXERS
        if i % N_MIXERS == 0:
            y = mixer_na(xn, na_w_in[j], na_rpb[j], na_w_out[j])
        else:
            y = mixer_mla(xn, mla_w_in[j], mla_q_norm[j], mla_w_qb[j],
                          mla_kv_norm[j], mla_w_kvb[j], mla_w_out[j])
        h = x + y
        gate = jax.nn.sigmoid(rmsnorm_2(h, ple_norm[i]) @ ple_w_gate[i])
        x = h + gate * (p[i] @ ple_w_proj[i])
    return rmsnorm_2(x, final_norm)


def setup_inputs(seed=0):
    out = dict(first_inputs(seed))
    for name, value in second_inputs(seed + 1).items():
        if name != "x":
            out[name + "_2"] = value
    return out


def reference(
    x, rel_bias_table, norm_pre, norm_post, nsa_w_in, nsa_cmp_pe_k, nsa_cmp_w1_k, nsa_cmp_w2_k,
    nsa_cmp_pe_v, nsa_cmp_w1_v, nsa_cmp_w2_v, nsa_w_out, diff_w_in, diff_lambda_q1,
    diff_lambda_k1, diff_lambda_q2, diff_lambda_k2, diff_subln, diff_w_out, p_2, norm_g_2,
    na_w_in_2, na_rpb_2, na_w_out_2, mla_w_in_2, mla_q_norm_2, mla_w_qb_2, mla_kv_norm_2,
    mla_w_kvb_2, mla_w_out_2, ple_norm_2, ple_w_gate_2, ple_w_proj_2, final_norm_2,
):
    x = first_block(
        x, rel_bias_table, norm_pre, norm_post, nsa_w_in, nsa_cmp_pe_k, nsa_cmp_w1_k,
        nsa_cmp_w2_k, nsa_cmp_pe_v, nsa_cmp_w1_v, nsa_cmp_w2_v, nsa_w_out, diff_w_in,
        diff_lambda_q1, diff_lambda_k1, diff_lambda_q2, diff_lambda_k2, diff_subln, diff_w_out,
    )
    return second_block(
        x, p_2, norm_g_2, na_w_in_2, na_rpb_2, na_w_out_2, mla_w_in_2, mla_q_norm_2, mla_w_qb_2,
        mla_kv_norm_2, mla_w_kvb_2, mla_w_out_2, ple_norm_2, ple_w_gate_2, ple_w_proj_2,
        final_norm_2,
    )


_drawn_inputs = setup_inputs


def setup_inputs(seed=0):
    import zlib

    import numpy as np

    out = dict(_drawn_inputs(seed))
    spreads = {}
    factors = {'diff_lambda_k1': 3.055,
     'diff_lambda_k2': 2.743,
     'norm_g_2': 6.584,
     'na_rpb_2': 8.0,
     'mla_q_norm_2': 8.0,
     'mla_kv_norm_2': 8.0,
     'ple_norm_2': 115.894}
    for name, (base, spread) in spreads.items():
        noise = np.random.default_rng([zlib.crc32(name.encode()), seed]).standard_normal(out[name].shape)
        drawn = base * np.exp(spread * noise) if base else spread * noise
        out[name] = __import__('jax').numpy.asarray(drawn.astype(out[name].dtype))
    for name, factor in factors.items():
        out[name] = (out[name] * factor).astype(out[name].dtype)
    return out
```

```python
from contextlib import ExitStack, contextmanager

import numpy as np

import concourse.bass as bass
from concourse import mybir

F32 = mybir.dt.float32
F32R = mybir.dt.float32r
ALU = mybir.AluOpType
ACT = mybir.ActivationFunctionType
AX = mybir.AxisListType.X

P = 128
D = 1024
T = 512
NT = T // P
KC = D // P
UNIT = 2048
EPS = 1e-6
BIG = 3.0e38
MASKED = -1e30
BUCKETS = 32
HEADS = 16
DIFF_HEADS = 8
LAMBDA_INIT = 0.8 - 0.6 * float(np.exp(-0.3))
SPAN = 1024
STRIP = 896
CMP = 31
GRID_W = 64
RPB_ROW, RPB_HEAD = 31, 15 * 31
RPB_PAD = 48
RPB_LEN = HEADS * RPB_HEAD + 2 * RPB_PAD
Q_RANK, KV_RANK = 384, 256
ROPE = 32
PLE = 256

RUNS = {}
N_UNITS = 0
N_BLOCKS = 0


def _run(name, blocks, nks, width, mode, k0=0):
    global N_UNITS, N_BLOCKS
    taker = "act" if name.endswith(("_z", "gate", "cmp")) else "dve"
    RUNS[name] = dict(name=name, blocks=blocks, nks=nks, width=width, mode=mode, k0=k0,
                      unit=N_UNITS, block=N_BLOCKS, taker=taker,
                      taken=sum(4 * r["blocks"] for r in RUNS.values() if r["taker"] == taker),
                      others=sum(4 * r["blocks"] for r in RUNS.values() if r["taker"] != taker))
    N_UNITS += blocks * len(nks)
    N_BLOCKS += blocks


_run("nsa_q", 2, (4, 4), 512, "features")
_run("nsa_k", 2, (4, 4), 512, "features")
_run("nsa_v", 1, (4, 4), 512, "tokens")
_run("nsa_gate", 1, (8,), 48, "tokens")
_run("nsa_z", 2, (4, 4), 512, "features")
_run("nsa_cmp", 1, (16, 16), 128, "compress")
_run("nsa_out", 2, (4, 4), 512, "tokens")
_run("diff_q", 2, (4, 4), 512, "features")
_run("diff_k", 2, (4, 4), 512, "features")
_run("diff_v", 2, (4, 4), 512, "tokens")
_run("diff_z", 2, (4, 4), 512, "features")
_run("diff_out", 2, (4, 4), 512, "tokens")
_run("na_q", 2, (4, 4), 512, "features")
_run("na_k", 2, (4, 4), 512, "features")
_run("na_v", 2, (4, 4), 512, "tokens")
_run("na_z", 2, (4, 4), 512, "features")
_run("na_out", 2, (4, 4), 512, "tokens")
_run("ple0_proj", 2, (2,), 512, "tokens")
_run("ple0_gate", 2, (4, 4), 512, "tokens")
_run("mla_cq", 1, (4, 4), 384, "tokens")
_run("mla_ckv", 1, (4, 4), 256, "tokens")
_run("mla_rope", 1, (8,), 128, "features")
_run("mla_z", 2, (4, 4), 512, "features")
_run("mla_q", 4, (3,), 512, "features")
_run("mla_k", 2, (2,), 512, "features", 3)
_run("mla_v", 2, (2,), 512, "tokens", 3)
_run("mla_out", 2, (4, 4), 512, "tokens")
_run("ple1_proj", 2, (2,), 512, "tokens")
_run("ple1_gate", 2, (4, 4), 512, "tokens")

GAINS = ["pre0", "post0", "pre1", "post1", "na", "ple0", "mla", "latent", "ple1", "final"]


def tri(n):
    return P * n * (n + 1) // 2


@contextmanager
def repeat(eng, n):
    if n == 1:
        yield 0
    else:
        with eng.Fori(0, n) as i:
            yield i


class Attention:

    def __init__(self, name, passes, per_head, causal, ahead, bufs, cmp=False):
        self.name, self.passes, self.per_head, self.causal = name, passes, per_head, causal
        self.maps = 2 * per_head
        self.ahead, self.bufs = ahead, bufs
        diff = name == "diff"
        self.turns = []
        for a in range(2):
            if cmp:
                self.turns.append(("cmp", a, None))
            if diff:
                self.turns.append(("full", a, 2 * a))
            else:
                self.turns += [("full", a, per_head * a + b) for b in range(per_head)]
        self.use = []
        n = 0
        for kind, _, _ in self.turns:
            self.use.append(n)
            n += 1 if kind == "cmp" else NT
        self.uses = n
        self.credit = 2 * n
        self.diff = diff
        self.maps_per_turn = 2 if diff else 1
        self.mla = name == "mla"

    def length(self, qt):
        return P * (qt + 1) if self.causal else T

    def p_at(self, qt):
        return tri(qt) if self.causal else T * qt

    def p_size(self):
        return tri(NT) if self.causal else NT * T

    def pt_at(self, kt):
        return tri(NT) - tri(NT - kt) if self.causal else T * kt

    def first_q(self, kt):
        return kt if self.causal else 0

    def turn_of(self, m):
        if self.diff:
            m = m - m % 2
        return next(t for t, (kind, _, mm) in enumerate(self.turns) if kind == "full" and mm == m)

    def released(self, m):
        return self.turned_by(m - self.bufs)

    def turned_by(self, m):
        return (m // self.maps) * self.uses + self.use[self.turn_of(m % self.maps)] + NT - 1

    def last_use(self, head):
        return max(self.use[t] + (NT if k == "full" else 1) - 1
                   for t, (k, a, _) in enumerate(self.turns) if a == head)

    def schedule(self):
        out = []
        step = 2 if self.diff else 1
        for t, (kind, a, m) in enumerate(self.turns):
            ends = t + 1 == len(self.turns) or self.turns[t + 1][1] != a
            if kind == "cmp":
                out.append((t, [], None, None))
            else:
                out.append((t, [m + self.ahead + s for s in range(step)], m + step, a if ends else None))
        return out

    def parts(self, scores):
        flat = [(m, qt) for m in scores for qt in range(NT)]
        n = len(flat) // NT
        return [flat[n * k:n * (k + 1)] for k in range(NT)] if flat else [[]] * NT


NORMS = [("pre0", ((0, D),), KC, 0), ("post0", ((0, D),), 0, 1), ("pre1", ((0, D),), KC, 2),
         ("post1", ((0, D),), 0, 3), ("na", ((0, D),), KC, 4), ("ple0", ((0, D),), KC, 5),
         ("mla", ((0, D),), KC, 6), ("latent", ((0, Q_RANK), (Q_RANK, Q_RANK + KV_RANK)), 5, 7),
         ("ple1", ((0, D),), KC, 8), ("final", ((0, D),), 0, 9)]


def norm_base(k):
    seg = sum(len(n[1]) for n in NORMS[:k])
    banks = sum((2 * NT if n[2] else 0) for n in NORMS[:k])
    return seg, k, banks


def _program(nc, A, out):
    with ExitStack() as ctx:
        def sb(name, cols, dt=F32):
            return ctx.enter_context(nc.sbuf_tensor(name, [P, cols], dt))

        def sem(name):
            return ctx.enter_context(nc.semaphore(name))

        x = sb("x", NT * D)
        u_hi, u_lo = sb("u_hi", KC * T, F32R), sb("u_lo", KC * T, F32R)
        stage = [sb(f"stage{b}", UNIT) for b in range(2)]
        w_hi = [sb(f"w_hi{b}", UNIT, F32R) for b in range(2)]
        w_lo = [sb(f"w_lo{b}", UNIT, F32R) for b in range(2)]
        gain = [sb(f"gain{b}", D) for b in range(2)]
        ident = sb("ident", P)
        ss = sb("ss", 2 * NT)
        ms = sb("ms", 2 * NT)
        half_exp = sb("half_exp", 1)
        neg_max = sb("neg_max", 4 * NT)
        row_sum = sb("row_sum", 4 * NT)
        inv = sb("inv", 4 * NT)
        zero, one = sb("zero", 1), sb("one", 1)
        neg_lam = sb("neg_lam", 4)
        gate = sb("gate", NT * 48)
        subln = sb("subln", DIFF_HEADS)
        ARENA = 26120
        arena = sb("arena", ARENA)
        psum = ctx.enter_context(nc.psum_tensor("psum", [P, 8, 512], F32))

        def bank(n, width=512):
            return psum[:, n, 0:width]

        def at(off, width=512, lo=0, hi=P):
            return arena[lo:hi, bass.ds(off, width)] if not isinstance(off, int) else arena[lo:hi, off:off + width]

        QT, KT, V, Z = 0, 4096, 8192, 12288
        TAIL = 16384
        N_CK, N_VC, N_PC = TAIL, TAIL + 64, TAIL + 320
        N_P = N_PC + HEADS * NT * CMP
        N_CB = ARENA - HEADS * NT * CMP
        bias_rows = nc.dram_tensor("bias_rows", (P, HEADS * SPAN), F32, kind="Internal").ap()
        rpb_rows = nc.dram_tensor("rpb_rows", (GRID_W, RPB_LEN), F32, kind="Internal").ap()

        w_loaded = [sem(f"w_loaded{b}") for b in range(2)]
        w_high, w_ready = sem("w_high"), sem("w_ready")
        w_used = sem("w_used")
        bank_done = sem("bank_done")
        bank_free = {"act": sem("bank_free_act"), "dve": sem("bank_free_dve")}
        stage_end, held = sem("stage_end"), sem("held")
        x_in, const_in, small_in = sem("x_in"), sem("const_in"), sem("small_in")
        gain_in = [sem("gain_in0"), sem("gain_in1")]
        out_written = sem("out_written")
        rows_made, rows_out = sem("rows_made"), sem("rows_out")
        strip_in, strip_used = [sem("strip_in0"), sem("strip_in1")], sem("strip_used")
        sq_done, ms_done, rstd_done, xn_done = sem("sq_done"), sem("ms_done"), sem("rstd_done"), sem("xn_done")
        turned, u_hi_done = sem("turned"), sem("u_hi_done")
        dve_step, act_step, pool_step, pe_step = sem("dve_step"), sem("act_step"), sem("pool_step"), sem("pe_step")
        own = {"dve": [dve_step, 0], "act": [act_step, 0], "pool": [pool_step, 0], "pe": [pe_step, 0]}

        def done(who, ins):
            own[who][1] += 1
            ins.then_inc(own[who][0], 1)

        def settle(who, eng):
            eng.wait_ge(own[who][0], own[who][1])

        stages = {"pe": 0, "act": 0, "dve": 0, "pool": 0}

        def finish(who, eng):
            stages[who] += 1
            eng.drain().then_inc(stage_end, 1)
            eng.wait_ge(stage_end, 4 * stages[who])

        def hold(eng):
            eng.sem_inc(held, 1)

        block = ctx.enter_context(nc.Block())

        @block.sync
        def _(sp):
            def unit(n, b):
                sp.dma_start(stage[b][:], A["weights"][n]).then_inc(w_loaded[b], 16)

            unit(0, 0)
            unit(1, 1)
            assert N_UNITS % 2 == 0
            with sp.Fori(1, N_UNITS // 2) as i:
                for b in range(2):
                    sp.wait_ge(w_ready, 2 * i + b - 1)
                    sp.dma_start(stage[b][:], A["weights"][bass.ds(2 * i + b, 1)].rearrange("o p n -> p (o n)"))\
                        .then_inc(w_loaded[b], 16)
            sp.wait_ge(out_written, 16 * NT)

        def split_high(act, n, b, arrivals):
            act.wait_ge(w_loaded[b], 16 * arrivals)
            nc.scalar.activation(w_hi[b][:], stage[b][:], ACT.Copy).then_inc(w_high, 1)

        def split_low(pool, n, b):
            pool.wait_ge(w_high, n + 1)
            nc.gpsimd.tensor_tensor(w_lo[b][:], stage[b][:], w_hi[b][:].bitcast(F32), ALU.subtract)\
                .then_inc(w_ready, 1)

        def pairs_before(run):
            return sum(r["blocks"] for r in RUNS.values() if r["unit"] < run["unit"] and len(r["nks"]) == 2)

        def blocks_of(eng, run):
            if len(run["nks"]) == 2 and run["name"] != "ple1_gate" and run["blocks"] > 1:
                with eng.Fori(0, run["blocks"]) as i:
                    yield i
            else:
                yield from range(run["blocks"])

        def next_unit(run, i, a):
            u = len(run["nks"])
            b = (run["unit"] + a + (0 if u == 2 else i)) % 2
            n = run["unit"] + u * i + a + 2
            if u == 2:
                return n, b, (run["unit"] + a) // 2 + i + 2
            return n, b, n // 2 + 1

        def exists(n):
            return not isinstance(n, int) or n < N_UNITS

        def wait_used(eng, run, i, a):
            if a + 1 < len(run["nks"]):
                eng.wait_ge(w_used, pairs_before(run) + i + 1)
            else:
                eng.wait_ge(bank_done, 4 * (run["block"] + i) + 4)

        def wait_bank(pe, run, i, j):
            other = "dve" if run["taker"] == "act" else "act"
            pe.wait_ge(bank_free[run["taker"]], run["taken"] + 4 * i + j + 1)
            pe.wait_ge(bank_free[other], run["others"] + j + 1)

        def project_tensor(pe, name, banks=4):
            run = RUNS[name]
            w = run["width"]
            for i in blocks_of(pe, run):
                k0 = run["k0"]
                for a, nk in enumerate(run["nks"]):
                    u = len(run["nks"])
                    b = (run["unit"] + a + (0 if u == 2 else i)) % 2
                    pe.wait_ge(w_ready, run["unit"] + u * i + a + 1)
                    for j in range(banks):
                        if a == 0:
                            wait_bank(pe, run, i, j if banks == 4 else 3)
                        for k in range(nk):
                            for wl, ul in ((0, 1), (1, 0), (0, 0)):
                                ww = (w_lo if wl else w_hi)[b]
                                uu = u_lo if ul else u_hi
                                at_u = (k0 + k) * T
                                if run["mode"] == "features":
                                    lhs, rhs = ww[:, k * w + j * P:k * w + (j + 1) * P], uu[:, at_u:at_u + T]
                                    dst = bank(j)
                                else:
                                    lhs, rhs = uu[:, at_u + j * P:at_u + (j + 1) * P], ww[:, k * w:(k + 1) * w]
                                    dst = bank(j, w)
                                mm = nc.tensor.matmul(dst, lhs, rhs, start=(a == 0 and k == 0 and (wl, ul) == (0, 1)),
                                                      stop=(a + 1 == u and k + 1 == nk and (wl, ul) == (0, 0)))
                        if a + 1 == u:
                            mm.then_inc(bank_done, 4 // banks)
                    if a + 1 < u:
                        mm.then_inc(w_used, 1)
                    k0 += nk

        def project_pool(pool, name):
            run = RUNS[name]
            for i in blocks_of(pool, run):
                for a in range(len(run["nks"])):
                    n, b, _ = next_unit(run, i, a)
                    if exists(n):
                        split_low(pool, n, b)

        def project_scalar(act, name, take=None, banks=4):
            run = RUNS[name]
            for i in blocks_of(act, run):
                for a in range(len(run["nks"])):
                    if a + 1 == len(run["nks"]) and take:
                        for j in range(banks):
                            act.wait_ge(bank_done, 4 * (run["block"] + i) + (j + 1 if banks == 4 else 4))
                            take(i, j).then_inc(bank_free["act"], 4 // banks)
                    n, b, arrivals = next_unit(run, i, a)
                    if exists(n):
                        wait_used(act, run, i, a)
                        split_high(act, n, b, arrivals)

        def project_vector(dve, name, take, banks=4):
            run = RUNS[name]
            for i in blocks_of(dve, run):
                for j in range(banks):
                    dve.wait_ge(bank_done, 4 * (run["block"] + i) + (j + 1 if banks == 4 else 4))
                    take(i, j).then_inc(bank_free["dve"], 4 // banks)

        def to_features(place, scale=1.0):
            def take(i, j):
                return nc.vector.tensor_scalar(at(place + j * T + i * 4 * T), bank(j), scale, None, ALU.mult)
            return take

        def to_tokens(place, row, width=512):
            def take(i, j):
                return nc.vector.tensor_scalar(at(place + j * row + i * 512, width), bank(j, width), 1.0, None, ALU.mult)
            return take

        def silu_features(place):
            def take(i, j):
                return nc.scalar.activation(at(place + j * T + i * 4 * T), bank(j), ACT.Silu)
            return take

        def add_residual(i, j):
            dst = x[:, bass.ds(j * D + i * 512, 512)] if not isinstance(i, int) else x[:, j * D + i * 512:j * D + i * 512 + 512]
            return nc.vector.tensor_tensor(dst, bank(j), dst, ALU.add)

        def seg_gain(k, s):
            lo, hi = NORMS[k][1][s]
            return gain[k % 2][:, lo:hi]

        def load_gain(act, k):
            act.dma_start(gain[k % 2][:], bass.AP(A["gains"].tensor, k * D, [[0, P], [1, D]])).then_inc(gain_in[k % 2], 16)

        def norm_vector(dve, k, src, xn, row):
            seg0, _, bank0 = norm_base(k)
            segs = NORMS[k][1]
            for s, (lo, hi) in enumerate(segs):
                for t in range(NT):
                    nc.vector.tensor_tensor_reduce(
                        out=at(xn + t * row + lo, hi - lo), in0=src(t, lo, hi), in1=src(t, lo, hi), scale=1.0,
                        scalar=0.0, op0=ALU.mult, op1=ALU.add,
                        accum_out=ss[:, s * NT + t:s * NT + t + 1]).then_inc(sq_done, 1)
                dve.wait_ge(sq_done, NT * (seg0 + s + 1))
                nc.vector.tensor_scalar(ms[:, s * NT:(s + 1) * NT], ss[:, s * NT:(s + 1) * NT], 1.0 / (hi - lo), EPS,
                                        ALU.mult, ALU.add).then_inc(ms_done, 1)
            dve.wait_ge(gain_in[k % 2], 16 * (k // 2 + 1))
            dve.wait_ge(rstd_done, seg0 + len(segs))
            for t in range(NT):
                for s, (lo, hi) in enumerate(segs):
                    ins = nc.vector.scalar_tensor_tensor(
                        out=at(xn + t * row + lo, hi - lo), in0=src(t, lo, hi), scalar=ss[:, s * NT + t:s * NT + t + 1],
                        in1=seg_gain(k, s), op0=ALU.mult, op1=ALU.mult)
                    ins.then_inc(xn_done, 1)
            if NORMS[k][2]:
                for b in range(2 * NT):
                    dve.wait_ge(u_hi_done, bank0 + b + 1)
                    d, n = turned_place(k, b)
                    nc.vector.tensor_tensor(d(u_lo), turned_bank(b, n), d(u_hi).bitcast(F32), ALU.subtract)

        def turned_place(k, b):
            t, h = b // 2, b % 2
            n = min(4, NORMS[k][2] - 4 * h)

            def d(u):
                return u[:].rearrange("p (c t) -> p c t", c=KC)[:, 4 * h:4 * h + n, t * P:(t + 1) * P]
            return d, n

        def turned_bank(b, n):
            return psum[:, b, 0:n * P].rearrange("p (c t) -> p c t", c=n)

        def norm_pool(pool, k):
            seg0 = norm_base(k)[0]
            for s in range(len(NORMS[k][1])):
                pool.wait_ge(ms_done, seg0 + s + 1)
                nc.gpsimd.tensor_tensor(ss[:, s * NT:(s + 1) * NT], ms[:, s * NT:(s + 1) * NT],
                                        half_exp[:, 0:1].to_broadcast([P, NT]), ALU.pow).then_inc(rstd_done, 1)

        def norm_tensor(pe, k, xn, row):
            segs = NORMS[k][1]
            xn0 = NT * norm_base(k)[0]
            for b in range(2 * NT):
                t, h = b // 2, b % 2
                n = min(4, NORMS[k][2] - 4 * h)
                pe.wait_ge(xn_done, xn0 + len(segs) * (t + 1))
                for c in range(n):
                    tr = nc.tensor.transpose(psum[:, b, c * P:(c + 1) * P], at(xn + t * row + (4 * h + c) * P, P), ident[:])
                tr.then_inc(turned, 1)

        def norm_scalar(act, k):
            bank0 = norm_base(k)[2]
            if k + 1 < len(NORMS):
                if k >= 1:
                    act.wait_ge(xn_done, NT * norm_base(k)[0])
                load_gain(act, k + 1)
            if NORMS[k][2]:
                for b in range(2 * NT):
                    act.wait_ge(turned, bank0 + b + 1)
                    d, n = turned_place(k, b)
                    nc.scalar.activation(d(u_hi), turned_bank(b, n), ACT.Copy).then_inc(u_hi_done, 1)

        def x_tile(t, lo, hi):
            return x[:, t * D + lo:t * D + hi]


        out_hi = sem("out_hi")

        def split_output_scalar(act, src, nth):
            for c in range(0, KC, 2):
                if nth == 1:
                    act.wait_ge(sub_out, c + 2)
                nc.scalar.activation(u_hi[:, c * T:(c + 2) * T], at(src + c * T, 2 * T), ACT.Copy).then_inc(out_hi, 1)

        def split_output_vector(dve, src, nth):
            for c in range(0, KC, 2):
                dve.wait_ge(out_hi, 4 * nth + c // 2 + 1)
                nc.vector.tensor_tensor(u_lo[:, c * T:(c + 2) * T], at(src + c * T, 2 * T),
                                        u_hi[:, c * T:(c + 2) * T].bitcast(F32), ALU.subtract)

        class Stage(Attention):

            def __init__(self, *args, **kw):
                super().__init__(*args, **kw)
                n = self.name
                self.s_ready, self.s_free = sem(f"{n}_scores"), sem(f"{n}_scores_taken")
                self.exp_done, self.inv_ready = sem(f"{n}_exp"), sem(f"{n}_inv")
                self.p_ready = sem(f"{n}_probs")
                self.pt_ready, self.pt_free = sem(f"{n}_turned"), sem(f"{n}_turned_taken")
                self.pv_done, self.o_free = sem(f"{n}_pv"), sem(f"{n}_out_taken")
                self.q_staged, self.v_staged = sem(f"{n}_q_staged"), sem(f"{n}_v_staged")
                self.bias_in = [sem(f"{n}_bias0"), sem(f"{n}_bias1")]
                self.diag = gain[1 if self.mla else 0]
                self.diag_done = sem(f"{n}_diag") if self.diff else None
                self.masked = sem(f"{n}_masked") if self.name == "na" else None
                self.vec = sem(f"{n}_vec")
                place = N_P if self.name == "nsa" else (TAIL + 2048 if self.mla else TAIL)
                self.P0 = place
                place += self.bufs * self.p_size()
                self.PT0 = place
                place += tri(NT) if self.causal else NT * T
                if self.name == "nsa":
                    self.BIAS, self.QS, self.PCS, self.PTC = V + 2048, V + 3072, V + 3584, place
                    place += T
                else:
                    self.bias_w = 0 if self.mla else (T if self.causal else STRIP)
                    self.BIAS = place
                    place += 2 * self.bias_w
                    self.QS, self.KS = place, place + T
                    place += 2 * T
                    self.VS = place
                    place += T * (2 if self.diff else 1)
                    self.MASK = place
                    place += GRID_W if self.name == "na" else 0
                assert place <= ARENA, (n, place)

            def rows(self, head):
                return 64 * head, 64 * head + 64

            def q_tile(self, m, qt):
                head = m // self.per_head
                if self.diff:
                    lo = 64 * (m % 2)
                    return at(self.QS + qt * P, P, lo, lo + 64)
                if self.mla:
                    return at(self.QS + qt * P, P, 0, 96)
                lo, hi = self.rows(head)
                return at(self.QS + qt * P, P, lo, hi)

            def k_cols(self, I, m, g, n):
                head = m // self.per_head
                if self.mla:
                    return at(self.KS, n, 0, 96)
                if self.diff:
                    lo = 64 * (m % 2)
                    return at(self.KS, n, lo, lo + 64)
                lo, hi = self.rows(head)
                if self.name == "nsa":
                    return at(KT + ((6 if m % 2 == 0 else 4) + g) * T, n, lo, hi)
                return at(self.KS, n, lo, hi)

            def bias_of(self, m, qt):
                n = self.length(qt)
                if self.mla:
                    return zero[:, 0:1].to_broadcast([P, n])
                if self.name == "na":
                    return at(self.BIAS + m * STRIP + (6 - 2 * qt) * GRID_W, n)
                b = m % 2 if self.diff else m // 2
                return at(self.BIAS + b * T + T - n, n)

            def p_tile(self, m, qt):
                return at(self.P0 + (m % self.bufs) * self.p_size() + self.p_at(qt), self.length(qt))

            def diag_tile(self, m, qt):
                b = (m // 2 if self.diff else m) % 2
                return self.diag[:, (b * NT + qt) * P:(b * NT + qt + 1) * P]

            def stat(self, buf, m, qt=None):
                b = m % self.bufs
                return buf[:, b * NT:(b + 1) * NT] if qt is None else buf[:, b * NT + qt:b * NT + qt + 1]

            def v_tile(self, t, g, kt):
                kind, head, m = self.turns[t]
                if kind == "cmp":
                    return at(N_VC + (2 * g + head) * 64, 64, 0, CMP)
                if self.name == "nsa":
                    return at(V + kt * T + (256 if m % 2 == 0 else 0) + (2 * g + head) * 64, 64)
                if self.diff:
                    return at(self.VS + head * T + kt * P, P)
                return at(self.VS + head * 256 + kt * 64, 64)

            def each_pass(self, eng, base, body):
                n = self.passes
                with eng.Fori(0, n - 1) as i:
                    body(i + base, False)
                body(base + n - 1, True)

        def place_of(att, I, last, m):
            if m < att.maps:
                return I, m
            return None if last else (I + 1, m - att.maps)

        def attend_tensor(pe, att, g=0, first=True):
            base = g * att.passes
            if first:
                pe.sem_inc(att.pt_ready, att.credit)
                pe.sem_inc(att.pv_done, att.credit)

            def score(I, m, qt):
                if qt == 0:
                    pe.wait_ge(att.q_staged, 2 * I + m // att.per_head + 1)
                n = att.length(qt)
                pe.wait_ge(att.s_free, 4 * (att.maps * I + m) + qt + 1)
                nc.tensor.matmul(bank(qt, n), att.q_tile(m, qt), att.k_cols(I, m, g, n),
                                 start=True, stop=True).then_inc(att.s_ready, 1)

            def turn(I, last, t, scores):
                kind, head, m = att.turns[t]
                use = att.uses * I + att.use[t]
                starts = t == 0 or att.turns[t - 1][1] != head
                ends = t + 1 == len(att.turns) or att.turns[t + 1][1] != head
                dv = P if att.diff else 64

                def turn_tile(kt):
                    pe.wait_ge(att.pt_free, use + kt + 1)
                    b = 4 + (att.use[t] + kt) % 2
                    if kind == "cmp":
                        for qt in range(NT):
                            tr = nc.tensor.transpose(psum[0:CMP, b, qt * P:(qt + 1) * P],
                                                     at(att.PCS + head * NT * CMP + qt * CMP, CMP), ident[:])
                    else:
                        q0 = att.first_q(kt)
                        for qt in range(q0, NT):
                            tr = nc.tensor.matmul(psum[:, b, (qt - q0) * P:(qt - q0 + 1) * P],
                                                  att.p_tile(m, qt)[:, kt * P:(kt + 1) * P], att.diag_tile(m, qt),
                                                  start=True, stop=True)
                    tr.then_inc(att.pt_ready, 1)

                def value_tile(kt, n_kt):
                    pe.wait_ge(att.pt_free, use + kt + 3)
                    if starts and kt == 0:
                        pe.wait_ge(att.o_free, 2 * I + head + 1)
                        pe.wait_ge(att.v_staged, 2 * I + head + 1)
                    if kind == "cmp":
                        rhs, q0 = at(att.PTC, T, 0, CMP), 0
                    else:
                        q0 = att.first_q(kt)
                        rhs = at(att.PT0 + att.pt_at(kt), T - q0 * P)
                    nc.tensor.matmul(psum[0:dv, 6 + head, q0 * P:T], att.v_tile(t, g, kt), rhs,
                                     start=(starts and kt == 0), stop=(ends and kt == n_kt - 1))\
                        .then_inc(att.pv_done, 1)

                if kind == "cmp":
                    pe.wait_ge(att.v_staged, 2 * I + head + 1)
                    turn_tile(0)
                    value_tile(0, 2)
                    return
                pe.wait_ge(att.p_ready, 4 * (2 * I + head) + 4 if att.diff else 4 * (att.maps * I + m) + 4)
                parts = att.parts(scores)
                turn_tile(0)
                for kt in range(NT):
                    for mm, qt in parts[kt]:
                        where = place_of(att, I, last, mm)
                        if where:
                            score(*where, qt)
                    if kt + 1 < NT:
                        turn_tile(kt + 1)
                    value_tile(kt, NT)

            for m in range(att.ahead):
                for qt in range(NT):
                    score(base, m, qt)

            def body(I, last):
                for t, scores, _, _ in att.schedule():
                    turn(I, last, t, scores)
            att.each_pass(pe, base, body)

        def attend_vector(dve, att, g=0, first=True):
            base = g * att.passes
            if first:
                dve.sem_inc(att.s_free, 4)
                dve.sem_inc(att.o_free, 2)

            def score(I, m):
                M = att.maps * I + m
                if att.name == "nsa":
                    dve.wait_ge(att.bias_in[m // 2], 16 * (I + 1))
                elif att.diff:
                    dve.wait_ge(att.bias_in[m % 2], 16 * (2 * I + m // 2 + 1))
                elif att.name == "na":
                    dve.wait_ge(att.masked, M + 1)
                dve.wait_ge(att.pt_ready, att.uses * I + (att.released(m) + 1 + att.credit))
                for qt in range(NT):
                    dve.wait_ge(att.s_ready, 4 * M + qt + 1)
                    hold(dve)
                    nc.vector.tensor_tensor_reduce(
                        out=att.p_tile(m, qt), in0=bank(qt, att.length(qt)), in1=att.bias_of(m, qt), scale=-1.0,
                        scalar=BIG, op0=ALU.add, op1=ALU.min, accum_out=att.stat(neg_max, m, qt))\
                        .then_inc(att.s_free, 1)

            def copy(dst, src):
                return nc.vector.tensor_scalar(dst, src, 1.0, None, ALU.mult)

            def stage_q(I, head):
                lo, hi = att.rows(head)
                if att.diff:
                    copy(at(att.QS), at(QT + (2 * I + head) * T))
                    ins = copy(at(att.KS), at(KT + (2 * I + head) * T))
                elif att.mla:
                    copy(at(att.QS, T, 0, 64), at(QT + I * T, T, lo, hi))
                    pe_lo = ROPE * (head + 2 * g)
                    copy(at(att.QS, T, 64, 96), at(TAIL + (I - base) * T, T, pe_lo, pe_lo + ROPE))
                    ins = copy(at(att.KS, T, 0, 64), at(KT + I * T, T, lo, hi))
                else:
                    ins = copy(at(att.QS, T, lo, hi), at(QT + I * T, T, lo, hi))
                    if att.name == "na":
                        ins = copy(at(att.KS, T, lo, hi), at(KT + I * T, T, lo, hi))
                ins.then_inc(att.q_staged, 1)

            def stage_v(I, head):
                if att.name == "nsa":
                    n = NT * CMP
                    row = (2 * g + head) * 4 - base + I
                    ins = copy(at(att.PCS + head * n, n), at(N_PC + n * row, n))
                else:
                    dv = P if att.diff else 64
                    col = (2 * I + head) * dv
                    v = arena[:, V:V + NT * D].rearrange("p (t c) -> p t c", c=D)
                    v = v[:, :, bass.ds(col, dv)] if not isinstance(col, int) else v[:, :, col:col + dv]
                    ins = copy(at(att.VS + head * NT * dv, NT * dv).rearrange("p (t c) -> p t c", c=dv), v)
                ins.then_inc(att.v_staged, 1)

            def score_and_stage(last):
                def run(I, m):
                    score(I, m)
                    if m % att.per_head == att.per_head - 1:
                        if m // att.per_head == 0:
                            stage_q(I, 1)
                        elif not last:
                            stage_q(I + 1, 0)
                return run

            def counted(ins):
                ins.then_inc(att.vec, 1)

            def own_count(M, step, steps):
                dve.wait_ge(att.vec, steps * M + step)

            def make_ready(I, m):
                M = att.maps * I + m
                r = att.stat(inv, m)
                dve.wait_ge(att.exp_done, 4 * M + (8 if att.diff else 4))
                counted(nc.vector.reciprocal(r, att.stat(row_sum, m)))
                if att.diff:
                    head = 2 * I + m // 2
                    c = att.stat(inv, m + 1)
                    counted(nc.vector.reciprocal(c, att.stat(row_sum, m + 1)))
                    own_count(head, 2, 3)
                    counted(nc.vector.scalar_tensor_tensor(out=c, in0=c, scalar=neg_lam[:, 0:1],
                                                           in1=att.stat(row_sum, m), op0=ALU.mult, op1=ALU.mult))
                    own_count(head, 3, 3)
                elif att.name == "nsa":
                    own_count(M, 1, 2)
                    head, branch = m // 2, 2 - m % 2
                    col = ((2 * g + head) * 4 - base) * 3 + branch + 3 * I
                    gates = gate[:].rearrange("p (t c) -> p t c", t=NT)
                    gates = gates[:, :, bass.ds(col, 1)] if not isinstance(col, int) else gates[:, :, col:col + 1]
                    r3 = r.rearrange("p (t o) -> p t o", o=1)
                    counted(nc.vector.tensor_tensor(r3, r3, gates, ALU.mult))
                    own_count(M, 2, 2)
                else:
                    own_count(M, 1, 1)
                dve.wait_ge(att.pt_ready, att.uses * I + (att.turned_by(m - att.maps_per_turn * 2) + 1 + att.credit))
                hold(dve)
                for qt in range(NT):
                    nc.vector.tensor_scalar(att.diag_tile(m, qt), ident[:], att.stat(inv, m, qt), None, ALU.mult)\
                        .then_inc(att.diag_done if att.diff else att.p_ready, 1)
                if att.diff:
                    for qt in range(NT):
                        nc.vector.scalar_tensor_tensor(
                            out=att.p_tile(m, qt), in0=att.p_tile(m + 1, qt), scalar=att.stat(inv, m + 1, qt),
                            in1=att.p_tile(m, qt), op0=ALU.mult, op1=ALU.add).then_inc(att.p_ready, 1)

            def take_head(I, head):
                dve.wait_ge(att.pv_done, att.uses * I + (att.last_use(head) + 1 + att.credit))
                if att.diff:
                    ins = nc.vector.tensor_scalar(at(QT + (2 * I + head) * T), bank(6 + head), 1.0, None, ALU.mult)
                else:
                    lo, hi = att.rows(head)
                    z = at(Z + I * T, T, lo, hi)
                    ins = nc.vector.tensor_tensor(z, psum[0:64, 6 + head, :], z, ALU.mult)
                ins.then_inc(att.o_free, 1)

            def body(I, last):
                for _, scores, ready, ends in att.schedule():
                    for m in scores:
                        where = place_of(att, I, last, m)
                        if where:
                            score_and_stage(last)(*where)
                    where = ready is not None and place_of(att, I, last, ready)
                    if where:
                        make_ready(*where)
                    if ends is not None:
                        take_head(I, ends)
                        if not last:
                            stage_v(I + 1, ends)

            stage_q(base, 0)
            stage_v(base, 0)
            stage_v(base, 1)
            for m in range(att.ahead):
                score_and_stage(False)(base, m)
            make_ready(base, 0)
            att.each_pass(dve, base, body)

        def attend_scalar(act, att, g=0, first=True):
            base = g * att.passes
            if first:
                act.sem_inc(att.pt_free, 2)

            def load_bias(I, m):
                if att.name == "na":
                    for r2 in range(2):
                        first_at = RPB_PAD + 15 + (1 - r2) * RPB_ROW + m * RPB_HEAD + 2 * RPB_HEAD * I
                        act.dma_start(
                            arena[r2 * 64:r2 * 64 + 64, att.BIAS + m * STRIP:att.BIAS + (m + 1) * STRIP]
                            .rearrange("p (j c) -> p j c", c=GRID_W),
                            bass.AP(rpb_rows.tensor, first_at, [[RPB_LEN - 1, 64], [RPB_ROW, 14], [1, GRID_W]]))\
                            .then_inc(att.bias_in[m], 16)
                    return
                if att.diff:
                    b, row = m % 2, 4 * I + m
                else:
                    b, row = m // 2, (2 * g + m // 2) * 4 - base + I
                act.dma_start(at(att.BIAS + b * T), bass.AP(bias_rows.tensor, P - 1 + SPAN * row,
                                                            [[HEADS * SPAN - 1, P], [1, T]]))\
                    .then_inc(att.bias_in[b], 16)

            def score(I, m, qt):
                act.wait_ge(att.s_free, 4 * (att.maps * I + m) + qt + 5)
                nc.scalar.activation(att.p_tile(m, qt), att.p_tile(m, qt), ACT.Exp, scale=-1.0,
                                     bias=att.stat(neg_max, m, qt), accum_out=att.stat(row_sum, m, qt))\
                    .then_inc(att.exp_done, 1)

            def copy_turned(I, t, kt):
                kind, head, m = att.turns[t]
                use = att.uses * I + att.use[t]
                b = 4 + (att.use[t] + kt) % 2
                act.wait_ge(att.pt_ready, use + kt + 1 + att.credit)
                if kind == "cmp":
                    act.wait_ge(att.pv_done, use - att.uses // 2 + 1 + att.credit)
                    ins = nc.scalar.activation(at(att.PTC, T, 0, CMP), psum[0:CMP, b, :], ACT.Copy)
                else:
                    full = [u for (k, _, _), u in zip(att.turns, att.use) if k == "full"]
                    n = full.index(att.use[t])
                    before = full[n - 1] - (att.uses if n == 0 else 0)
                    act.wait_ge(att.pv_done, att.uses * I + (before + kt + 1 + att.credit))
                    w = T - att.first_q(kt) * P
                    ins = nc.scalar.activation(at(att.PT0 + att.pt_at(kt), w), bank(b, w), ACT.Copy)
                ins.then_inc(att.pt_free, 1)

            def body(I, last):
                if att.diff:
                    load_bias(I, 2)
                    load_bias(I, 3)
                elif att.name != "mla" and not last:
                    load_bias(I + 1, 0)
                for t, scores, _, _ in att.schedule():
                    if att.turns[t][0] == "cmp":
                        copy_turned(I, t, 0)
                        continue
                    parts = att.parts(scores)
                    for kt in range(NT):
                        copy_turned(I, t, kt)
                        for mm, qt in parts[kt]:
                            where = place_of(att, I, last, mm)
                            if where:
                                score(*where, qt)
                    for k in scores:
                        if not last and k < att.maps:
                            if att.name == "na" and k == 1 or att.name == "nsa" and k == 3:
                                load_bias(I + 1, k)
                            elif att.diff and k >= 2:
                                load_bias(I + 1, k - 2)

            if att.name != "mla":
                for m in ((0, 2) if att.name == "nsa" else (0, 1)):
                    load_bias(base, m)
            for m in range(att.ahead):
                for qt in range(NT):
                    score(base, m, qt)
            att.each_pass(act, base, body)

        def attend_pool(pool, att):
            def body(I, last):
                for m in range(att.maps):
                    pool.wait_ge(att.bias_in[m], 32 * (I + 1))
                    hold(pool)
                    strip = at(att.BIAS + m * STRIP, STRIP).rearrange("p (j c) -> p j c", c=GRID_W)
                    mask = at(att.MASK, GRID_W).unsqueeze(1).to_broadcast([P, STRIP // GRID_W, GRID_W])
                    nc.gpsimd.tensor_tensor(strip, strip, mask, ALU.add).then_inc(att.masked, 1)
            att.each_pass(pool, 0, body)

        nsa = Stage("nsa", passes=4, per_head=2, causal=True, ahead=2, bufs=4, cmp=True)
        diff = Stage("diff", passes=4, per_head=2, causal=True, ahead=2, bufs=4)
        na = Stage("na", passes=8, per_head=1, causal=False, ahead=1, bufs=2)
        mla = Stage("mla", passes=4, per_head=1, causal=False, ahead=1, bufs=2)

        pe_k, pe_v = at(N_CB - 64, 32), at(N_CB - 32, 32)
        w2_k, w2_v = at(N_CB - 256, P), at(N_CB - 128, 64)
        ONEHOT, TABLE, ROWMASK, ROWS, LAMBDAS = Z, Z + SPAN, Z + SPAN + HEADS, Z + 2 * SPAN + HEADS, Z + 3 * SPAN + HEADS
        lam_sum, lam_exp, rpb_out = sem("lam_sum"), sem("lam_exp"), sem("rpb_out")
        consts = [(ident[:], "ident"), (at(ONEHOT, SPAN, 0, BUCKETS), "onehot"), (at(TABLE, HEADS, 0, BUCKETS), "table"),
                  (at(ROWMASK, SPAN, 0, HEADS), "rowmask"), (subln[:], "subln"), (pe_k, "pe_k"), (pe_v, "pe_v"),
                  (w2_k, "w2_k"), (w2_v, "w2_v")]

        def setup_scalar(act):
            act.dma_start(x[:].rearrange("p (t d) -> p t d", t=NT), A["x"].rearrange("(t p) d -> p t d", p=P))\
                .then_inc(x_in, 16)
            load_gain(act, 0)
            for dst, name in consts:
                act.dma_start(dst, A[name]).then_inc(const_in, 16)
            act.dma_start(at(LAMBDAS, 256), bass.AP(A["lambdas"].tensor, 0, [[0, P], [1, 256]])).then_inc(const_in, 16)
            act.dma_start(rpb_rows, bass.AP(A["rpb"].tensor, 0, [[0, GRID_W], [1, RPB_LEN]])).then_inc(rpb_out, 16)
            for b in range(2):
                act.wait_ge(w_loaded[b], 16)
                nc.scalar.activation(w_hi[b][:], stage[b][:], ACT.Copy).then_inc(w_high, 1)
            act.wait_ge(lam_sum, 2)
            nc.scalar.activation(neg_lam[:, 2:4], neg_lam[:, 0:2], ACT.Exp).then_inc(lam_exp, 1)
            act.wait_ge(rows_made, 3)
            act.dma_start(bass.AP(bias_rows.tensor, 0, [[SPAN, HEADS], [HEADS * SPAN, P], [1, SPAN]]),
                          at(ROWS, SPAN, 0, HEADS).unsqueeze(1).to_broadcast([HEADS, P, SPAN])).then_inc(rows_out, 16)

        def setup_pool(pool):
            for b in range(2):
                split_low(pool, b, b)

        def setup_tensor(pe):
            pe.wait_ge(const_in, 16 * (len(consts) + 1))
            for b in range(2):
                mm = nc.tensor.matmul(psum[0:HEADS, b, :], at(TABLE, HEADS, 0, BUCKETS),
                                      at(ONEHOT + b * 512, 512, 0, BUCKETS), start=True, stop=True)
            mm.then_inc(rows_made, 1)

        def setup_vector(dve):
            dve.sem_inc(bank_free["dve"], 4)
            dve.sem_inc(bank_free["act"], 4)
            nc.vector.memset(zero[:], 0.0)
            nc.vector.memset(one[:], 1.0)
            done("dve", nc.vector.memset(half_exp[:], -0.5))
            dve.wait_ge(const_in, 16 * (len(consts) + 1))
            for k in range(2):
                nc.vector.tensor_tensor_reduce(
                    out=at(ROWS + k * 64, 64), in0=at(LAMBDAS + 128 * k, 64), in1=at(LAMBDAS + 128 * k + 64, 64),
                    scale=1.0, scalar=0.0, op0=ALU.mult, op1=ALU.add, accum_out=neg_lam[:, k:k + 1]).then_inc(lam_sum, 1)
            done("dve", nc.vector.tensor_scalar(subln[:], subln[:], 1.0 - LAMBDA_INIT, None, ALU.mult))
            dve.wait_ge(lam_exp, 1)
            done("dve", nc.vector.tensor_tensor(neg_lam[:, 0:1], neg_lam[:, 3:4], neg_lam[:, 2:3], ALU.subtract))
            settle("dve", dve)
            done("dve", nc.vector.tensor_scalar(neg_lam[:, 0:1], neg_lam[:, 0:1], -LAMBDA_INIT, None, ALU.add))
            dve.wait_ge(rows_made, 1)
            for b in range(2):
                nc.vector.tensor_tensor(at(ROWS + b * 512, 512, 0, HEADS), psum[0:HEADS, b, :],
                                        at(ROWMASK + b * 512, 512, 0, HEADS), ALU.add).then_inc(rows_made, 1)
            dve.wait_ge(x_in, 16)

        def load_strips(act, r):
            if r == 0:
                act.wait_ge(rows_out, 16)
            if r >= 2:
                act.wait_ge(strip_used, 4 * (r - 1))
            act.dma_start(at(TAIL + (r % 2) * 4 * STRIP, 4 * STRIP).rearrange("p (h j) -> p h j", h=4),
                          bass.AP(bias_rows.tensor, P - 1 + 4 * SPAN * r,
                                  [[HEADS * SPAN - 1, P], [SPAN, 4], [1, STRIP]])).then_inc(strip_in[r % 2], 16)

        def cut_strips(dve, r):
            dve.wait_ge(strip_in[r % 2], 16 * (r // 2 + 1))
            strips = at(TAIL + (r % 2) * 4 * STRIP, 4 * STRIP).rearrange("p (h j) -> p h j", h=4)
            for qt in range(NT):
                j = 415 - P * qt
                dst = at(N_CB + 4 * r * NT * CMP, 4 * NT * CMP).rearrange("p (h t c) -> p h t c", h=4, t=NT)
                nc.vector.tensor_copy(dst[:, :, qt, :], strips[:, :, j:j + 16 * (CMP - 1) + 1:16]).then_inc(strip_used, 1)

        X, HID = N_P, N_P + 32 * 4 * CMP
        MX, LSUM = HID + 8 * CMP, HID + 8 * CMP + 64
        assert LSUM + 64 <= N_CB - 256
        cmp_x, cmp_hi, cmp_lo = sem("cmp_x"), sem("cmp_hi"), sem("cmp_lo")
        cmp_kv, cmp_kv_taken, cmp_s = sem("cmp_kv"), sem("cmp_kv_taken"), sem("cmp_s")
        cmp_shifted, cmp_exp = sem("cmp_shifted"), sem("cmp_exp")
        XQ = 32 * 4 * CMP // 4

        def compress_vector(dve):
            n = 0
            for side, pos in ((0, pe_k), (1, pe_v)):
                for half in range(2):
                    for gp in range(2):
                        src = at(KT + (2 * side + gp) * T, T, 64 * half, 64 * half + 64)
                        src = bass.AP(src.tensor, src.offset, [src.ap[0], [1, 32], [16, CMP]])
                        dst = at(X, 32 * 4 * CMP, 64 * side, 64 * side + 64).rearrange("p (o q c) -> p o q c", o=32, q=4)
                        nc.vector.tensor_tensor(
                            dst[:, :, 2 * half + gp, :], src,
                            pos[64 * half:64 * half + 64, :].unsqueeze(2).to_broadcast([64, 32, CMP]),
                            ALU.add).then_inc(cmp_x, 1)
            for q in range(4):
                dve.wait_ge(cmp_hi, q + 1)
                nc.vector.tensor_tensor(u_lo[:, q * XQ:(q + 1) * XQ], at(X + q * XQ, XQ),
                                        u_hi[:, q * XQ:(q + 1) * XQ].bitcast(F32), ALU.subtract).then_inc(cmp_lo, 1)
            dve.wait_ge(cmp_kv, 1)
            for half in range(2):
                nc.vector.tensor_copy(at(N_CK, 2 * CMP, 64 * half, 64 * half + 64),
                                      psum[64 * half:64 * half + 64, 2, 2 * CMP * half:2 * CMP * (half + 1)])\
                    .then_inc(cmp_kv_taken, 1)
            nc.vector.tensor_copy(at(N_VC, 256, 0, CMP), psum[0:CMP, 3, 0:256]).then_inc(cmp_kv_taken, 1)
            n = 4 * NT * CMP
            for g in range(4):
                dve.wait_ge(cmp_s, g + 1)
                done("dve", nc.vector.tensor_tensor(at(N_PC + g * n, n), bank(4 + g, n), at(N_CB + g * n, n), ALU.add))
            settle("dve", dve)
            pc = at(N_PC, HEADS * NT * CMP).rearrange("p (h c) -> p h c", c=CMP)

            def spread(off):
                return at(off, 64).unsqueeze(2).to_broadcast([P, 64, CMP])
            done("dve", nc.vector.tensor_reduce(at(MX, 64), pc, AX, ALU.max))
            settle("dve", dve)
            nc.vector.tensor_tensor(pc, pc, spread(MX), ALU.subtract).then_inc(cmp_shifted, 1)
            dve.wait_ge(cmp_exp, 1)
            done("dve", nc.vector.tensor_reduce(at(LSUM, 64), pc, AX, ALU.add))
            settle("dve", dve)
            done("dve", nc.vector.reciprocal(at(LSUM, 64), at(LSUM, 64)))
            settle("dve", dve)
            r = at(LSUM, 64).rearrange("p (h t) -> p h t", t=NT)
            g0 = gate[:].rearrange("p (t h b) -> p h t b", t=NT, b=3)[:, :, :, 0]
            done("dve", nc.vector.tensor_tensor(r, r, g0, ALU.mult))
            settle("dve", dve)
            done("dve", nc.vector.memset(r[0:CMP, :, 0:1], 0.0))
            settle("dve", dve)
            done("dve", nc.vector.tensor_tensor(pc, pc, spread(LSUM), ALU.mult))

        def compress_scalar(act):
            act.wait_ge(cmp_x, 8)
            for q in range(4):
                nc.scalar.activation(u_hi[:, q * XQ:(q + 1) * XQ], at(X + q * XQ, XQ), ACT.Copy).then_inc(cmp_hi, 1)

            def hidden(i, j):
                nc.scalar.activation(at(HID, 4 * CMP), bank(0, 4 * CMP), ACT.Silu)
                return nc.scalar.activation(at(HID + 4 * CMP, 4 * CMP), bank(1, 4 * CMP), ACT.Silu)
            project_scalar(act, "nsa_cmp", hidden, banks=1)
            act.wait_ge(cmp_shifted, 1)
            pc = at(N_PC, HEADS * NT * CMP)
            nc.scalar.activation(pc, pc, ACT.Exp).then_inc(cmp_exp, 1)

        def compress_tensor(pe):
            run = RUNS["nsa_cmp"]
            n = 4 * CMP
            pe.wait_ge(cmp_lo, 4)
            wait_bank(pe, run, 0, 3)
            for a in range(2):
                b = (run["unit"] + a) % 2
                pe.wait_ge(w_ready, run["unit"] + a + 1)
                for o in range(16):
                    for side in range(2):
                        rows = slice(64 * side, 64 * side + 64)
                        for wl, ul in ((0, 1), (1, 0), (0, 0)):
                            c = (16 * a + o) * n
                            mm = nc.tensor.matmul(
                                bank(side, n), (w_lo if wl else w_hi)[b][rows, o * P:(o + 1) * P],
                                (u_lo if ul else u_hi)[rows, c:c + n],
                                start=(a == 0 and o == 0 and (wl, ul) == (0, 1)),
                                stop=(a == 1 and o == 15 and (wl, ul) == (0, 0)))
                mm.then_inc(*((w_used, 1) if a == 0 else (bank_done, 4)))
            pe.wait_ge(bank_free["act"], run["taken"] + 8)
            nc.tensor.matmul(bank(2, n), w2_k, at(HID, n), start=True, stop=True)
            for half in range(2):
                for gp in range(2):
                    q = 2 * half + gp
                    mm = nc.tensor.matmul(psum[0:CMP, 3, (2 * gp + half) * 64:(2 * gp + half + 1) * 64],
                                          at(HID + n + q * CMP, CMP), w2_v, start=True, stop=True)
            mm.then_inc(cmp_kv, 1)
            pe.wait_ge(cmp_kv_taken, 3)
            for g in range(4):
                gp, half = g // 2, g % 2
                rows = (64 * half, 64 * half + 64)
                for j in range(4):
                    for qt in range(NT):
                        c = (j * NT + qt) * CMP
                        mm = nc.tensor.matmul(psum[:, 4 + g, c:c + CMP], at(QT + (4 * gp + j) * T + qt * P, P, *rows),
                                              at(N_CK + gp * CMP, CMP, *rows), start=True, stop=True)
                mm.then_inc(cmp_s, 1)

        SQ, ONES, RSTD, ROWS_R = TAIL, TAIL + DIFF_HEADS * T, TAIL + DIFF_HEADS * T + 1, TAIL + DIFF_HEADS * T + 64
        NR = DIFF_HEADS * NT
        sub_sq, sub_sum, sub_in, sub_pow, sub_ones = (sem(f"sub_{n}") for n in ("sq", "sum", "in", "pow", "ones"))
        sub_turned, sub_rows, sub_spread, sub_scaled, sub_out = \
            (sem(f"sub_{n}") for n in ("turned", "rows", "spread", "scaled", "out"))

        def subln_scalar(act):
            for u in range(DIFF_HEADS):
                nc.scalar.activation(at(SQ + u * T), at(QT + u * T), ACT.Square).then_inc(sub_sq, 1)

        def subln_tensor(pe):
            pe.wait_ge(sub_ones, 1)
            for u in range(DIFF_HEADS):
                pe.wait_ge(sub_sq, u + 1)
                for t in range(NT):
                    r = u * NT + t
                    mm = nc.tensor.matmul(psum[:, 0, r:r + 1], at(SQ + u * T + t * P, P), at(ONES, 1), start=True, stop=True)
            mm.then_inc(sub_sum, 1)
            pe.wait_ge(sub_pow, 1)
            nc.tensor.transpose(psum[0:NR, 1, 0:P], at(RSTD, NR), ident[:]).then_inc(sub_turned, 1)
            pe.wait_ge(sub_rows, 1)
            for u in range(DIFF_HEADS):
                for t in range(NT):
                    r = u * NT + t
                    mm = nc.tensor.matmul(bank(u)[:, t * P:(t + 1) * P], ident[0:NR, r:r + 1].to_broadcast([NR, P]),
                                          at(ROWS_R, P, 0, NR), start=True, stop=True)
                mm.then_inc(sub_spread, 1)

        def subln_vector(dve):
            nc.vector.memset(at(ONES, 1), 1.0 / P).then_inc(sub_ones, 1)
            dve.wait_ge(sub_sum, 1)
            nc.vector.tensor_scalar(at(RSTD, NR), psum[:, 0, 0:NR], EPS, None, ALU.add).then_inc(sub_in, 1)
            dve.wait_ge(sub_turned, 1)
            nc.vector.tensor_copy(at(ROWS_R, P, 0, NR), psum[0:NR, 1, 0:P]).then_inc(sub_rows, 1)
            for u in range(DIFF_HEADS):
                dve.wait_ge(sub_spread, u + 1)
                nc.vector.scalar_tensor_tensor(out=at(QT + u * T), in0=bank(u), scalar=subln[:, u:u + 1],
                                               in1=at(QT + u * T), op0=ALU.mult, op1=ALU.mult).then_inc(sub_scaled, 1)
                dve.wait_ge(sub_scaled, u + 1)
                nc.vector.tensor_tensor(at(Z + u * T), at(Z + u * T), at(QT + u * T), ALU.mult).then_inc(sub_out, 1)

        def subln_pool(pool):
            pool.wait_ge(sub_in, 1)
            nc.gpsimd.tensor_tensor(at(RSTD, NR), at(RSTD, NR), half_exp[:, 0:1].to_broadcast([P, NR]), ALU.pow)\
                .then_inc(sub_pow, 1)

        PP, PIN, E = 4096, 0, Z
        p_in, p_turned, p_hi = sem("p_in"), sem("p_turned"), sem("p_hi")
        e_used, e_mul = sem("e_used"), sem("e_mul")

        def p_place(u, t):
            return u[:].rearrange("p (c t) -> p c t", c=KC)[:, 0:2, t * P:(t + 1) * P]

        def p_bank(t):
            return psum[:, t, 0:2 * P].rearrange("p (c t) -> p c t", c=2)

        def ple_tensor(pe, nth):
            pe.wait_ge(p_in, 16 * (nth + 1))
            for t in range(NT):
                for c in range(2):
                    tr = nc.tensor.transpose(psum[:, t, c * P:(c + 1) * P], at(PIN + t * PLE + c * P, P), ident[:])
                tr.then_inc(p_turned, 1)

        def ple_scalar(act, nth):
            act.dma_start(at(PIN, NT * PLE).rearrange("p (t c) -> p t c", t=NT),
                          A["p"][nth].rearrange("(t p) c -> p t c", p=P)).then_inc(p_in, 16)
            for t in range(NT):
                act.wait_ge(p_turned, NT * nth + t + 1)
                nc.scalar.activation(p_place(u_hi, t), p_bank(t), ACT.Copy).then_inc(p_hi, 1)

        def ple_vector(dve, nth):
            for t in range(NT):
                dve.wait_ge(p_hi, NT * nth + t + 1)
                nc.vector.tensor_tensor(p_place(u_lo, t), p_bank(t), p_place(u_hi, t).bitcast(F32), ALU.subtract)

        def gate_scalar(act, nth):
            def take(i, j):
                act.wait_ge(e_used, 8 * nth + 4 * i + j + 1)
                return nc.scalar.activation(at(E + j * 512), bank(j), ACT.Sigmoid)
            project_scalar(act, f"ple{nth}_gate", take)

        def gate_vector(dve, nth):
            if nth == 0:
                dve.sem_inc(e_used, 4)
            run = RUNS[f"ple{nth}_gate"]
            for i in blocks_of(dve, run):
                for j in range(4):
                    dve.wait_ge(bank_free["act"], run["taken"] + 4 * i + j + 5)
                    nc.vector.tensor_tensor(at(E + j * 512), at(E + j * 512), at(PP + j * D + i * 512), ALU.mult)\
                        .then_inc(e_mul, 1)
                    dve.wait_ge(e_mul, 8 * nth + 4 * i + j + 1)
                    dst = x[:, bass.ds(j * D + i * 512, 512)] if not isinstance(i, int) else \
                        x[:, j * D + i * 512:j * D + i * 512 + 512]
                    nc.vector.tensor_tensor(dst, dst, at(E + j * 512), ALU.add).then_inc(e_used, 1)

        CQ, LXN, ROPE_K, ROPE_Q = mla.P0, mla.P0 + NT * 640, mla.P0 + 2 * NT * 640, mla.P0 + 2 * NT * 640 + T
        rope_in = sem("rope_in")
        MLA_SCALE = (64 + ROPE) ** -0.5

        def rotate(dve, b, table, tmp, dst):
            done("dve", nc.vector.tensor_tensor(at(tmp, T, 64, 96), psum[64:96, b, :], at(table, T, 64, 96), ALU.mult))
            done("dve", nc.vector.tensor_tensor(at(tmp + T, T, 64, 96), psum[96:128, b, :], at(table, T, 96, 128), ALU.mult))
            settle("dve", dve)
            return nc.vector.tensor_tensor(dst, at(tmp, T, 64, 96), at(tmp + T, T, 64, 96), ALU.add)

        def load_rope(act):
            act.dma_start(at(ROPE_K, 2 * T), A["rope"]).then_inc(rope_in, 16)

        def rope_vector(dve):
            dve.wait_ge(rope_in, 16)
            project_vector(dve, "mla_rope", lambda i, j: rotate(dve, 0, ROPE_K, QT, at(mla.KS, T, 64, 96)), banks=1)

        def mla_q_vector(dve):
            def take(i, j):
                h = 4 * i + j
                u, half = h // 2, h % 2
                nc.vector.tensor_scalar(at(QT + u * T, T, 64 * half, 64 * half + 64), psum[0:64, j, :], MLA_SCALE, None, ALU.mult)
                lo = 32 * (half + 2 * (u // 4))
                return rotate(dve, j, ROPE_Q, CQ + 2 * T * (h % 2), at(TAIL + (u % 4) * T, T, lo, lo + 32))
            project_vector(dve, "mla_q", take)

        @block.tensor
        def _(pe):
            setup_tensor(pe)
            finish("pe", pe)
            norm_tensor(pe, 0, 0, D)
            finish("pe", pe)
            for name in ("nsa_q", "nsa_k", "nsa_v"):
                project_tensor(pe, name)
            project_tensor(pe, "nsa_gate")
            project_tensor(pe, "nsa_z")
            finish("pe", pe)
            compress_tensor(pe)
            finish("pe", pe)
            attend_tensor(pe, nsa, 0)
            attend_tensor(pe, nsa, 1, first=False)
            finish("pe", pe)
            finish("pe", pe)
            project_tensor(pe, "nsa_out")
            finish("pe", pe)
            norm_tensor(pe, 2, 0, D)
            finish("pe", pe)
            for name in ("diff_q", "diff_k", "diff_v", "diff_z"):
                project_tensor(pe, name)
            finish("pe", pe)
            attend_tensor(pe, diff)
            finish("pe", pe)
            subln_tensor(pe)
            finish("pe", pe)
            project_tensor(pe, "diff_out")
            finish("pe", pe)
            norm_tensor(pe, 4, 0, D)
            finish("pe", pe)
            for name in ("na_q", "na_k", "na_v", "na_z"):
                project_tensor(pe, name)
            finish("pe", pe)
            attend_tensor(pe, na)
            finish("pe", pe)
            finish("pe", pe)
            project_tensor(pe, "na_out")
            finish("pe", pe)
            ple_tensor(pe, 0)
            finish("pe", pe)
            project_tensor(pe, "ple0_proj")
            finish("pe", pe)
            norm_tensor(pe, 5, 0, D)
            finish("pe", pe)
            project_tensor(pe, "ple0_gate")
            finish("pe", pe)
            norm_tensor(pe, 6, 0, D)
            finish("pe", pe)
            project_tensor(pe, "mla_cq")
            project_tensor(pe, "mla_ckv")
            project_tensor(pe, "mla_rope", banks=1)
            project_tensor(pe, "mla_z")
            finish("pe", pe)
            norm_tensor(pe, 7, LXN, 640)
            finish("pe", pe)
            for name in ("mla_q", "mla_k", "mla_v"):
                project_tensor(pe, name)
            finish("pe", pe)
            attend_tensor(pe, mla, 0)
            attend_tensor(pe, mla, 1, first=False)
            finish("pe", pe)
            finish("pe", pe)
            project_tensor(pe, "mla_out")
            finish("pe", pe)
            ple_tensor(pe, 1)
            finish("pe", pe)
            project_tensor(pe, "ple1_proj")
            finish("pe", pe)
            norm_tensor(pe, 8, 0, D)
            finish("pe", pe)
            project_tensor(pe, "ple1_gate")
            finish("pe", pe)

        @block.scalar
        def _(act):
            setup_scalar(act)
            finish("act", act)
            norm_scalar(act, 0)
            finish("act", act)
            load_strips(act, 0)
            load_strips(act, 1)
            project_scalar(act, "nsa_q")
            load_strips(act, 2)
            load_strips(act, 3)
            project_scalar(act, "nsa_k")
            project_scalar(act, "nsa_v")
            project_scalar(act, "nsa_gate", lambda i, j: nc.scalar.activation(
                gate[:, j * 48:(j + 1) * 48], bank(j, 48), ACT.Sigmoid))
            project_scalar(act, "nsa_z", silu_features(Z))
            finish("act", act)
            compress_scalar(act)
            finish("act", act)
            attend_scalar(act, nsa, 0)
            attend_scalar(act, nsa, 1, first=False)
            finish("act", act)
            split_output_scalar(act, Z, 0)
            finish("act", act)
            project_scalar(act, "nsa_out")
            finish("act", act)
            norm_scalar(act, 1)
            norm_scalar(act, 2)
            finish("act", act)
            for name in ("diff_q", "diff_k", "diff_v"):
                project_scalar(act, name)
            project_scalar(act, "diff_z", silu_features(Z))
            finish("act", act)
            attend_scalar(act, diff)
            finish("act", act)
            subln_scalar(act)
            split_output_scalar(act, Z, 1)
            finish("act", act)
            project_scalar(act, "diff_out")
            finish("act", act)
            norm_scalar(act, 3)
            norm_scalar(act, 4)
            finish("act", act)
            act.wait_ge(rpb_out, 16)
            act.dma_start(at(na.MASK, GRID_W), A["colmask"]).then_inc(small_in, 16)
            for name in ("na_q", "na_k", "na_v"):
                project_scalar(act, name)
            project_scalar(act, "na_z", silu_features(Z))
            finish("act", act)
            attend_scalar(act, na)
            finish("act", act)
            split_output_scalar(act, Z, 2)
            finish("act", act)
            project_scalar(act, "na_out")
            finish("act", act)
            ple_scalar(act, 0)
            finish("act", act)
            project_scalar(act, "ple0_proj")
            finish("act", act)
            norm_scalar(act, 5)
            finish("act", act)
            gate_scalar(act, 0)
            finish("act", act)
            norm_scalar(act, 6)
            finish("act", act)
            load_rope(act)
            for name in ("mla_cq", "mla_ckv", "mla_rope"):
                project_scalar(act, name)
            project_scalar(act, "mla_z", silu_features(Z))
            finish("act", act)
            norm_scalar(act, 7)
            finish("act", act)
            for name in ("mla_q", "mla_k", "mla_v"):
                project_scalar(act, name)
            finish("act", act)
            attend_scalar(act, mla, 0)
            attend_scalar(act, mla, 1, first=False)
            finish("act", act)
            split_output_scalar(act, Z, 3)
            finish("act", act)
            project_scalar(act, "mla_out")
            finish("act", act)
            ple_scalar(act, 1)
            finish("act", act)
            project_scalar(act, "ple1_proj")
            finish("act", act)
            norm_scalar(act, 8)
            finish("act", act)
            gate_scalar(act, 1)
            finish("act", act)
            xn0 = NT * norm_base(9)[0]
            for t in range(NT):
                act.wait_ge(xn_done, xn0 + t + 1)
                act.dma_start(out[t * P:(t + 1) * P, :], at(t * D, D)).then_inc(out_written, 16)
            act.wait_ge(out_written, 16 * NT)

        @block.gpsimd
        def _(pool):
            setup_pool(pool)
            finish("pool", pool)
            norm_pool(pool, 0)
            finish("pool", pool)
            for name in ("nsa_q", "nsa_k", "nsa_v", "nsa_gate", "nsa_z"):
                project_pool(pool, name)
            finish("pool", pool)
            project_pool(pool, "nsa_cmp")
            finish("pool", pool)
            finish("pool", pool)
            finish("pool", pool)
            project_pool(pool, "nsa_out")
            finish("pool", pool)
            norm_pool(pool, 1)
            norm_pool(pool, 2)
            finish("pool", pool)
            for name in ("diff_q", "diff_k", "diff_v", "diff_z"):
                project_pool(pool, name)
            finish("pool", pool)
            finish("pool", pool)
            subln_pool(pool)
            finish("pool", pool)
            project_pool(pool, "diff_out")
            finish("pool", pool)
            norm_pool(pool, 3)
            norm_pool(pool, 4)
            finish("pool", pool)
            for name in ("na_q", "na_k", "na_v", "na_z"):
                project_pool(pool, name)
            finish("pool", pool)
            attend_pool(pool, na)
            finish("pool", pool)
            finish("pool", pool)
            project_pool(pool, "na_out")
            finish("pool", pool)
            finish("pool", pool)
            project_pool(pool, "ple0_proj")
            finish("pool", pool)
            norm_pool(pool, 5)
            finish("pool", pool)
            project_pool(pool, "ple0_gate")
            finish("pool", pool)
            norm_pool(pool, 6)
            finish("pool", pool)
            for name in ("mla_cq", "mla_ckv", "mla_rope", "mla_z"):
                project_pool(pool, name)
            finish("pool", pool)
            norm_pool(pool, 7)
            finish("pool", pool)
            for name in ("mla_q", "mla_k", "mla_v"):
                project_pool(pool, name)
            finish("pool", pool)
            finish("pool", pool)
            finish("pool", pool)
            project_pool(pool, "mla_out")
            finish("pool", pool)
            finish("pool", pool)
            project_pool(pool, "ple1_proj")
            finish("pool", pool)
            norm_pool(pool, 8)
            finish("pool", pool)
            project_pool(pool, "ple1_gate")
            finish("pool", pool)
            norm_pool(pool, 9)

        def y_tile(t, lo, hi):
            return at(KT + t * D + lo, hi - lo)

        def cq_tile(t, lo, hi):
            return at(CQ + t * 640 + lo, hi - lo)

        def post_norm(dve, k):
            norm_vector(dve, k, y_tile, 0, D)
            dve.wait_ge(xn_done, NT * norm_base(k + 1)[0])
            for t in range(NT):
                done("dve", nc.vector.tensor_tensor(x_tile(t, 0, D), x_tile(t, 0, D), at(t * D, D), ALU.add))
            settle("dve", dve)

        @block.vector
        def _(dve):
            setup_vector(dve)
            finish("dve", dve)
            norm_vector(dve, 0, x_tile, 0, D)
            finish("dve", dve)
            project_vector(dve, "nsa_q", to_features(QT, 0.125))
            cut_strips(dve, 0)
            cut_strips(dve, 1)
            project_vector(dve, "nsa_k", to_features(KT))
            cut_strips(dve, 2)
            cut_strips(dve, 3)
            project_vector(dve, "nsa_v", to_tokens(V, 512))
            finish("dve", dve)
            compress_vector(dve)
            finish("dve", dve)
            attend_vector(dve, nsa, 0)
            attend_vector(dve, nsa, 1, first=False)
            finish("dve", dve)
            split_output_vector(dve, Z, 0)
            finish("dve", dve)
            project_vector(dve, "nsa_out", to_tokens(KT, D))
            finish("dve", dve)
            post_norm(dve, 1)
            norm_vector(dve, 2, x_tile, 0, D)
            finish("dve", dve)
            project_vector(dve, "diff_q", to_features(QT, 0.125))
            project_vector(dve, "diff_k", to_features(KT))
            project_vector(dve, "diff_v", to_tokens(V, D))
            finish("dve", dve)
            attend_vector(dve, diff)
            finish("dve", dve)
            subln_vector(dve)
            split_output_vector(dve, Z, 1)
            finish("dve", dve)
            project_vector(dve, "diff_out", to_tokens(KT, D))
            finish("dve", dve)
            post_norm(dve, 3)
            norm_vector(dve, 4, x_tile, 0, D)
            finish("dve", dve)
            project_vector(dve, "na_q", to_features(QT, 0.125))
            project_vector(dve, "na_k", to_features(KT))
            project_vector(dve, "na_v", to_tokens(V, D))
            dve.wait_ge(small_in, 16)
            finish("dve", dve)
            attend_vector(dve, na)
            finish("dve", dve)
            split_output_vector(dve, Z, 2)
            finish("dve", dve)
            project_vector(dve, "na_out", add_residual)
            finish("dve", dve)
            ple_vector(dve, 0)
            finish("dve", dve)
            project_vector(dve, "ple0_proj", to_tokens(PP, D))
            finish("dve", dve)
            norm_vector(dve, 5, x_tile, 0, D)
            finish("dve", dve)
            gate_vector(dve, 0)
            finish("dve", dve)
            norm_vector(dve, 6, x_tile, 0, D)
            finish("dve", dve)
            project_vector(dve, "mla_cq", to_tokens(CQ, 640, Q_RANK))
            project_vector(dve, "mla_ckv", to_tokens(CQ + Q_RANK, 640, KV_RANK))
            rope_vector(dve)
            finish("dve", dve)
            norm_vector(dve, 7, cq_tile, LXN, 640)
            finish("dve", dve)
            mla_q_vector(dve)
            project_vector(dve, "mla_k", to_features(KT))
            project_vector(dve, "mla_v", to_tokens(V, D))
            finish("dve", dve)
            attend_vector(dve, mla, 0)
            attend_vector(dve, mla, 1, first=False)
            finish("dve", dve)
            split_output_vector(dve, Z, 3)
            finish("dve", dve)
            project_vector(dve, "mla_out", add_residual)
            finish("dve", dve)
            ple_vector(dve, 1)
            finish("dve", dve)
            project_vector(dve, "ple1_proj", to_tokens(PP, D))
            finish("dve", dve)
            norm_vector(dve, 8, x_tile, 0, D)
            finish("dve", dve)
            gate_vector(dve, 1)
            finish("dve", dve)
            norm_vector(dve, 9, x_tile, 0, D)


def _constants():
    n = np.arange(SPAN)
    dist = np.maximum(511 - n, 0)
    exact = BUCKETS // 2
    nf = np.maximum(dist, 1).astype(np.float32)
    large = exact + (np.log(nf / np.float32(exact)) / np.float32(np.log(128 / exact))
                     * np.float32(BUCKETS - exact)).astype(np.int32)
    bucket = np.where(dist < exact, dist, np.minimum(large, BUCKETS - 1))
    onehot = (np.arange(BUCKETS)[:, None] == bucket[None, :]).astype(np.float32)
    rowmask = np.tile(np.where(511 - n >= 0, 0.0, MASKED).astype(np.float32), (HEADS, 1))
    col = np.arange(GRID_W)
    start = np.clip(col - 8, 0, GRID_W - 16)
    inside = (col[None, :] >= start[:, None]) & (col[None, :] < start[:, None] + 16)
    colmask = np.tile(np.where(inside, 0.0, MASKED).astype(np.float32), (2, 1))
    inv = (1.0 / (np.float32(10000.0) ** (np.arange(0, ROPE, 2, dtype=np.float32) / np.float32(ROPE)))).astype(np.float32)
    ang = np.arange(T, dtype=np.float32)[None, :] * inv[:, None]
    cos, sin = np.cos(ang), np.sin(ang)
    rope = np.zeros((P, T), np.float32)
    rope[64:96] = np.concatenate([cos, cos])
    rope[96:128] = np.concatenate([-sin, sin])
    rope = np.concatenate([rope, rope * np.float32((64 + ROPE) ** -0.5)], axis=1)
    return dict(onehot=onehot, rowmask=rowmask, colmask=colmask, rope=rope, ident=np.eye(P, dtype=np.float32))


def _units(w, run):
    units = []
    for i in range(run["blocks"]):
        k = 0
        for nk in run["nks"]:
            part = w[k * P:(k + nk) * P, i * run["width"]:(i + 1) * run["width"]]
            u = np.zeros((P, UNIT), w.dtype)
            u[:, :nk * run["width"]] = part.reshape(nk, P, run["width"]).transpose(1, 0, 2).reshape(P, -1)
            units.append(u)
            k += nk
    return units


def _layout(inputs):
    f = {k: np.asarray(v) for k, v in inputs.items()}
    w = f["nsa_w_in"][0]
    kv = [w[:, D + 256 * n:D + 256 * (n + 1)] for n in range(6)]
    slots = np.array([(2 * gp + half) * 4 + j for gp in range(2) for j in range(4) for half in range(2)])
    cols = (slots[:, None] * 64 + np.arange(64)).reshape(-1)
    mats = {"nsa_q": w[:, :D][:, cols], "nsa_k": np.concatenate([kv[0], kv[1], kv[2], kv[4]], 1),
            "nsa_v": np.concatenate([kv[3], kv[5]], 1), "nsa_gate": w[:, 2560:2608], "nsa_z": w[:, 2608:][:, cols],
            "nsa_out": f["nsa_w_out"][0][cols]}
    for n, name in enumerate(("q", "k", "v", "z")):
        mats[f"diff_{name}"] = f["diff_w_in"][0][:, n * D:(n + 1) * D]
        mats[f"na_{name}"] = f["na_w_in_2"][0][:, n * D:(n + 1) * D]
    mats["diff_out"], mats["na_out"], mats["mla_out"] = f["diff_w_out"][0], f["na_w_out_2"][0], f["mla_w_out_2"][0]
    w = f["mla_w_in_2"][0]
    mats["mla_cq"], mats["mla_ckv"] = w[:, :Q_RANK], w[:, Q_RANK:Q_RANK + KV_RANK]
    r = w[:, Q_RANK + KV_RANK:Q_RANK + KV_RANK + ROPE]
    swapped = np.concatenate([r[:, 16:], r[:, :16]], 1)
    mats["mla_rope"] = np.concatenate([r, swapped, r, swapped], 1)
    mats["mla_z"] = w[:, Q_RANK + KV_RANK + ROPE:]
    q = f["mla_w_qb_2"][0].reshape(Q_RANK, HEADS, 96)
    mats["mla_q"] = np.concatenate([q, q[:, :, 80:96], q[:, :, 64:80]], 2).reshape(Q_RANK, HEADS * P)
    k = f["mla_w_kvb_2"][0].reshape(KV_RANK, HEADS, P)
    mats["mla_k"], mats["mla_v"] = k[:, :, :64].reshape(KV_RANK, D), k[:, :, 64:].reshape(KV_RANK, D)
    for i in range(2):
        mats[f"ple{i}_gate"], mats[f"ple{i}_proj"] = f["ple_w_gate_2"][i], f["ple_w_proj_2"][i]
    units = []
    for name, run in RUNS.items():
        if name == "nsa_cmp":
            w1 = [f[n][0].reshape(32, 64, P).transpose(1, 0, 2).reshape(64, 32 * P) for n in ("nsa_cmp_w1_k", "nsa_cmp_w1_v")]
            w1 = np.concatenate(w1, 0)
            units += [w1[:, :UNIT], w1[:, UNIT:]]
        else:
            units += _units(mats[name], run)
    latent = np.zeros(D, np.float32)
    latent[:Q_RANK], latent[Q_RANK:Q_RANK + KV_RANK] = f["mla_q_norm_2"][0], f["mla_kv_norm_2"][0]
    gains = [f["norm_pre"][0], f["norm_post"][0], f["norm_pre"][1], f["norm_post"][1], f["norm_g_2"][0],
             f["ple_norm_2"][0], f["norm_g_2"][1], latent, f["ple_norm_2"][1], f["final_norm_2"]]
    rpb = np.zeros((1, RPB_LEN), np.float32)
    rpb[0, RPB_PAD:-RPB_PAD] = f["na_rpb_2"][0].reshape(-1)
    twice = lambda a: np.concatenate([a, a], 0)
    data = dict(
        x=f["x"][0], weights=np.stack(units), gains=np.stack(gains), table=f["rel_bias_table"],
        subln=f["diff_subln"][0].reshape(DIFF_HEADS, P).T,
        pe_k=twice(f["nsa_cmp_pe_k"][0].T), pe_v=twice(f["nsa_cmp_pe_v"][0].T),
        w2_k=twice(f["nsa_cmp_w2_k"][0].T).T, w2_v=f["nsa_cmp_w2_v"][0],
        lambdas=np.concatenate([f[f"diff_lambda_{n}"] for n in ("q1", "k1", "q2", "k2")], 1), rpb=rpb, p=f["p_2"][:, 0])
    data.update(_constants())
    return {k: np.ascontiguousarray(v) for k, v in data.items()}


def kernel(**inputs):
    import concourse.bacc as bacc
    from concourse.bass_utils import run_bass_kernel_spmd

    data = _layout(inputs)
    nc = bacc.Bacc("TRN2", target_bir_lowering=False, num_devices=1)
    aps = {k: nc.dram_tensor(f"in_{k}", v.shape, F32, kind="ExternalInput").ap() for k, v in data.items()}
    out = nc.dram_tensor("out_x", (T, D), F32, kind="ExternalOutput").ap()
    _program(nc, aps, out)
    r = run_bass_kernel_spmd(nc, [{f"in_{k}": v for k, v in data.items()}], core_ids=[0])
    return r.results[0]["out_x"].reshape(1, T, D)
```

```python
from contextlib import ExitStack, contextmanager

import numpy as np

import concourse.bass as bass
from concourse import mybir

F32 = mybir.dt.float32
F32R = mybir.dt.float32r
ALU = mybir.AluOpType
ACT = mybir.ActivationFunctionType
AX = mybir.AxisListType.X

P = 128
D = 1024
T = 512
NT = T // P
KC = D // P
UNIT = 2048
EPS = 1e-6
BIG = 3.0e38
MASKED = -1e30
BUCKETS = 32
HEADS = 16
DIFF_HEADS = 8
LAMBDA_INIT = 0.8 - 0.6 * float(np.exp(-0.3))
SPAN = 1024
STRIP = 896
CMP = 31
GRID_W = 64
RPB_ROW, RPB_HEAD = 31, 15 * 31
RPB_PAD = 48
RPB_LEN = HEADS * RPB_HEAD + 2 * RPB_PAD
Q_RANK, KV_RANK = 384, 256
ROPE = 32
PLE = 256

RUNS = {}
N_UNITS = 0
N_BLOCKS = 0


def _run(name, blocks, nks, width, mode, k0=0):
    global N_UNITS, N_BLOCKS
    taker = "act" if name.endswith(("_z", "gate", "cmp")) else "dve"
    RUNS[name] = dict(name=name, blocks=blocks, nks=nks, width=width, mode=mode, k0=k0,
                      unit=N_UNITS, block=N_BLOCKS, taker=taker,
                      taken=sum(4 * r["blocks"] for r in RUNS.values() if r["taker"] == taker),
                      others=sum(4 * r["blocks"] for r in RUNS.values() if r["taker"] != taker))
    N_UNITS += blocks * len(nks)
    N_BLOCKS += blocks


_run("nsa_q", 2, (4, 4), 512, "features")
_run("nsa_k", 2, (4, 4), 512, "features")
_run("nsa_v", 1, (4, 4), 512, "tokens")
_run("nsa_gate", 1, (8,), 48, "tokens")
_run("nsa_z", 2, (4, 4), 512, "features")
_run("nsa_cmp", 1, (16, 16), 128, "compress")
_run("nsa_out", 2, (4, 4), 512, "tokens")
_run("diff_q", 2, (4, 4), 512, "features")
_run("diff_k", 2, (4, 4), 512, "features")
_run("diff_v", 2, (4, 4), 512, "tokens")
_run("diff_z", 2, (4, 4), 512, "features")
_run("diff_out", 2, (4, 4), 512, "tokens")
_run("na_q", 2, (4, 4), 512, "features")
_run("na_k", 2, (4, 4), 512, "features")
_run("na_v", 2, (4, 4), 512, "tokens")
_run("na_z", 2, (4, 4), 512, "features")
_run("na_out", 2, (4, 4), 512, "tokens")
_run("ple0_proj", 2, (2,), 512, "tokens")
_run("ple0_gate", 2, (4, 4), 512, "tokens")
_run("mla_cq", 1, (4, 4), 384, "tokens")
_run("mla_ckv", 1, (4, 4), 256, "tokens")
_run("mla_rope", 1, (8,), 128, "features")
_run("mla_z", 2, (4, 4), 512, "features")
_run("mla_q", 4, (3,), 512, "features")
_run("mla_k", 2, (2,), 512, "features", 3)
_run("mla_v", 2, (2,), 512, "tokens", 3)
_run("mla_out", 2, (4, 4), 512, "tokens")
_run("ple1_proj", 2, (2,), 512, "tokens")
_run("ple1_gate", 2, (4, 4), 512, "tokens")

GAINS = ["pre0", "post0", "pre1", "post1", "na", "ple0", "mla", "latent", "ple1", "final"]


def tri(n):
    return P * n * (n + 1) // 2


@contextmanager
def repeat(eng, first, end):
    if end == first + 1:
        yield first
    else:
        with eng.Fori(first, end) as i:
            yield i


LOOK = 2


class Attention:

    def __init__(self, name, passes, per_head, causal, ahead, bufs, cmp=False):
        self.name, self.passes, self.per_head, self.causal = name, passes, per_head, causal
        self.maps = 2 * per_head
        self.ahead, self.bufs = ahead, bufs
        diff = name == "diff"
        self.turns = []
        for a in range(2):
            if cmp:
                self.turns.append(("cmp", a, None))
            if diff:
                self.turns.append(("full", a, 2 * a))
            else:
                self.turns += [("full", a, per_head * a + b) for b in range(per_head)]
        self.use = []
        n = 0
        for kind, _, _ in self.turns:
            self.use.append(n)
            n += 1 if kind == "cmp" else NT
        self.uses = n
        self.tiles = [(t, kt) for t, (kind, _, _) in enumerate(self.turns) for kt in range(1 if kind == "cmp" else NT)]
        self.credit = 2 * n
        self.diff = diff
        self.maps_per_turn = 2 if diff else 1
        self.mla = name == "mla"

    def length(self, qt):
        return P * (qt + 1) if self.causal else T

    def p_at(self, qt):
        return tri(qt) if self.causal else T * qt

    def p_size(self):
        return tri(NT) if self.causal else NT * T

    def pt_at(self, kt):
        return tri(NT) - tri(NT - kt) if self.causal else T * kt

    def first_q(self, kt):
        return kt if self.causal else 0

    def turn_of(self, m):
        if self.diff:
            m = m - m % 2
        return next(t for t, (kind, _, mm) in enumerate(self.turns) if kind == "full" and mm == m)

    def released(self, m):
        return self.turned_by(m - self.bufs)

    def turned_by(self, m):
        return (m // self.maps) * self.uses + self.use[self.turn_of(m % self.maps)] + NT - 1

    def last_use(self, head):
        return max(self.use[t] + (NT if k == "full" else 1) - 1
                   for t, (k, a, _) in enumerate(self.turns) if a == head)

    def scores_beside(self, n):
        t, kt = self.tiles[n]
        kind, _, m = self.turns[t]
        if kind == "cmp" or kt < LOOK:
            return []
        step = self.maps_per_turn
        flat = [(m + self.ahead + s, qt) for s in range(step) for qt in range(NT)]
        share = len(flat) // (NT - LOOK)
        return flat[share * (kt - LOOK):share * (kt - LOOK + 1)]

    def first_turn(self, t):
        return self.turns[t][0] == "full" and (t == 0 or self.turns[t - 1][:2] != self.turns[t][:2])

    def head_end(self, a):
        return self.last_use(a) + 1

    def high_index(self, t):
        return NT * sum(kind == "full" for kind, _, _ in self.turns[:t])


NORMS = [("pre0", ((0, D),), KC, 0), ("post0", ((0, D),), 0, 1), ("pre1", ((0, D),), KC, 2),
         ("post1", ((0, D),), 0, 3), ("na", ((0, D),), KC, 4), ("ple0", ((0, D),), KC, 5),
         ("mla", ((0, D),), KC, 6), ("latent", ((0, Q_RANK), (Q_RANK, Q_RANK + KV_RANK)), 5, 7),
         ("ple1", ((0, D),), KC, 8), ("final", ((0, D),), 0, 9)]


def norm_base(k):
    seg = sum(len(n[1]) for n in NORMS[:k])
    banks = sum((2 * NT if n[2] else 0) for n in NORMS[:k])
    return seg, k, banks


def _program(nc, A, out):
    with ExitStack() as ctx:
        def sb(name, cols, dt=F32):
            return ctx.enter_context(nc.sbuf_tensor(name, [P, cols], dt))

        def sem(name):
            return ctx.enter_context(nc.semaphore(name))

        x = sb("x", NT * D)
        u_hi, u_lo = sb("u_hi", KC * T, F32R), sb("u_lo", KC * T, F32R)
        stage = [sb(f"stage{b}", UNIT) for b in range(2)]
        w_hi = [sb(f"w_hi{b}", UNIT, F32R) for b in range(2)]
        w_lo = [sb(f"w_lo{b}", UNIT, F32R) for b in range(2)]
        gain = [sb(f"gain{b}", D) for b in range(2)]
        ident = sb("ident", P)
        ss = sb("ss", 2 * NT)
        ms = sb("ms", 2 * NT)
        half_exp = sb("half_exp", 1)
        neg_max = sb("neg_max", 4 * NT)
        row_sum = sb("row_sum", 4 * NT)
        inv = sb("inv", 4 * NT)
        zero, one = sb("zero", 1), sb("one", 1)
        neg_lam = sb("neg_lam", 4)
        gate = sb("gate", NT * 48)
        subln = sb("subln", DIFF_HEADS)
        spare_r = sb("spare_r", 2 * T, F32R)
        ARENA = 25096
        arena = sb("arena", ARENA)
        psum = ctx.enter_context(nc.psum_tensor("psum", [P, 8, 512], F32))

        def bank(n, width=512):
            return psum[:, n, 0:width]

        def at(off, width=512, lo=0, hi=P):
            return arena[lo:hi, bass.ds(off, width)] if not isinstance(off, int) else arena[lo:hi, off:off + width]

        QT, KT, V, Z = 0, 4096, 8192, 12288
        TAIL = 16384
        N_CK, N_VC, N_PC = TAIL, TAIL + 64, TAIL + 64 + 4 * P
        N_P = N_PC + HEADS * NT * CMP
        N_CB = ARENA - HEADS * NT * CMP
        bias_rows = nc.dram_tensor("bias_rows", (P, HEADS * SPAN), F32, kind="Internal").ap()
        rpb_rows = nc.dram_tensor("rpb_rows", (GRID_W, RPB_LEN), F32, kind="Internal").ap()

        w_loaded = [sem(f"w_loaded{b}") for b in range(2)]
        w_high, w_ready = sem("w_high"), sem("w_ready")
        w_used = sem("w_used")
        bank_done = sem("bank_done")
        bank_free = {"act": sem("bank_free_act"), "dve": sem("bank_free_dve")}
        stage_end, held = sem("stage_end"), sem("held")
        x_in, const_in, small_in = sem("x_in"), sem("const_in"), sem("small_in")
        gain_in = [sem("gain_in0"), sem("gain_in1")]
        out_written = sem("out_written")
        rows_made, rows_out = sem("rows_made"), sem("rows_out")
        strip_in, strip_used = [sem("strip_in0"), sem("strip_in1")], sem("strip_used")
        sq_done, ms_done, rstd_done, xn_done = sem("sq_done"), sem("ms_done"), sem("rstd_done"), sem("xn_done")
        turned, u_hi_done = sem("turned"), sem("u_hi_done")
        dve_step, act_step, pool_step, pe_step = sem("dve_step"), sem("act_step"), sem("pool_step"), sem("pe_step")
        own = {"dve": [dve_step, 0], "act": [act_step, 0], "pool": [pool_step, 0], "pe": [pe_step, 0]}

        def done(who, ins):
            own[who][1] += 1
            ins.then_inc(own[who][0], 1)

        def settle(who, eng):
            eng.wait_ge(own[who][0], own[who][1])

        stages = {"pe": 0, "act": 0, "dve": 0, "pool": 0}

        def finish(who, eng):
            stages[who] += 1
            eng.drain().then_inc(stage_end, 1)
            eng.wait_ge(stage_end, 4 * stages[who])

        def hold(eng):
            eng.sem_inc(held, 1)

        block = ctx.enter_context(nc.Block())

        @block.sync
        def _(sp):
            def unit(n, b):
                sp.dma_start(stage[b][:], A["weights"][n]).then_inc(w_loaded[b], 16)

            unit(0, 0)
            unit(1, 1)
            assert N_UNITS % 2 == 0
            with sp.Fori(1, N_UNITS // 2) as i:
                for b in range(2):
                    sp.wait_ge(w_ready, 2 * i + b - 1)
                    sp.dma_start(stage[b][:], A["weights"][bass.ds(2 * i + b, 1)].rearrange("o p n -> p (o n)"))\
                        .then_inc(w_loaded[b], 16)
            sp.wait_ge(out_written, 16 * NT)

        def split_high(act, n, b, arrivals):
            act.wait_ge(w_loaded[b], 16 * arrivals)
            nc.scalar.activation(w_hi[b][:], stage[b][:], ACT.Copy).then_inc(w_high, 1)

        def split_low(pool, n, b):
            pool.wait_ge(w_high, n + 1)
            nc.gpsimd.tensor_tensor(w_lo[b][:], stage[b][:], w_hi[b][:].bitcast(F32), ALU.subtract)\
                .then_inc(w_ready, 1)

        def pairs_before(run):
            return sum(r["blocks"] for r in RUNS.values() if r["unit"] < run["unit"] and len(r["nks"]) == 2)

        def blocks_of(eng, run):
            if len(run["nks"]) == 2 and run["name"] != "ple1_gate" and run["blocks"] > 1:
                with eng.Fori(0, run["blocks"]) as i:
                    yield i
            else:
                yield from range(run["blocks"])

        def next_unit(run, i, a):
            u = len(run["nks"])
            b = (run["unit"] + a + (0 if u == 2 else i)) % 2
            n = run["unit"] + u * i + a + 2
            if u == 2:
                return n, b, (run["unit"] + a) // 2 + i + 2
            return n, b, n // 2 + 1

        def exists(n):
            return not isinstance(n, int) or n < N_UNITS

        def wait_used(eng, run, i, a):
            if a + 1 < len(run["nks"]):
                eng.wait_ge(w_used, pairs_before(run) + i + 1)
            else:
                eng.wait_ge(bank_done, 4 * (run["block"] + i) + 4)

        def wait_bank(pe, run, i, j):
            other = "dve" if run["taker"] == "act" else "act"
            pe.wait_ge(bank_free[run["taker"]], run["taken"] + 4 * i + j + 1)
            pe.wait_ge(bank_free[other], run["others"] + j + 1)

        def project_tensor(pe, name, banks=4):
            run = RUNS[name]
            w = run["width"]
            for i in blocks_of(pe, run):
                k0 = run["k0"]
                for a, nk in enumerate(run["nks"]):
                    u = len(run["nks"])
                    b = (run["unit"] + a + (0 if u == 2 else i)) % 2
                    pe.wait_ge(w_ready, run["unit"] + u * i + a + 1)
                    for j in range(banks):
                        if a == 0:
                            wait_bank(pe, run, i, j if banks == 4 else 3)
                        for k in range(nk):
                            for wl, ul in ((0, 1), (1, 0), (0, 0)):
                                ww = (w_lo if wl else w_hi)[b]
                                uu = u_lo if ul else u_hi
                                at_u = (k0 + k) * T
                                if run["mode"] == "features":
                                    lhs, rhs = ww[:, k * w + j * P:k * w + (j + 1) * P], uu[:, at_u:at_u + T]
                                    dst = bank(j)
                                else:
                                    lhs, rhs = uu[:, at_u + j * P:at_u + (j + 1) * P], ww[:, k * w:(k + 1) * w]
                                    dst = bank(j, w)
                                mm = nc.tensor.matmul(dst, lhs, rhs, start=(a == 0 and k == 0 and (wl, ul) == (0, 1)),
                                                      stop=(a + 1 == u and k + 1 == nk and (wl, ul) == (0, 0)))
                        if a + 1 == u:
                            mm.then_inc(bank_done, 4 // banks)
                    if a + 1 < u:
                        mm.then_inc(w_used, 1)
                    k0 += nk

        def project_pool(pool, name):
            run = RUNS[name]
            for i in blocks_of(pool, run):
                for a in range(len(run["nks"])):
                    n, b, _ = next_unit(run, i, a)
                    if exists(n):
                        split_low(pool, n, b)

        def project_scalar(act, name, take=None, banks=4):
            run = RUNS[name]
            for i in blocks_of(act, run):
                for a in range(len(run["nks"])):
                    if a + 1 == len(run["nks"]) and take:
                        for j in range(banks):
                            act.wait_ge(bank_done, 4 * (run["block"] + i) + (j + 1 if banks == 4 else 4))
                            take(i, j).then_inc(bank_free["act"], 4 // banks)
                    n, b, arrivals = next_unit(run, i, a)
                    if exists(n):
                        wait_used(act, run, i, a)
                        split_high(act, n, b, arrivals)

        def project_vector(dve, name, take, banks=4):
            run = RUNS[name]
            for i in blocks_of(dve, run):
                for j in range(banks):
                    dve.wait_ge(bank_done, 4 * (run["block"] + i) + (j + 1 if banks == 4 else 4))
                    take(i, j).then_inc(bank_free["dve"], 4 // banks)

        def to_features(place, scale=1.0):
            def take(i, j):
                return nc.vector.tensor_scalar(at(place + j * T + i * 4 * T), bank(j), scale, None, ALU.mult)
            return take

        def to_tokens(place, row, width=512):
            def take(i, j):
                return nc.vector.tensor_scalar(at(place + j * row + i * 512, width), bank(j, width), 1.0, None, ALU.mult)
            return take

        def silu_features(place):
            def take(i, j):
                return nc.scalar.activation(at(place + j * T + i * 4 * T), bank(j), ACT.Silu)
            return take

        def add_residual(i, j):
            dst = x[:, bass.ds(j * D + i * 512, 512)] if not isinstance(i, int) else x[:, j * D + i * 512:j * D + i * 512 + 512]
            return nc.vector.tensor_tensor(dst, bank(j), dst, ALU.add)

        def seg_gain(k, s):
            lo, hi = NORMS[k][1][s]
            return gain[k % 2][:, lo:hi]

        def load_gain(act, k):
            act.dma_start(gain[k % 2][:], bass.AP(A["gains"].tensor, k * D, [[0, P], [1, D]])).then_inc(gain_in[k % 2], 16)

        def norm_vector(dve, k, src, xn, row):
            seg0, _, bank0 = norm_base(k)
            segs = NORMS[k][1]
            for s, (lo, hi) in enumerate(segs):
                for t in range(NT):
                    nc.vector.tensor_tensor_reduce(
                        out=at(xn + t * row + lo, hi - lo), in0=src(t, lo, hi), in1=src(t, lo, hi), scale=1.0,
                        scalar=0.0, op0=ALU.mult, op1=ALU.add,
                        accum_out=ss[:, s * NT + t:s * NT + t + 1]).then_inc(sq_done, 1)
                dve.wait_ge(sq_done, NT * (seg0 + s + 1))
                nc.vector.tensor_scalar(ms[:, s * NT:(s + 1) * NT], ss[:, s * NT:(s + 1) * NT], 1.0 / (hi - lo), EPS,
                                        ALU.mult, ALU.add).then_inc(ms_done, 1)
            dve.wait_ge(gain_in[k % 2], 16 * (k // 2 + 1))
            dve.wait_ge(rstd_done, seg0 + len(segs))
            for t in range(NT):
                for s, (lo, hi) in enumerate(segs):
                    ins = nc.vector.scalar_tensor_tensor(
                        out=at(xn + t * row + lo, hi - lo), in0=src(t, lo, hi), scalar=ss[:, s * NT + t:s * NT + t + 1],
                        in1=seg_gain(k, s), op0=ALU.mult, op1=ALU.mult)
                    ins.then_inc(xn_done, 1)
            if NORMS[k][2]:
                for b in range(2 * NT):
                    dve.wait_ge(u_hi_done, bank0 + b + 1)
                    d, n = turned_place(k, b)
                    nc.vector.tensor_tensor(d(u_lo), turned_bank(b, n), d(u_hi).bitcast(F32), ALU.subtract)

        def turned_place(k, b):
            t, h = b // 2, b % 2
            n = min(4, NORMS[k][2] - 4 * h)

            def d(u):
                return u[:].rearrange("p (c t) -> p c t", c=KC)[:, 4 * h:4 * h + n, t * P:(t + 1) * P]
            return d, n

        def turned_bank(b, n):
            return psum[:, b, 0:n * P].rearrange("p (c t) -> p c t", c=n)

        def norm_pool(pool, k):
            seg0 = norm_base(k)[0]
            for s in range(len(NORMS[k][1])):
                pool.wait_ge(ms_done, seg0 + s + 1)
                nc.gpsimd.tensor_tensor(ss[:, s * NT:(s + 1) * NT], ms[:, s * NT:(s + 1) * NT],
                                        half_exp[:, 0:1].to_broadcast([P, NT]), ALU.pow).then_inc(rstd_done, 1)

        def norm_tensor(pe, k, xn, row):
            segs = NORMS[k][1]
            xn0 = NT * norm_base(k)[0]
            for b in range(2 * NT):
                t, h = b // 2, b % 2
                n = min(4, NORMS[k][2] - 4 * h)
                pe.wait_ge(xn_done, xn0 + len(segs) * (t + 1))
                for c in range(n):
                    tr = nc.tensor.transpose(psum[:, b, c * P:(c + 1) * P], at(xn + t * row + (4 * h + c) * P, P), ident[:])
                tr.then_inc(turned, 1)

        def norm_scalar(act, k):
            bank0 = norm_base(k)[2]
            if k + 1 < len(NORMS):
                if k >= 1:
                    act.wait_ge(xn_done, NT * norm_base(k)[0])
                load_gain(act, k + 1)
            if NORMS[k][2]:
                for b in range(2 * NT):
                    act.wait_ge(turned, bank0 + b + 1)
                    d, n = turned_place(k, b)
                    nc.scalar.activation(d(u_hi), turned_bank(b, n), ACT.Copy).then_inc(u_hi_done, 1)

        def x_tile(t, lo, hi):
            return x[:, t * D + lo:t * D + hi]


        out_hi = sem("out_hi")

        def split_output_scalar(act, src, nth):
            for c in range(0, KC, 2):
                if nth == 1:
                    act.wait_ge(sub_out, c + 2)
                nc.scalar.activation(u_hi[:, c * T:(c + 2) * T], at(src + c * T, 2 * T), ACT.Copy).then_inc(out_hi, 1)

        def split_output_vector(dve, src, nth):
            for c in range(0, KC, 2):
                dve.wait_ge(out_hi, 4 * nth + c // 2 + 1)
                nc.vector.tensor_tensor(u_lo[:, c * T:(c + 2) * T], at(src + c * T, 2 * T),
                                        u_hi[:, c * T:(c + 2) * T].bitcast(F32), ALU.subtract)

        class Stage(Attention):

            def __init__(self, *args, **kw):
                super().__init__(*args, **kw)
                n = self.name
                self.s_ready, self.s_free = sem(f"{n}_scores"), sem(f"{n}_scores_taken")
                self.exp_done = sem(f"{n}_exp")
                self.p_ready = sem(f"{n}_probs")
                self.pt_ready, self.pt_high = sem(f"{n}_turned"), sem(f"{n}_turned_high")
                self.pt_free = sem(f"{n}_turned_taken")
                self.pv_done, self.o_free, self.summed = sem(f"{n}_pv"), sem(f"{n}_out_taken"), sem(f"{n}_summed")
                self.qk_high, self.q_staged = sem(f"{n}_qk_high"), sem(f"{n}_q_staged")
                self.low_out = sem(f"{n}_low_out")
                self.v_high, self.v_staged = sem(f"{n}_v_high"), sem(f"{n}_v_staged")
                self.fixed_high, self.fixed_k, self.fixed_v = sem(f"{n}_fixed_high"), sem(f"{n}_fixed_k"), sem(f"{n}_fixed_v")
                self.bias_in = [sem(f"{n}_bias0"), sem(f"{n}_bias1")]
                self.diag = gain[1 if self.mla else 0]
                self.diag_done = sem(f"{n}_diag") if self.diff else None
                self.masked = sem(f"{n}_masked") if self.name == "na" else None
                self.vec = sem(f"{n}_vec")
                self.nsa = self.name == "nsa"
                self.pt_banks = 3 if self.nsa else 4
                assert self.uses % self.pt_banks == 0
                place = N_P if self.nsa else TAIL
                if self.mla:
                    self.KR = self.LOWV = TAIL + 8 * T
                    place = self.KR + T
                self.P0 = place
                place += self.bufs * self.p_size()
                if self.nsa:
                    self.BIAS, self.LOWV, self.PCS, self.PTC = V + 2048, V + 3072, V + 3584, place
                    place += T
                else:
                    self.BIAS = place
                    place += 0 if self.mla else 2 * (T if self.causal else STRIP)
                    self.MASK = place
                    place += GRID_W if self.name == "na" else 0
                    if self.name == "na":
                        self.LOWV = place
                        place += T
                assert place <= ARENA, (n, place)
                first = 3 if self.causal else 4
                slots = [(u, c * T) for u in (u_hi, u_lo) for c in range(first, KC)] + [(spare_r, 0), (spare_r, T)]

                def take(count):
                    return [slots.pop(0) for _ in range(count)]
                if self.diff or self.mla:
                    self.QH, self.QL, self.KH, self.KL = take(2), take(2), take(2), take(2)
                    self.VH = take(2)
                    self.VL = take(2) if self.diff else None
                else:
                    self.QS = take(2)
                    self.KH = take(4 if self.nsa else 2)
                    self.KL = take(2 if self.nsa else 1)
                    self.VH = take(4 if self.nsa else 2)

            def rows(self, head):
                return 64 * head, 64 * head + 64

            def rope_rows(self, head):
                return ((64, 96), (0, 32))[head]

            def score_products(self, m, qt, n):
                head = m // self.per_head
                q = slice(qt * P, qt * P + P)
                if self.diff or self.mla:
                    lo, hi = self.rows(m % 2) if self.diff else ((0, 96), (0, P))[head]
                    pairs = ((self.QL, self.KH), (self.QH, self.KL), (self.QH, self.KH))
                    return [(slot(a[head], q, lo, hi), slot(b[head], slice(0, n), lo, hi)) for a, b in pairs]
                lo, hi = self.rows(head)
                if self.nsa:
                    kh, kl = self.KH[2 * (m % 2) + head], self.KL[m % 2]
                else:
                    kh, kl = self.KH[head], self.KL[0]
                return [(slot(self.QS[head], q, lo, hi), slot(kl, slice(0, n), lo, hi)),
                        (slot(self.QS[head], q), slot(kh, slice(0, n)))]

            def value_products(self, t, kt, turned_cols):
                kind, head, m = self.turns[t]
                high, low = u_hi[:, turned_cols], u_lo[:, turned_cols]
                k = slice(kt * P, kt * P + P)
                if self.diff:
                    vh, vl = slot(self.VH[head], k), slot(self.VL[head], k)
                    return [(vl, high), (vh, low), (vh, high)]
                v = slot(self.VH[2 * (m % 2) + head if self.nsa else head], k)
                return [(v, low), (v, high)]

            def bias_of(self, m, qt):
                n = self.length(qt)
                if self.mla:
                    return zero[:, 0:1].to_broadcast([P, n])
                if self.name == "na":
                    return at(self.BIAS + m * STRIP + (6 - 2 * qt) * GRID_W, n)
                b = m % 2 if self.diff else m // 2
                return at(self.BIAS + b * T + T - n, n)

            def p_tile(self, m, qt):
                return at(self.P0 + (m % self.bufs) * self.p_size() + self.p_at(qt), self.length(qt))

            def turned_cols(self, kt):
                return slice(self.pt_at(kt), self.pt_at(kt) + T - self.first_q(kt) * P)

            def diag_tile(self, m, qt):
                b = (m // 2 if self.diff else m) % 2
                return self.diag[:, (b * NT + qt) * P:(b * NT + qt + 1) * P]

            def stat(self, buf, m, qt=None):
                b = m % self.bufs
                return buf[:, b * NT:(b + 1) * NT] if qt is None else buf[:, b * NT + qt:b * NT + qt + 1]

            def each_pass(self, eng, base, body):
                n = self.passes
                body(base, 2, True)
                with repeat(eng, 1, n - 2) as i:
                    body(i + base, 2)
                body(base + n - 2, 1)
                body(base + n - 1, 0)

            def turned_bank(self, n):
                return 2 + n % self.pt_banks

        def slot(place, cols=slice(0, T), lo=0, hi=P):
            buf, c = place
            return buf[lo:hi, c + cols.start:c + cols.stop]

        def by_tile(place, lo, width):
            return slot(place).rearrange("p (t c) -> p t c", t=NT)[:, :, lo:lo + width]

        def values_of(row, col, width):
            v = arena[:, V:V + NT * row].rearrange("p (t c) -> p t c", t=NT)
            return v[:, :, bass.ds(col, width)] if not isinstance(col, int) else v[:, :, col:col + width]

        def place_of(att, I, left, m):
            if m < att.maps:
                return I, m
            return (I + 1, m - att.maps) if left else None

        def tile_at(att, I, left, n):
            if n < att.uses:
                return I, n
            return (I + 1, n - att.uses) if left else None

        def next_v(att, I, left, a):
            if a == 0:
                return I, 1
            return (I + 1, 0) if left else None

        def next_qk(att, I, left, a):
            if att.nsa:
                return (I + 1, a) if left else None
            if a == 0:
                return (I + 1, 1) if left else None
            return (I + 2, 0) if left == 2 else None

        def head_before(I, first, a):
            if a == 1:
                return I, 0
            return None if first else (I - 1, 1)

        def qk_parts(att, I, a):
            lo, hi = att.rows(a)
            other = (64 - lo, 128 - lo)
            if att.diff:
                return [(slot(att.QH[a]), slot(att.QL[a]), at(QT + (2 * I + a) * T)),
                        (slot(att.KH[a]), slot(att.KL[a]), at(KT + (2 * I + a) * T))]
            every = slice(0, T)
            if att.mla:
                rope = att.rope_rows(a)
                return [(slot(att.QH[a], every, lo, hi), slot(att.QL[a], every, lo, hi), at(QT + I * T, T, lo, hi)),
                        (slot(att.KH[a], every, lo, hi), slot(att.KL[a], every, lo, hi), at(KT + I * T, T, lo, hi)),
                        (slot(att.QH[a], every, *rope), slot(att.QL[a], every, *rope), at(TAIL + I * T, T, *rope))]
            out = [(slot(att.QS[a], every, lo, hi), slot(att.QS[a], every, *other), at(QT + I * T, T, lo, hi))]
            if att.name == "na":
                k = at(KT + I * T, T, lo, hi)
                out.append((slot(att.KH[a], every, lo, hi), slot(att.KL[0], every, lo, hi), k))
                out.append((slot(att.KH[a], every, *other), None, k))
            return out

        def v_parts(att, I, a):
            if att.diff:
                return (slot(att.VH[a]).rearrange("p (t c) -> p t c", t=NT),
                        slot(att.VL[a]).rearrange("p (t c) -> p t c", t=NT), values_of(D, (2 * I + a) * P, P))
            return by_tile(att.VH[a], 0, 64), by_tile(att.VH[a], 64, 64), values_of(D, (2 * I + a) * 64, 64)

        def fixed_k_parts(att, g):
            every, out = slice(0, T), []
            for a in range(2):
                lo, hi = att.rows(a)
                if att.nsa:
                    for branch in range(2):
                        k = at(KT + ((6, 4)[branch] + g) * T, T, lo, hi)
                        kh = att.KH[2 * branch + a]
                        out.append((slot(kh, every, lo, hi), slot(att.KL[branch], every, lo, hi), k))
                        out.append((slot(kh, every, 64 - lo, 128 - lo), None, k))
                else:
                    rope = att.rope_rows(a)
                    out.append((slot(att.KH[a], every, *rope), slot(att.KL[a], every, *rope), at(att.KR, T, *rope)))
            if att.mla:
                nothing = zero[32:64, 0:1].to_broadcast([32, T])
                out += [(slot(x_[1], every, 32, 64), None, nothing) for x_ in (att.KH, att.KL, att.QH, att.QL)]
            return out

        def fixed_v_parts(att, g):
            return [(by_tile(att.VH[2 * branch + a], 0, 64), by_tile(att.VH[2 * branch + a], 64, 64),
                     values_of(T, (256, 0)[branch] + (2 * g + a) * 64, 64)) for branch in range(2) for a in range(2)]

        def attend_tensor(pe, att, g=0, first=True):
            base = g * att.passes
            if first:
                pe.sem_inc(att.pt_ready, att.credit)
                pe.sem_inc(att.pv_done, att.credit)

            def score(I, m, qt):
                if qt == 0:
                    pe.wait_ge(att.q_staged, 2 * I + m // att.per_head + 1)
                n = att.length(qt)
                pe.wait_ge(att.s_free, 4 * (att.maps * I + m) + qt + 1)
                pairs = att.score_products(m, qt, n)
                for nth, (lhs, rhs) in enumerate(pairs):
                    mm = nc.tensor.matmul(bank(qt % 2, n), lhs, rhs, start=(nth == 0), stop=(nth == len(pairs) - 1))
                mm.then_inc(att.s_ready, 1)

            def turn_tile(I, n):
                t, kt = att.tiles[n]
                kind, head, m = att.turns[t]
                if kind == "cmp":
                    pe.wait_ge(att.v_staged, 2 * I + head + 1)
                pe.wait_ge(att.pt_free, att.uses * I + n + 1)
                b = att.turned_bank(n)
                if kind == "cmp":
                    for qt in range(NT):
                        tr = nc.tensor.transpose(psum[0:CMP, b, qt * P:(qt + 1) * P],
                                                 at(att.PCS + head * NT * CMP + qt * CMP, CMP), ident[:])
                else:
                    q0 = att.first_q(kt)
                    for qt in range(q0, NT):
                        if kt == 0:
                            pe.wait_ge(att.p_ready, 4 * (2 * I + head if att.diff else att.maps * I + m) + qt + 1)
                        tr = nc.tensor.matmul(psum[:, b, (qt - q0) * P:(qt - q0 + 1) * P],
                                              att.p_tile(m, qt)[:, kt * P:(kt + 1) * P], att.diag_tile(m, qt),
                                              start=True, stop=True)
                tr.then_inc(att.pt_ready, 1)

            def value_tile(I, n):
                t, kt = att.tiles[n]
                kind, head, m = att.turns[t]
                starts = n == 0 or att.turns[att.tiles[n - 1][0]][1] != head
                ends = n + 1 == att.uses or att.turns[att.tiles[n + 1][0]][1] != head
                if starts:
                    pe.wait_ge(att.o_free, 2 * I + head + 1)
                    pe.wait_ge(att.v_staged, 2 * I + head + 1)
                pe.wait_ge(att.pt_free, att.uses * I + n + 1 + att.pt_banks)
                if kind == "cmp":
                    pairs = [(at(N_VC + (2 * g + head) * P, P, 0, CMP), at(att.PTC, T, 0, CMP))]
                    q0 = 0
                else:
                    q0 = att.first_q(kt)
                    pairs = att.value_products(t, kt, att.turned_cols(kt))
                for nth, (lhs, rhs) in enumerate(pairs):
                    mm = nc.tensor.matmul(psum[:, 6 + head, q0 * P:T], lhs, rhs, start=(starts and nth == 0),
                                          stop=(ends and nth == len(pairs) - 1))
                mm.then_inc(att.pv_done, 1)

            if att.nsa or att.mla:
                pe.wait_ge(att.fixed_k, g + 1)
            if att.nsa:
                pe.wait_ge(att.fixed_v, g + 1)
            for m in range(att.ahead):
                for qt in range(NT):
                    score(base, m, qt)
            for n in range(LOOK):
                turn_tile(base, n)

            def body(I, left, first=False):
                for n in range(att.uses):
                    for m, qt in att.scores_beside(n):
                        where = place_of(att, I, left, m)
                        if where:
                            score(*where, qt)
                    where = tile_at(att, I, left, n + LOOK)
                    if where:
                        turn_tile(*where)
                    value_tile(I, n)
            att.each_pass(pe, base, body)

        def attend_vector(dve, att, g=0, first=True):
            base = g * att.passes
            if first:
                dve.sem_inc(att.s_free, 2)
                dve.sem_inc(att.o_free, 2)
                dve.sem_inc(att.pt_free, att.pt_banks)

            def score(I, m, qt):
                M = att.maps * I + m
                if qt == 0:
                    if att.nsa:
                        dve.wait_ge(att.bias_in[m // 2], 16 * (I + 1))
                    elif att.diff:
                        dve.wait_ge(att.bias_in[m % 2], 16 * (2 * I + m // 2 + 1))
                    elif att.name == "na":
                        dve.wait_ge(att.masked, M + 1)
                    dve.wait_ge(att.pt_ready, att.uses * I + (att.released(m) + 1 + att.credit))
                dve.wait_ge(att.s_ready, 4 * M + qt + 1)
                hold(dve)
                nc.vector.tensor_tensor_reduce(
                    out=att.p_tile(m, qt), in0=bank(qt % 2, att.length(qt)), in1=att.bias_of(m, qt), scale=-1.0,
                    scalar=BIG, op0=ALU.add, op1=ALU.min, accum_out=att.stat(neg_max, m, qt))\
                    .then_inc(att.s_free, 1)

            def low_parts(triples):
                for high, low, src in triples:
                    if low is not None:
                        ins = nc.vector.tensor_tensor(low, src, high.bitcast(F32), ALU.subtract)
                return ins

            def stage_qk(I, a):
                dve.wait_ge(att.qk_high, 2 * I + a + 1)
                low_parts(qk_parts(att, I, a)).then_inc(att.q_staged, 1)

            def stage_compressed(I, a):
                n = NT * CMP
                row = (2 * g + a) * 4 - base + I
                before = next(att.use[t] for t, (kind, h, _) in enumerate(att.turns) if kind == "cmp" and h == a)
                dve.wait_ge(att.pt_ready, att.uses * I + (before - att.uses + 1 + att.credit))
                nc.vector.tensor_scalar(at(att.PCS + a * n, n), at(N_PC + n * row, n), 1.0, None, ALU.mult)\
                    .then_inc(att.v_staged, 1)

            def counted(ins):
                ins.then_inc(att.vec, 1)

            def own_count(M, step, steps):
                dve.wait_ge(att.vec, steps * M + step)

            def make_ready(I, m):
                M = att.maps * I + m
                r = att.stat(inv, m)
                dve.wait_ge(att.exp_done, 4 * M + (8 if att.diff else 4))
                counted(nc.vector.reciprocal(r, att.stat(row_sum, m)))
                if att.diff:
                    head = 2 * I + m // 2
                    c = att.stat(inv, m + 1)
                    counted(nc.vector.reciprocal(c, att.stat(row_sum, m + 1)))
                    own_count(head, 2, 3)
                    counted(nc.vector.scalar_tensor_tensor(out=c, in0=c, scalar=neg_lam[:, 0:1],
                                                           in1=att.stat(row_sum, m), op0=ALU.mult, op1=ALU.mult))
                    own_count(head, 3, 3)
                elif att.nsa:
                    own_count(M, 1, 2)
                    head, branch = m // 2, 2 - m % 2
                    col = ((2 * g + head) * 4 - base) * 3 + branch + 3 * I
                    gates = gate[:].rearrange("p (t c) -> p t c", t=NT)
                    gates = gates[:, :, bass.ds(col, 1)] if not isinstance(col, int) else gates[:, :, col:col + 1]
                    r3 = r.rearrange("p (t o) -> p t o", o=1)
                    counted(nc.vector.tensor_tensor(r3, r3, gates, ALU.mult))
                    own_count(M, 2, 2)
                else:
                    own_count(M, 1, 1)
                dve.wait_ge(att.pt_ready, att.uses * I + (att.turned_by(m - att.maps_per_turn * 2) + 1 + att.credit))
                hold(dve)
                for qt in range(NT):
                    nc.vector.tensor_scalar(att.diag_tile(m, qt), ident[:], att.stat(inv, m, qt), None, ALU.mult)\
                        .then_inc(att.diag_done if att.diff else att.p_ready, 1)
                if att.diff:
                    for qt in range(NT):
                        nc.vector.scalar_tensor_tensor(
                            out=att.p_tile(m, qt), in0=att.p_tile(m + 1, qt), scalar=att.stat(inv, m + 1, qt),
                            in1=att.p_tile(m, qt), op0=ALU.mult, op1=ALU.add).then_inc(att.p_ready, 1)

            def take_turned(I, n):
                t, kt = att.tiles[n]
                kind = att.turns[t][0]
                b = att.turned_bank(n)
                if kind == "cmp":
                    dve.wait_ge(att.pt_ready, att.uses * I + att.use[t] + 1 + att.credit)
                    dve.wait_ge(att.pv_done, att.uses * I + (att.use[t] - att.uses // 2 + 1 + att.credit))
                    ins = nc.vector.tensor_scalar(at(att.PTC, T, 0, CMP), psum[0:CMP, b, :], 1.0, None, ALU.mult)
                else:
                    dve.wait_ge(att.pt_high, att.high_index(len(att.turns)) * I + att.high_index(t) + kt + 1)
                    cols = att.turned_cols(kt)
                    ins = nc.vector.tensor_tensor(u_lo[:, cols], bank(b, cols.stop - cols.start),
                                                  u_hi[:, cols].bitcast(F32), ALU.subtract)
                ins.then_inc(att.pt_free, 1)

            def take_head(I, head):
                dve.wait_ge(att.pv_done, att.uses * I + (att.last_use(head) + 1 + att.credit))
                o = psum[:, 6 + head, :]
                if att.diff:
                    ins = nc.vector.tensor_scalar(at(QT + (2 * I + head) * T), o, 1.0, None, ALU.mult)
                else:
                    z, part = at(Z + I * T, T, *att.rows(head)), at(att.LOWV, T, *att.rows(head))
                    dve.wait_ge(att.low_out, 2 * I + head + 1)
                    nc.vector.tensor_tensor(part, o[0:64], part, ALU.add).then_inc(att.summed, 1)
                    dve.wait_ge(att.summed, 2 * I + head + 1)
                    ins = nc.vector.tensor_tensor(z, part, z, ALU.mult)
                ins.then_inc(att.o_free, 1)

            def body(I, left, first=False):
                for n, (t, kt) in enumerate(att.tiles):
                    kind, a, m = att.turns[t]
                    for mm, qt in att.scores_beside(n):
                        where = place_of(att, I, left, mm)
                        if where:
                            score(*where, qt)
                    where = tile_at(att, I, left, n + LOOK)
                    if where:
                        take_turned(*where)
                    if kind == "cmp":
                        continue
                    if kt == 0:
                        where = place_of(att, I, left, m + att.maps_per_turn)
                        if where:
                            make_ready(*where)
                    if kt == 3 and att.first_turn(t) and next_qk(att, I, left, a):
                        stage_qk(*next_qk(att, I, left, a))
                    if kt == 2 and att.first_turn(t) and head_before(I, first, a):
                        take_head(*head_before(I, first, a))
                    if kt == 2 and att.first_turn(t) and att.nsa and next_v(att, I, left, a):
                        stage_compressed(*next_v(att, I, left, a))

            if att.nsa or att.mla:
                dve.wait_ge(att.fixed_high, g + 1)
                low_parts(fixed_k_parts(att, g)).then_inc(att.fixed_k, 1)
            stage_qk(base, 0)
            stage_qk(base, 1)
            if att.nsa:
                stage_compressed(base, 0)
            for m in range(att.ahead):
                for qt in range(NT):
                    score(base, m, qt)
            if not att.nsa:
                stage_qk(base + 1, 0)
            make_ready(base, 0)
            for n in range(LOOK):
                take_turned(base, n)
            att.each_pass(dve, base, body)
            take_head(base + att.passes - 1, 1)

        def attend_scalar(act, att, g=0):
            base = g * att.passes

            def load_bias(I, m):
                if att.name == "na":
                    for r2 in range(2):
                        first_at = RPB_PAD + 15 + (1 - r2) * RPB_ROW + m * RPB_HEAD + 2 * RPB_HEAD * I
                        act.dma_start(
                            arena[r2 * 64:r2 * 64 + 64, att.BIAS + m * STRIP:att.BIAS + (m + 1) * STRIP]
                            .rearrange("p (j c) -> p j c", c=GRID_W),
                            bass.AP(rpb_rows.tensor, first_at, [[RPB_LEN - 1, 64], [RPB_ROW, 14], [1, GRID_W]]))\
                            .then_inc(att.bias_in[m], 16)
                    return
                if att.diff:
                    b, row = m % 2, 4 * I + m
                else:
                    b, row = m // 2, (2 * g + m // 2) * 4 - base + I
                act.dma_start(at(att.BIAS + b * T), bass.AP(bias_rows.tensor, P - 1 + SPAN * row,
                                                            [[HEADS * SPAN - 1, P], [1, T]]))\
                    .then_inc(att.bias_in[b], 16)

            def score(I, m, qt):
                act.wait_ge(att.s_free, 4 * (att.maps * I + m) + qt + 3)
                nc.scalar.activation(att.p_tile(m, qt), att.p_tile(m, qt), ACT.Exp, scale=-1.0,
                                     bias=att.stat(neg_max, m, qt), accum_out=att.stat(row_sum, m, qt))\
                    .then_inc(att.exp_done, 1)

            def high_parts(triples):
                for high, _, src in triples:
                    ins = nc.scalar.activation(high, src, ACT.Copy)
                return ins

            def stage_v(I, a):
                act.wait_ge(att.pv_done, att.uses * I + (att.last_use(a) - att.uses + 1 + att.credit))
                high_parts([v_parts(att, I, a)]).then_inc(att.v_high, 1)

            def take_turned(I, n):
                t, kt = att.tiles[n]
                if att.turns[t][0] == "cmp":
                    return
                act.wait_ge(att.pt_ready, att.uses * I + (n + 1 + att.credit))
                full = [u for (k, _, _), u in zip(att.turns, att.use) if k == "full"]
                nth = full.index(att.use[t])
                before = full[nth - 1] - (att.uses if nth == 0 else 0)
                act.wait_ge(att.pv_done, att.uses * I + (before + kt + 1 + att.credit))
                cols = att.turned_cols(kt)
                nc.scalar.activation(u_hi[:, cols], bank(att.turned_bank(n), cols.stop - cols.start), ACT.Copy)\
                    .then_inc(att.pt_high, 1)

            def copy_low_out(I, head):
                act.wait_ge(att.pv_done, att.uses * I + (att.last_use(head) + 1 + att.credit))
                act.wait_ge(att.o_free, 2 * I + head + 1)
                nc.scalar.activation(at(att.LOWV, T, *att.rows(head)), psum[64:P, 6 + head, :], ACT.Copy)\
                    .then_inc(att.low_out, 1)

            def next_bias(I, left, a):
                if att.name == "na":
                    if left == 2:
                        load_bias(I + 2, a)
                elif not att.mla:
                    maps = (0, 1) if att.diff else (0,)
                    if a == 0 and (att.nsa or left):
                        if left:
                            for b in maps:
                                load_bias(I + 1, 2 + b)
                    elif a == 1 and left == 2:
                        for b in maps:
                            load_bias(I + 2, b)

            def body(I, left, first=False):
                for n, (t, kt) in enumerate(att.tiles):
                    kind, a, m = att.turns[t]
                    where = tile_at(att, I, left, n + LOOK)
                    if where:
                        take_turned(*where)
                    for mm, qt in att.scores_beside(n):
                        where = place_of(att, I, left, mm)
                        if where:
                            score(*where, qt)
                    if kind == "cmp":
                        continue
                    if kt == 0 and att.first_turn(t) and next_qk(att, I, left, a):
                        high_parts(qk_parts(att, *next_qk(att, I, left, a))).then_inc(att.qk_high, 1)
                    if kt == 1 and att.first_turn(t) and head_before(I, first, a) and not att.diff:
                        copy_low_out(*head_before(I, first, a))
                    if kt == 1 and not att.nsa and next_v(att, I, left, a):
                        stage_v(*next_v(att, I, left, a))
                    if n + 1 == att.head_end(a):
                        next_bias(I, left, a)

            if att.nsa:
                load_bias(base, 0)
                load_bias(base, 2)
            elif not att.mla:
                load_bias(base, 0)
                load_bias(base, 1)
            if att.nsa or att.mla:
                if g:
                    act.wait_ge(att.pv_done, att.uses * base + att.credit)
                high_parts(fixed_k_parts(att, g) + (fixed_v_parts(att, g) if att.nsa else [])).then_inc(att.fixed_high, 1)
            for a in range(2):
                high_parts(qk_parts(att, base, a)).then_inc(att.qk_high, 1)
            if not att.nsa:
                stage_v(base, 0)
            for m in range(att.ahead):
                for qt in range(NT):
                    score(base, m, qt)
                if att.name == "na":
                    load_bias(base + 1, m)
                elif att.nsa and m == 1:
                    load_bias(base + 1, 0)
                elif att.diff:
                    load_bias(base + m // 2, (m + 2) % 4)
            if not att.nsa:
                high_parts(qk_parts(att, base + 1, 0)).then_inc(att.qk_high, 1)
            for n in range(LOOK):
                take_turned(base, n)
            att.each_pass(act, base, body)
            if not att.diff:
                copy_low_out(base + att.passes - 1, 1)

        def attend_pool(pool, att, g=0):
            def low_values(I, a):
                high, low, src = v_parts(att, I, a)
                pool.wait_ge(att.v_high, 2 * I + a + 1)
                hold(pool)
                nc.gpsimd.tensor_tensor(low, src, high.bitcast(F32), ALU.subtract).then_inc(att.v_staged, 1)

            def mask_strip(I, m):
                if att.name != "na":
                    return
                pool.wait_ge(att.bias_in[m], 32 * (I + 1))
                hold(pool)
                strip = at(att.BIAS + m * STRIP, STRIP).rearrange("p (j c) -> p j c", c=GRID_W)
                mask = at(att.MASK, GRID_W).unsqueeze(1).to_broadcast([P, STRIP // GRID_W, GRID_W])
                nc.gpsimd.tensor_tensor(strip, strip, mask, ALU.add).then_inc(att.masked, 1)

            if att.nsa:
                pool.wait_ge(att.fixed_high, g + 1)
                for high, low, src in fixed_v_parts(att, g):
                    ins = nc.gpsimd.tensor_tensor(low, src, high.bitcast(F32), ALU.subtract)
                ins.then_inc(att.fixed_v, 1)
                return
            mask_strip(0, 0)
            mask_strip(0, 1)
            low_values(0, 0)

            def body(I, left, first=False):
                for a in range(2):
                    if left:
                        mask_strip(I + 1, a)
                    if next_v(att, I, left, a):
                        low_values(*next_v(att, I, left, a))
            att.each_pass(pool, 0, body)

        nsa = Stage("nsa", passes=4, per_head=2, causal=True, ahead=2, bufs=4, cmp=True)
        diff = Stage("diff", passes=4, per_head=2, causal=True, ahead=4, bufs=4)
        na = Stage("na", passes=8, per_head=1, causal=False, ahead=2, bufs=2)
        mla = Stage("mla", passes=8, per_head=1, causal=False, ahead=2, bufs=2)

        pe_k, pe_v = at(N_CB - 64, 32), at(N_CB - 32, 32)
        w2_k, w2_v = at(N_CB - 256, P), at(N_CB - 128, 64)
        ONEHOT, TABLE, ROWMASK, ROWS, LAMBDAS = Z, Z + SPAN, Z + SPAN + HEADS, Z + 2 * SPAN + HEADS, Z + 3 * SPAN + HEADS
        lam_sum, lam_exp, rpb_out = sem("lam_sum"), sem("lam_exp"), sem("rpb_out")
        consts = [(ident[:], "ident"), (at(ONEHOT, SPAN, 0, BUCKETS), "onehot"), (at(TABLE, HEADS, 0, BUCKETS), "table"),
                  (at(ROWMASK, SPAN, 0, HEADS), "rowmask"), (subln[:], "subln"), (pe_k, "pe_k"), (pe_v, "pe_v"),
                  (w2_k, "w2_k"), (w2_v, "w2_v")]

        def setup_scalar(act):
            act.dma_start(x[:].rearrange("p (t d) -> p t d", t=NT), A["x"].rearrange("(t p) d -> p t d", p=P))\
                .then_inc(x_in, 16)
            load_gain(act, 0)
            for dst, name in consts:
                act.dma_start(dst, A[name]).then_inc(const_in, 16)
            act.dma_start(at(LAMBDAS, 256), bass.AP(A["lambdas"].tensor, 0, [[0, P], [1, 256]])).then_inc(const_in, 16)
            act.dma_start(rpb_rows, bass.AP(A["rpb"].tensor, 0, [[0, GRID_W], [1, RPB_LEN]])).then_inc(rpb_out, 16)
            for b in range(2):
                act.wait_ge(w_loaded[b], 16)
                nc.scalar.activation(w_hi[b][:], stage[b][:], ACT.Copy).then_inc(w_high, 1)
            act.wait_ge(lam_sum, 2)
            nc.scalar.activation(neg_lam[:, 2:4], neg_lam[:, 0:2], ACT.Exp).then_inc(lam_exp, 1)
            act.wait_ge(rows_made, 3)
            act.dma_start(bass.AP(bias_rows.tensor, 0, [[SPAN, HEADS], [HEADS * SPAN, P], [1, SPAN]]),
                          at(ROWS, SPAN, 0, HEADS).unsqueeze(1).to_broadcast([HEADS, P, SPAN])).then_inc(rows_out, 16)

        def setup_pool(pool):
            for b in range(2):
                split_low(pool, b, b)

        def setup_tensor(pe):
            pe.wait_ge(const_in, 16 * (len(consts) + 1))
            for b in range(2):
                mm = nc.tensor.matmul(psum[0:HEADS, b, :], at(TABLE, HEADS, 0, BUCKETS),
                                      at(ONEHOT + b * 512, 512, 0, BUCKETS), start=True, stop=True)
            mm.then_inc(rows_made, 1)

        def setup_vector(dve):
            dve.sem_inc(bank_free["dve"], 4)
            dve.sem_inc(bank_free["act"], 4)
            nc.vector.memset(zero[:], 0.0)
            nc.vector.memset(one[:], 1.0)
            done("dve", nc.vector.memset(half_exp[:], -0.5))
            dve.wait_ge(const_in, 16 * (len(consts) + 1))
            for k in range(2):
                nc.vector.tensor_tensor_reduce(
                    out=at(ROWS + k * 64, 64), in0=at(LAMBDAS + 128 * k, 64), in1=at(LAMBDAS + 128 * k + 64, 64),
                    scale=1.0, scalar=0.0, op0=ALU.mult, op1=ALU.add, accum_out=neg_lam[:, k:k + 1]).then_inc(lam_sum, 1)
            done("dve", nc.vector.tensor_scalar(subln[:], subln[:], 1.0 - LAMBDA_INIT, None, ALU.mult))
            dve.wait_ge(lam_exp, 1)
            done("dve", nc.vector.tensor_tensor(neg_lam[:, 0:1], neg_lam[:, 3:4], neg_lam[:, 2:3], ALU.subtract))
            settle("dve", dve)
            done("dve", nc.vector.tensor_scalar(neg_lam[:, 0:1], neg_lam[:, 0:1], -LAMBDA_INIT, None, ALU.add))
            dve.wait_ge(rows_made, 1)
            for b in range(2):
                nc.vector.tensor_tensor(at(ROWS + b * 512, 512, 0, HEADS), psum[0:HEADS, b, :],
                                        at(ROWMASK + b * 512, 512, 0, HEADS), ALU.add).then_inc(rows_made, 1)
            dve.wait_ge(x_in, 16)

        def load_strips(act, r):
            if r == 0:
                act.wait_ge(rows_out, 16)
            if r >= 2:
                act.wait_ge(strip_used, 4 * (r - 1))
            act.dma_start(at((Z, TAIL)[r % 2], 4 * STRIP).rearrange("p (h j) -> p h j", h=4),
                          bass.AP(bias_rows.tensor, P - 1 + 4 * SPAN * r,
                                  [[HEADS * SPAN - 1, P], [SPAN, 4], [1, STRIP]])).then_inc(strip_in[r % 2], 16)

        def cut_strips(dve, r):
            dve.wait_ge(strip_in[r % 2], 16 * (r // 2 + 1))
            strips = at((Z, TAIL)[r % 2], 4 * STRIP).rearrange("p (h j) -> p h j", h=4)
            for qt in range(NT):
                j = 415 - P * qt
                dst = at(N_CB + 4 * r * NT * CMP, 4 * NT * CMP).rearrange("p (h t c) -> p h t c", h=4, t=NT)
                nc.vector.tensor_copy(dst[:, :, qt, :], strips[:, :, j:j + 16 * (CMP - 1) + 1:16]).then_inc(strip_used, 1)

        X, HID = N_PC, N_PC + 32 * 4 * CMP
        MX, LSUM = HID + 8 * CMP, HID + 8 * CMP + 64
        assert LSUM + 64 <= N_CB - 256
        cmp_x, cmp_hi, cmp_lo = sem("cmp_x"), sem("cmp_hi"), sem("cmp_lo")
        cmp_kv, cmp_kv_taken, cmp_s = sem("cmp_kv"), sem("cmp_kv_taken"), sem("cmp_s")
        cmp_shifted, cmp_exp = sem("cmp_shifted"), sem("cmp_exp")
        XQ = 32 * 4 * CMP // 4

        def compress_vector(dve):
            n = 0
            for side, pos in ((0, pe_k), (1, pe_v)):
                for half in range(2):
                    for gp in range(2):
                        src = at(KT + (2 * side + gp) * T, T, 64 * half, 64 * half + 64)
                        src = bass.AP(src.tensor, src.offset, [src.ap[0], [1, 32], [16, CMP]])
                        dst = at(X, 32 * 4 * CMP, 64 * side, 64 * side + 64).rearrange("p (o q c) -> p o q c", o=32, q=4)
                        nc.vector.tensor_tensor(
                            dst[:, :, 2 * half + gp, :], src,
                            pos[64 * half:64 * half + 64, :].unsqueeze(2).to_broadcast([64, 32, CMP]),
                            ALU.add).then_inc(cmp_x, 1)
            for q in range(4):
                dve.wait_ge(cmp_hi, q + 1)
                nc.vector.tensor_tensor(u_lo[:, q * XQ:(q + 1) * XQ], at(X + q * XQ, XQ),
                                        u_hi[:, q * XQ:(q + 1) * XQ].bitcast(F32), ALU.subtract).then_inc(cmp_lo, 1)
            dve.wait_ge(cmp_kv, 1)
            for half in range(2):
                nc.vector.tensor_copy(at(N_CK, 2 * CMP, 64 * half, 64 * half + 64),
                                      psum[64 * half:64 * half + 64, 2, 2 * CMP * half:2 * CMP * (half + 1)])\
                    .then_inc(cmp_kv_taken, 1)
            vc = at(N_VC, 4 * P, 0, CMP).rearrange("p (g c) -> p g c", g=4)
            nc.vector.memset(vc[:, :, 64:P], 0.0)
            nc.vector.tensor_copy(vc[:, :, 0:64], psum[0:CMP, 3, 0:256].rearrange("p (g c) -> p g c", g=4))\
                .then_inc(cmp_kv_taken, 1)
            n = 4 * NT * CMP
            for g in range(4):
                dve.wait_ge(cmp_s, g + 1)
                done("dve", nc.vector.tensor_tensor(at(N_PC + g * n, n), bank(4 + g, n), at(N_CB + g * n, n), ALU.add))
            settle("dve", dve)
            pc = at(N_PC, HEADS * NT * CMP).rearrange("p (h c) -> p h c", c=CMP)

            def spread(off):
                return at(off, 64).unsqueeze(2).to_broadcast([P, 64, CMP])
            done("dve", nc.vector.tensor_reduce(at(MX, 64), pc, AX, ALU.max))
            settle("dve", dve)
            nc.vector.tensor_tensor(pc, pc, spread(MX), ALU.subtract).then_inc(cmp_shifted, 1)
            dve.wait_ge(cmp_exp, 1)
            done("dve", nc.vector.tensor_reduce(at(LSUM, 64), pc, AX, ALU.add))
            settle("dve", dve)
            done("dve", nc.vector.reciprocal(at(LSUM, 64), at(LSUM, 64)))
            settle("dve", dve)
            r = at(LSUM, 64).rearrange("p (h t) -> p h t", t=NT)
            g0 = gate[:].rearrange("p (t h b) -> p h t b", t=NT, b=3)[:, :, :, 0]
            done("dve", nc.vector.tensor_tensor(r, r, g0, ALU.mult))
            settle("dve", dve)
            done("dve", nc.vector.memset(r[0:CMP, :, 0:1], 0.0))
            settle("dve", dve)
            done("dve", nc.vector.tensor_tensor(pc, pc, spread(LSUM), ALU.mult))

        def compress_scalar(act):
            act.wait_ge(cmp_x, 8)
            for q in range(4):
                nc.scalar.activation(u_hi[:, q * XQ:(q + 1) * XQ], at(X + q * XQ, XQ), ACT.Copy).then_inc(cmp_hi, 1)

            def hidden(i, j):
                nc.scalar.activation(at(HID, 4 * CMP), bank(0, 4 * CMP), ACT.Silu)
                return nc.scalar.activation(at(HID + 4 * CMP, 4 * CMP), bank(1, 4 * CMP), ACT.Silu)
            project_scalar(act, "nsa_cmp", hidden, banks=1)
            act.wait_ge(cmp_shifted, 1)
            pc = at(N_PC, HEADS * NT * CMP)
            nc.scalar.activation(pc, pc, ACT.Exp).then_inc(cmp_exp, 1)

        def compress_tensor(pe):
            run = RUNS["nsa_cmp"]
            n = 4 * CMP
            pe.wait_ge(cmp_lo, 4)
            wait_bank(pe, run, 0, 3)
            for a in range(2):
                b = (run["unit"] + a) % 2
                pe.wait_ge(w_ready, run["unit"] + a + 1)
                for o in range(16):
                    for side in range(2):
                        rows = slice(64 * side, 64 * side + 64)
                        for wl, ul in ((0, 1), (1, 0), (0, 0)):
                            c = (16 * a + o) * n
                            mm = nc.tensor.matmul(
                                bank(side, n), (w_lo if wl else w_hi)[b][rows, o * P:(o + 1) * P],
                                (u_lo if ul else u_hi)[rows, c:c + n],
                                start=(a == 0 and o == 0 and (wl, ul) == (0, 1)),
                                stop=(a == 1 and o == 15 and (wl, ul) == (0, 0)))
                mm.then_inc(*((w_used, 1) if a == 0 else (bank_done, 4)))
            pe.wait_ge(bank_free["act"], run["taken"] + 8)
            nc.tensor.matmul(bank(2, n), w2_k, at(HID, n), start=True, stop=True)
            for half in range(2):
                for gp in range(2):
                    q = 2 * half + gp
                    mm = nc.tensor.matmul(psum[0:CMP, 3, (2 * gp + half) * 64:(2 * gp + half + 1) * 64],
                                          at(HID + n + q * CMP, CMP), w2_v, start=True, stop=True)
            mm.then_inc(cmp_kv, 1)
            pe.wait_ge(cmp_kv_taken, 3)
            for g in range(4):
                gp, half = g // 2, g % 2
                rows = (64 * half, 64 * half + 64)
                for j in range(4):
                    for qt in range(NT):
                        c = (j * NT + qt) * CMP
                        mm = nc.tensor.matmul(psum[:, 4 + g, c:c + CMP], at(QT + (4 * gp + j) * T + qt * P, P, *rows),
                                              at(N_CK + gp * CMP, CMP, *rows), start=True, stop=True)
                mm.then_inc(cmp_s, 1)

        SQ, ONES, RSTD, ROWS_R = TAIL, TAIL + DIFF_HEADS * T, TAIL + DIFF_HEADS * T + 1, TAIL + DIFF_HEADS * T + 64
        NR = DIFF_HEADS * NT
        sub_sq, sub_sum, sub_in, sub_pow, sub_ones = (sem(f"sub_{n}") for n in ("sq", "sum", "in", "pow", "ones"))
        sub_turned, sub_rows, sub_spread, sub_scaled, sub_out = \
            (sem(f"sub_{n}") for n in ("turned", "rows", "spread", "scaled", "out"))

        def subln_scalar(act):
            for u in range(DIFF_HEADS):
                nc.scalar.activation(at(SQ + u * T), at(QT + u * T), ACT.Square).then_inc(sub_sq, 1)

        def subln_tensor(pe):
            pe.wait_ge(sub_ones, 1)
            for u in range(DIFF_HEADS):
                pe.wait_ge(sub_sq, u + 1)
                for t in range(NT):
                    r = u * NT + t
                    mm = nc.tensor.matmul(psum[:, 0, r:r + 1], at(SQ + u * T + t * P, P), at(ONES, 1), start=True, stop=True)
            mm.then_inc(sub_sum, 1)
            pe.wait_ge(sub_pow, 1)
            nc.tensor.transpose(psum[0:NR, 1, 0:P], at(RSTD, NR), ident[:]).then_inc(sub_turned, 1)
            pe.wait_ge(sub_rows, 1)
            for u in range(DIFF_HEADS):
                for t in range(NT):
                    r = u * NT + t
                    mm = nc.tensor.matmul(bank(u)[:, t * P:(t + 1) * P], ident[0:NR, r:r + 1].to_broadcast([NR, P]),
                                          at(ROWS_R, P, 0, NR), start=True, stop=True)
                mm.then_inc(sub_spread, 1)

        def subln_vector(dve):
            nc.vector.memset(at(ONES, 1), 1.0 / P).then_inc(sub_ones, 1)
            dve.wait_ge(sub_sum, 1)
            nc.vector.tensor_scalar(at(RSTD, NR), psum[:, 0, 0:NR], EPS, None, ALU.add).then_inc(sub_in, 1)
            dve.wait_ge(sub_turned, 1)
            nc.vector.tensor_copy(at(ROWS_R, P, 0, NR), psum[0:NR, 1, 0:P]).then_inc(sub_rows, 1)
            for u in range(DIFF_HEADS):
                dve.wait_ge(sub_spread, u + 1)
                nc.vector.scalar_tensor_tensor(out=at(QT + u * T), in0=bank(u), scalar=subln[:, u:u + 1],
                                               in1=at(QT + u * T), op0=ALU.mult, op1=ALU.mult).then_inc(sub_scaled, 1)
                dve.wait_ge(sub_scaled, u + 1)
                nc.vector.tensor_tensor(at(Z + u * T), at(Z + u * T), at(QT + u * T), ALU.mult).then_inc(sub_out, 1)

        def subln_pool(pool):
            pool.wait_ge(sub_in, 1)
            nc.gpsimd.tensor_tensor(at(RSTD, NR), at(RSTD, NR), half_exp[:, 0:1].to_broadcast([P, NR]), ALU.pow)\
                .then_inc(sub_pow, 1)

        PP, PIN, E = 4096, 0, Z
        p_in, p_turned, p_hi = sem("p_in"), sem("p_turned"), sem("p_hi")
        e_used, e_mul = sem("e_used"), sem("e_mul")

        def p_place(u, t):
            return u[:].rearrange("p (c t) -> p c t", c=KC)[:, 0:2, t * P:(t + 1) * P]

        def p_bank(t):
            return psum[:, t, 0:2 * P].rearrange("p (c t) -> p c t", c=2)

        def ple_tensor(pe, nth):
            pe.wait_ge(p_in, 16 * (nth + 1))
            for t in range(NT):
                for c in range(2):
                    tr = nc.tensor.transpose(psum[:, t, c * P:(c + 1) * P], at(PIN + t * PLE + c * P, P), ident[:])
                tr.then_inc(p_turned, 1)

        def ple_scalar(act, nth):
            act.dma_start(at(PIN, NT * PLE).rearrange("p (t c) -> p t c", t=NT),
                          A["p"][nth].rearrange("(t p) c -> p t c", p=P)).then_inc(p_in, 16)
            for t in range(NT):
                act.wait_ge(p_turned, NT * nth + t + 1)
                nc.scalar.activation(p_place(u_hi, t), p_bank(t), ACT.Copy).then_inc(p_hi, 1)

        def ple_vector(dve, nth):
            for t in range(NT):
                dve.wait_ge(p_hi, NT * nth + t + 1)
                nc.vector.tensor_tensor(p_place(u_lo, t), p_bank(t), p_place(u_hi, t).bitcast(F32), ALU.subtract)

        def gate_scalar(act, nth):
            def take(i, j):
                act.wait_ge(e_used, 8 * nth + 4 * i + j + 1)
                return nc.scalar.activation(at(E + j * 512), bank(j), ACT.Sigmoid)
            project_scalar(act, f"ple{nth}_gate", take)

        def gate_vector(dve, nth):
            if nth == 0:
                dve.sem_inc(e_used, 4)
            run = RUNS[f"ple{nth}_gate"]
            for i in blocks_of(dve, run):
                for j in range(4):
                    dve.wait_ge(bank_free["act"], run["taken"] + 4 * i + j + 5)
                    nc.vector.tensor_tensor(at(E + j * 512), at(E + j * 512), at(PP + j * D + i * 512), ALU.mult)\
                        .then_inc(e_mul, 1)
                    dve.wait_ge(e_mul, 8 * nth + 4 * i + j + 1)
                    dst = x[:, bass.ds(j * D + i * 512, 512)] if not isinstance(i, int) else \
                        x[:, j * D + i * 512:j * D + i * 512 + 512]
                    nc.vector.tensor_tensor(dst, dst, at(E + j * 512), ALU.add).then_inc(e_used, 1)

        CQ, LXN, ROPE_K, ROPE_Q = mla.P0, V, mla.P0 + NT * 640, mla.P0 + NT * 640 + T
        assert ROPE_Q + T <= ARENA
        rope_in = sem("rope_in")
        MLA_SCALE = (64 + ROPE) ** -0.5

        def rotate(dve, b, table, tmp, dst):
            done("dve", nc.vector.tensor_tensor(at(tmp, T, 64, 96), psum[64:96, b, :], at(table, T, 64, 96), ALU.mult))
            done("dve", nc.vector.tensor_tensor(at(tmp + T, T, 64, 96), psum[96:128, b, :], at(table, T, 96, 128), ALU.mult))
            settle("dve", dve)
            return nc.vector.tensor_tensor(dst, at(tmp, T, 64, 96), at(tmp + T, T, 64, 96), ALU.add)

        def load_rope(act):
            act.dma_start(at(ROPE_K, 2 * T), A["rope"]).then_inc(rope_in, 16)

        def rope_vector(dve):
            dve.wait_ge(rope_in, 16)
            def take(i, j):
                done("dve", rotate(dve, 0, ROPE_K, QT, at(mla.KR, T, 64, 96)))
                settle("dve", dve)
                return nc.vector.tensor_copy(at(mla.KR, T, 0, 32), at(mla.KR, T, 64, 96))
            project_vector(dve, "mla_rope", take, banks=1)

        def mla_q_vector(dve):
            def take(i, j):
                h = 4 * i + j
                u, half = h // 2, h % 2
                nc.vector.tensor_scalar(at(QT + u * T, T, 64 * half, 64 * half + 64), psum[0:64, j, :], MLA_SCALE, None, ALU.mult)
                return rotate(dve, j, ROPE_Q, CQ + 2 * T * (h % 2), at(TAIL + u * T, T, *mla.rope_rows(half)))
            project_vector(dve, "mla_q", take)

        @block.tensor
        def _(pe):
            setup_tensor(pe)
            finish("pe", pe)
            norm_tensor(pe, 0, 0, D)
            finish("pe", pe)
            for name in ("nsa_q", "nsa_k", "nsa_v"):
                project_tensor(pe, name)
            project_tensor(pe, "nsa_gate")
            project_tensor(pe, "nsa_z")
            finish("pe", pe)
            compress_tensor(pe)
            finish("pe", pe)
            attend_tensor(pe, nsa, 0)
            attend_tensor(pe, nsa, 1, first=False)
            finish("pe", pe)
            finish("pe", pe)
            project_tensor(pe, "nsa_out")
            finish("pe", pe)
            norm_tensor(pe, 2, 0, D)
            finish("pe", pe)
            for name in ("diff_q", "diff_k", "diff_v", "diff_z"):
                project_tensor(pe, name)
            finish("pe", pe)
            attend_tensor(pe, diff)
            finish("pe", pe)
            subln_tensor(pe)
            finish("pe", pe)
            project_tensor(pe, "diff_out")
            finish("pe", pe)
            norm_tensor(pe, 4, 0, D)
            finish("pe", pe)
            for name in ("na_q", "na_k", "na_v", "na_z"):
                project_tensor(pe, name)
            finish("pe", pe)
            attend_tensor(pe, na)
            finish("pe", pe)
            finish("pe", pe)
            project_tensor(pe, "na_out")
            finish("pe", pe)
            ple_tensor(pe, 0)
            finish("pe", pe)
            project_tensor(pe, "ple0_proj")
            finish("pe", pe)
            norm_tensor(pe, 5, 0, D)
            finish("pe", pe)
            project_tensor(pe, "ple0_gate")
            finish("pe", pe)
            norm_tensor(pe, 6, 0, D)
            finish("pe", pe)
            project_tensor(pe, "mla_cq")
            project_tensor(pe, "mla_ckv")
            project_tensor(pe, "mla_rope", banks=1)
            project_tensor(pe, "mla_z")
            finish("pe", pe)
            norm_tensor(pe, 7, LXN, 640)
            finish("pe", pe)
            for name in ("mla_q", "mla_k", "mla_v"):
                project_tensor(pe, name)
            finish("pe", pe)
            attend_tensor(pe, mla)
            finish("pe", pe)
            finish("pe", pe)
            project_tensor(pe, "mla_out")
            finish("pe", pe)
            ple_tensor(pe, 1)
            finish("pe", pe)
            project_tensor(pe, "ple1_proj")
            finish("pe", pe)
            norm_tensor(pe, 8, 0, D)
            finish("pe", pe)
            project_tensor(pe, "ple1_gate")
            finish("pe", pe)

        @block.scalar
        def _(act):
            setup_scalar(act)
            finish("act", act)
            norm_scalar(act, 0)
            finish("act", act)
            load_strips(act, 0)
            load_strips(act, 1)
            project_scalar(act, "nsa_q")
            load_strips(act, 2)
            load_strips(act, 3)
            project_scalar(act, "nsa_k")
            project_scalar(act, "nsa_v")
            project_scalar(act, "nsa_gate", lambda i, j: nc.scalar.activation(
                gate[:, j * 48:(j + 1) * 48], bank(j, 48), ACT.Sigmoid))
            act.wait_ge(strip_used, 4 * 4)
            project_scalar(act, "nsa_z", silu_features(Z))
            finish("act", act)
            compress_scalar(act)
            finish("act", act)
            attend_scalar(act, nsa, 0)
            attend_scalar(act, nsa, 1)
            finish("act", act)
            split_output_scalar(act, Z, 0)
            finish("act", act)
            project_scalar(act, "nsa_out")
            finish("act", act)
            norm_scalar(act, 1)
            norm_scalar(act, 2)
            finish("act", act)
            for name in ("diff_q", "diff_k", "diff_v"):
                project_scalar(act, name)
            project_scalar(act, "diff_z", silu_features(Z))
            finish("act", act)
            attend_scalar(act, diff)
            finish("act", act)
            subln_scalar(act)
            split_output_scalar(act, Z, 1)
            finish("act", act)
            project_scalar(act, "diff_out")
            finish("act", act)
            norm_scalar(act, 3)
            norm_scalar(act, 4)
            finish("act", act)
            act.wait_ge(rpb_out, 16)
            act.dma_start(at(na.MASK, GRID_W), A["colmask"]).then_inc(small_in, 16)
            for name in ("na_q", "na_k", "na_v"):
                project_scalar(act, name)
            project_scalar(act, "na_z", silu_features(Z))
            finish("act", act)
            attend_scalar(act, na)
            finish("act", act)
            split_output_scalar(act, Z, 2)
            finish("act", act)
            project_scalar(act, "na_out")
            finish("act", act)
            ple_scalar(act, 0)
            finish("act", act)
            project_scalar(act, "ple0_proj")
            finish("act", act)
            norm_scalar(act, 5)
            finish("act", act)
            gate_scalar(act, 0)
            finish("act", act)
            norm_scalar(act, 6)
            finish("act", act)
            load_rope(act)
            for name in ("mla_cq", "mla_ckv", "mla_rope"):
                project_scalar(act, name)
            project_scalar(act, "mla_z", silu_features(Z))
            finish("act", act)
            norm_scalar(act, 7)
            finish("act", act)
            for name in ("mla_q", "mla_k", "mla_v"):
                project_scalar(act, name)
            finish("act", act)
            attend_scalar(act, mla)
            finish("act", act)
            split_output_scalar(act, Z, 3)
            finish("act", act)
            project_scalar(act, "mla_out")
            finish("act", act)
            ple_scalar(act, 1)
            finish("act", act)
            project_scalar(act, "ple1_proj")
            finish("act", act)
            norm_scalar(act, 8)
            finish("act", act)
            gate_scalar(act, 1)
            finish("act", act)
            xn0 = NT * norm_base(9)[0]
            for t in range(NT):
                act.wait_ge(xn_done, xn0 + t + 1)
                act.dma_start(out[t * P:(t + 1) * P, :], at(t * D, D)).then_inc(out_written, 16)
            act.wait_ge(out_written, 16 * NT)

        @block.gpsimd
        def _(pool):
            setup_pool(pool)
            finish("pool", pool)
            norm_pool(pool, 0)
            finish("pool", pool)
            for name in ("nsa_q", "nsa_k", "nsa_v", "nsa_gate", "nsa_z"):
                project_pool(pool, name)
            finish("pool", pool)
            project_pool(pool, "nsa_cmp")
            finish("pool", pool)
            attend_pool(pool, nsa, 0)
            attend_pool(pool, nsa, 1)
            finish("pool", pool)
            finish("pool", pool)
            project_pool(pool, "nsa_out")
            finish("pool", pool)
            norm_pool(pool, 1)
            norm_pool(pool, 2)
            finish("pool", pool)
            for name in ("diff_q", "diff_k", "diff_v", "diff_z"):
                project_pool(pool, name)
            finish("pool", pool)
            attend_pool(pool, diff)
            finish("pool", pool)
            subln_pool(pool)
            finish("pool", pool)
            project_pool(pool, "diff_out")
            finish("pool", pool)
            norm_pool(pool, 3)
            norm_pool(pool, 4)
            finish("pool", pool)
            for name in ("na_q", "na_k", "na_v", "na_z"):
                project_pool(pool, name)
            finish("pool", pool)
            attend_pool(pool, na)
            finish("pool", pool)
            finish("pool", pool)
            project_pool(pool, "na_out")
            finish("pool", pool)
            finish("pool", pool)
            project_pool(pool, "ple0_proj")
            finish("pool", pool)
            norm_pool(pool, 5)
            finish("pool", pool)
            project_pool(pool, "ple0_gate")
            finish("pool", pool)
            norm_pool(pool, 6)
            finish("pool", pool)
            for name in ("mla_cq", "mla_ckv", "mla_rope", "mla_z"):
                project_pool(pool, name)
            finish("pool", pool)
            norm_pool(pool, 7)
            finish("pool", pool)
            for name in ("mla_q", "mla_k", "mla_v"):
                project_pool(pool, name)
            finish("pool", pool)
            attend_pool(pool, mla)
            finish("pool", pool)
            finish("pool", pool)
            project_pool(pool, "mla_out")
            finish("pool", pool)
            finish("pool", pool)
            project_pool(pool, "ple1_proj")
            finish("pool", pool)
            norm_pool(pool, 8)
            finish("pool", pool)
            project_pool(pool, "ple1_gate")
            finish("pool", pool)
            norm_pool(pool, 9)

        def y_tile(t, lo, hi):
            return at(KT + t * D + lo, hi - lo)

        def cq_tile(t, lo, hi):
            return at(CQ + t * 640 + lo, hi - lo)

        def post_norm(dve, k):
            norm_vector(dve, k, y_tile, 0, D)
            dve.wait_ge(xn_done, NT * norm_base(k + 1)[0])
            for t in range(NT):
                done("dve", nc.vector.tensor_tensor(x_tile(t, 0, D), x_tile(t, 0, D), at(t * D, D), ALU.add))
            settle("dve", dve)

        @block.vector
        def _(dve):
            setup_vector(dve)
            finish("dve", dve)
            norm_vector(dve, 0, x_tile, 0, D)
            finish("dve", dve)
            project_vector(dve, "nsa_q", to_features(QT, 0.125))
            cut_strips(dve, 0)
            cut_strips(dve, 1)
            project_vector(dve, "nsa_k", to_features(KT))
            cut_strips(dve, 2)
            cut_strips(dve, 3)
            project_vector(dve, "nsa_v", to_tokens(V, 512))
            finish("dve", dve)
            compress_vector(dve)
            finish("dve", dve)
            attend_vector(dve, nsa, 0)
            attend_vector(dve, nsa, 1, first=False)
            finish("dve", dve)
            split_output_vector(dve, Z, 0)
            finish("dve", dve)
            project_vector(dve, "nsa_out", to_tokens(KT, D))
            finish("dve", dve)
            post_norm(dve, 1)
            norm_vector(dve, 2, x_tile, 0, D)
            finish("dve", dve)
            project_vector(dve, "diff_q", to_features(QT, 0.125))
            project_vector(dve, "diff_k", to_features(KT))
            project_vector(dve, "diff_v", to_tokens(V, D))
            finish("dve", dve)
            attend_vector(dve, diff)
            finish("dve", dve)
            subln_vector(dve)
            split_output_vector(dve, Z, 1)
            finish("dve", dve)
            project_vector(dve, "diff_out", to_tokens(KT, D))
            finish("dve", dve)
            post_norm(dve, 3)
            norm_vector(dve, 4, x_tile, 0, D)
            finish("dve", dve)
            project_vector(dve, "na_q", to_features(QT, 0.125))
            project_vector(dve, "na_k", to_features(KT))
            project_vector(dve, "na_v", to_tokens(V, D))
            dve.wait_ge(small_in, 16)
            finish("dve", dve)
            attend_vector(dve, na)
            finish("dve", dve)
            split_output_vector(dve, Z, 2)
            finish("dve", dve)
            project_vector(dve, "na_out", add_residual)
            finish("dve", dve)
            ple_vector(dve, 0)
            finish("dve", dve)
            project_vector(dve, "ple0_proj", to_tokens(PP, D))
            finish("dve", dve)
            norm_vector(dve, 5, x_tile, 0, D)
            finish("dve", dve)
            gate_vector(dve, 0)
            finish("dve", dve)
            norm_vector(dve, 6, x_tile, 0, D)
            finish("dve", dve)
            project_vector(dve, "mla_cq", to_tokens(CQ, 640, Q_RANK))
            project_vector(dve, "mla_ckv", to_tokens(CQ + Q_RANK, 640, KV_RANK))
            rope_vector(dve)
            finish("dve", dve)
            norm_vector(dve, 7, cq_tile, LXN, 640)
            finish("dve", dve)
            mla_q_vector(dve)
            project_vector(dve, "mla_k", to_features(KT))
            project_vector(dve, "mla_v", to_tokens(V, D))
            finish("dve", dve)
            attend_vector(dve, mla)
            finish("dve", dve)
            split_output_vector(dve, Z, 3)
            finish("dve", dve)
            project_vector(dve, "mla_out", add_residual)
            finish("dve", dve)
            ple_vector(dve, 1)
            finish("dve", dve)
            project_vector(dve, "ple1_proj", to_tokens(PP, D))
            finish("dve", dve)
            norm_vector(dve, 8, x_tile, 0, D)
            finish("dve", dve)
            gate_vector(dve, 1)
            finish("dve", dve)
            norm_vector(dve, 9, x_tile, 0, D)


def _constants():
    n = np.arange(SPAN)
    dist = np.maximum(511 - n, 0)
    exact = BUCKETS // 2
    nf = np.maximum(dist, 1).astype(np.float32)
    large = exact + (np.log(nf / np.float32(exact)) / np.float32(np.log(128 / exact))
                     * np.float32(BUCKETS - exact)).astype(np.int32)
    bucket = np.where(dist < exact, dist, np.minimum(large, BUCKETS - 1))
    onehot = (np.arange(BUCKETS)[:, None] == bucket[None, :]).astype(np.float32)
    rowmask = np.tile(np.where(511 - n >= 0, 0.0, MASKED).astype(np.float32), (HEADS, 1))
    col = np.arange(GRID_W)
    start = np.clip(col - 8, 0, GRID_W - 16)
    inside = (col[None, :] >= start[:, None]) & (col[None, :] < start[:, None] + 16)
    colmask = np.tile(np.where(inside, 0.0, MASKED).astype(np.float32), (2, 1))
    inv = (1.0 / (np.float32(10000.0) ** (np.arange(0, ROPE, 2, dtype=np.float32) / np.float32(ROPE)))).astype(np.float32)
    ang = np.arange(T, dtype=np.float32)[None, :] * inv[:, None]
    cos, sin = np.cos(ang), np.sin(ang)
    rope = np.zeros((P, T), np.float32)
    rope[64:96] = np.concatenate([cos, cos])
    rope[96:128] = np.concatenate([-sin, sin])
    rope = np.concatenate([rope, rope * np.float32((64 + ROPE) ** -0.5)], axis=1)
    return dict(onehot=onehot, rowmask=rowmask, colmask=colmask, rope=rope, ident=np.eye(P, dtype=np.float32))


def _units(w, run):
    units = []
    for i in range(run["blocks"]):
        k = 0
        for nk in run["nks"]:
            part = w[k * P:(k + nk) * P, i * run["width"]:(i + 1) * run["width"]]
            u = np.zeros((P, UNIT), w.dtype)
            u[:, :nk * run["width"]] = part.reshape(nk, P, run["width"]).transpose(1, 0, 2).reshape(P, -1)
            units.append(u)
            k += nk
    return units


def _layout(inputs):
    f = {k: np.asarray(v) for k, v in inputs.items()}
    w = f["nsa_w_in"][0]
    kv = [w[:, D + 256 * n:D + 256 * (n + 1)] for n in range(6)]
    slots = np.array([(2 * gp + half) * 4 + j for gp in range(2) for j in range(4) for half in range(2)])
    cols = (slots[:, None] * 64 + np.arange(64)).reshape(-1)
    mats = {"nsa_q": w[:, :D][:, cols], "nsa_k": np.concatenate([kv[0], kv[1], kv[2], kv[4]], 1),
            "nsa_v": np.concatenate([kv[3], kv[5]], 1), "nsa_gate": w[:, 2560:2608], "nsa_z": w[:, 2608:][:, cols],
            "nsa_out": f["nsa_w_out"][0][cols]}
    for n, name in enumerate(("q", "k", "v", "z")):
        mats[f"diff_{name}"] = f["diff_w_in"][0][:, n * D:(n + 1) * D]
        mats[f"na_{name}"] = f["na_w_in_2"][0][:, n * D:(n + 1) * D]
    mats["diff_out"], mats["na_out"], mats["mla_out"] = f["diff_w_out"][0], f["na_w_out_2"][0], f["mla_w_out_2"][0]
    w = f["mla_w_in_2"][0]
    mats["mla_cq"], mats["mla_ckv"] = w[:, :Q_RANK], w[:, Q_RANK:Q_RANK + KV_RANK]
    r = w[:, Q_RANK + KV_RANK:Q_RANK + KV_RANK + ROPE]
    swapped = np.concatenate([r[:, 16:], r[:, :16]], 1)
    mats["mla_rope"] = np.concatenate([r, swapped, r, swapped], 1)
    mats["mla_z"] = w[:, Q_RANK + KV_RANK + ROPE:]
    q = f["mla_w_qb_2"][0].reshape(Q_RANK, HEADS, 96)
    mats["mla_q"] = np.concatenate([q, q[:, :, 80:96], q[:, :, 64:80]], 2).reshape(Q_RANK, HEADS * P)
    k = f["mla_w_kvb_2"][0].reshape(KV_RANK, HEADS, P)
    mats["mla_k"], mats["mla_v"] = k[:, :, :64].reshape(KV_RANK, D), k[:, :, 64:].reshape(KV_RANK, D)
    for i in range(2):
        mats[f"ple{i}_gate"], mats[f"ple{i}_proj"] = f["ple_w_gate_2"][i], f["ple_w_proj_2"][i]
    units = []
    for name, run in RUNS.items():
        if name == "nsa_cmp":
            w1 = [f[n][0].reshape(32, 64, P).transpose(1, 0, 2).reshape(64, 32 * P) for n in ("nsa_cmp_w1_k", "nsa_cmp_w1_v")]
            w1 = np.concatenate(w1, 0)
            units += [w1[:, :UNIT], w1[:, UNIT:]]
        else:
            units += _units(mats[name], run)
    latent = np.zeros(D, np.float32)
    latent[:Q_RANK], latent[Q_RANK:Q_RANK + KV_RANK] = f["mla_q_norm_2"][0], f["mla_kv_norm_2"][0]
    gains = [f["norm_pre"][0], f["norm_post"][0], f["norm_pre"][1], f["norm_post"][1], f["norm_g_2"][0],
             f["ple_norm_2"][0], f["norm_g_2"][1], latent, f["ple_norm_2"][1], f["final_norm_2"]]
    rpb = np.zeros((1, RPB_LEN), np.float32)
    rpb[0, RPB_PAD:-RPB_PAD] = f["na_rpb_2"][0].reshape(-1)
    twice = lambda a: np.concatenate([a, a], 0)
    data = dict(
        x=f["x"][0], weights=np.stack(units), gains=np.stack(gains), table=f["rel_bias_table"],
        subln=f["diff_subln"][0].reshape(DIFF_HEADS, P).T,
        pe_k=twice(f["nsa_cmp_pe_k"][0].T), pe_v=twice(f["nsa_cmp_pe_v"][0].T),
        w2_k=twice(f["nsa_cmp_w2_k"][0].T).T, w2_v=f["nsa_cmp_w2_v"][0],
        lambdas=np.concatenate([f[f"diff_lambda_{n}"] for n in ("q1", "k1", "q2", "k2")], 1), rpb=rpb, p=f["p_2"][:, 0])
    data.update(_constants())
    return {k: np.ascontiguousarray(v) for k, v in data.items()}


def kernel(**inputs):
    import concourse.bacc as bacc
    from concourse.bass_utils import run_bass_kernel_spmd

    data = _layout(inputs)
    nc = bacc.Bacc("TRN2", target_bir_lowering=False, num_devices=1)
    aps = {k: nc.dram_tensor(f"in_{k}", v.shape, F32, kind="ExternalInput").ap() for k, v in data.items()}
    out = nc.dram_tensor("out_x", (T, D), F32, kind="ExternalOutput").ap()
    _program(nc, aps, out)
    r = run_bass_kernel_spmd(nc, [{f"in_{k}": v for k, v in data.items()}], core_ids=[0])
    return r.results[0]["out_x"].reshape(1, T, D)
```

```python
from contextlib import ExitStack, contextmanager

import numpy as np

import concourse.bass as bass
from concourse import mybir

F32 = mybir.dt.float32
F32R = mybir.dt.float32r
ALU = mybir.AluOpType
ACT = mybir.ActivationFunctionType
AX = mybir.AxisListType.X

P = 128
D = 1024
T = 512
NT = T // P
KC = D // P
UNIT = 2048
EPS = 1e-6
BIG = 3.0e38
MASKED = -1e30
BUCKETS = 32
HEADS = 16
DIFF_HEADS = 8
LAMBDA_INIT = 0.8 - 0.6 * float(np.exp(-0.3))
SPAN = 1024
STRIP = 896
CMP = 31
GRID_W = 64
RPB_ROW, RPB_HEAD = 31, 15 * 31
RPB_PAD = 48
RPB_LEN = HEADS * RPB_HEAD + 2 * RPB_PAD
Q_RANK, KV_RANK = 384, 256
ROPE = 32
PLE = 256

RUNS = {}
N_UNITS = 0
N_BLOCKS = 0


def _run(name, blocks, nks, width, mode, k0=0):
    global N_UNITS, N_BLOCKS
    taker = "act" if name.endswith(("_z", "gate", "cmp")) else "dve"
    RUNS[name] = dict(name=name, blocks=blocks, nks=nks, width=width, mode=mode, k0=k0,
                      unit=N_UNITS, block=N_BLOCKS, taker=taker,
                      taken=sum(4 * r["blocks"] for r in RUNS.values() if r["taker"] == taker),
                      others=sum(4 * r["blocks"] for r in RUNS.values() if r["taker"] != taker))
    N_UNITS += blocks * len(nks)
    N_BLOCKS += blocks


_run("nsa_q", 2, (4, 4), 512, "features")
_run("nsa_k", 2, (4, 4), 512, "features")
_run("nsa_v", 1, (4, 4), 512, "tokens")
_run("nsa_gate", 1, (8,), 48, "tokens")
_run("nsa_z", 2, (4, 4), 512, "features")
_run("nsa_cmp", 1, (16, 16), 128, "compress")
_run("nsa_out", 2, (4, 4), 512, "tokens")
_run("diff_q", 2, (4, 4), 512, "features")
_run("diff_k", 2, (4, 4), 512, "features")
_run("diff_v", 2, (4, 4), 512, "tokens")
_run("diff_z", 2, (4, 4), 512, "features")
_run("diff_out", 2, (4, 4), 512, "tokens")
_run("na_q", 2, (4, 4), 512, "features")
_run("na_k", 2, (4, 4), 512, "features")
_run("na_v", 2, (4, 4), 512, "tokens")
_run("na_z", 2, (4, 4), 512, "features")
_run("na_out", 2, (4, 4), 512, "tokens")
_run("ple0_proj", 2, (2,), 512, "tokens")
_run("ple0_gate", 2, (4, 4), 512, "tokens")
_run("mla_cq", 1, (4, 4), 384, "tokens")
_run("mla_ckv", 1, (4, 4), 256, "tokens")
_run("mla_rope", 1, (8,), 128, "features")
_run("mla_z", 2, (4, 4), 512, "features")
_run("mla_q", 4, (3,), 512, "features")
_run("mla_k", 2, (2,), 512, "features", 3)
_run("mla_v", 2, (2,), 512, "tokens", 3)
_run("mla_out", 2, (4, 4), 512, "tokens")
_run("ple1_proj", 2, (2,), 512, "tokens")
_run("ple1_gate", 2, (4, 4), 512, "tokens")

GAINS = ["pre0", "post0", "pre1", "post1", "na", "ple0", "mla", "latent", "ple1", "final"]


def tri(n):
    return P * n * (n + 1) // 2


@contextmanager
def repeat(eng, first, end):
    if end == first + 1:
        yield first
    else:
        with eng.Fori(first, end) as i:
            yield i


LOOK = 2


class Attention:

    def __init__(self, name, passes, per_head, causal, ahead, bufs, cmp=False, scores_first=True, qk_at=0, low_out_at=1):
        self.scores_first, self.qk_at, self.low_out_at = scores_first, qk_at, low_out_at
        self.name, self.passes, self.per_head, self.causal = name, passes, per_head, causal
        self.maps = 2 * per_head
        self.ahead, self.bufs = ahead, bufs
        diff = name == "diff"
        self.turns = []
        for a in range(2):
            if cmp:
                self.turns.append(("cmp", a, None))
            if diff:
                self.turns.append(("full", a, 2 * a))
            else:
                self.turns += [("full", a, per_head * a + b) for b in range(per_head)]
        self.use = []
        n = 0
        for kind, _, _ in self.turns:
            self.use.append(n)
            n += 1 if kind == "cmp" else NT
        self.uses = n
        self.tiles = [(t, kt) for t, (kind, _, _) in enumerate(self.turns) for kt in range(1 if kind == "cmp" else NT)]
        self.credit = 2 * n
        self.diff = diff
        self.maps_per_turn = 2 if diff else 1
        self.mla = name == "mla"

    def length(self, qt):
        return P * (qt + 1) if self.causal else T

    def p_at(self, qt):
        return tri(qt) if self.causal else T * qt

    def p_size(self):
        return tri(NT) if self.causal else NT * T

    def pt_at(self, kt):
        return tri(NT) - tri(NT - kt) if self.causal else T * kt

    def first_q(self, kt):
        return kt if self.causal else 0

    def turn_of(self, m):
        if self.diff:
            m = m - m % 2
        return next(t for t, (kind, _, mm) in enumerate(self.turns) if kind == "full" and mm == m)

    def released(self, m):
        return self.turned_by(m - self.bufs)

    def turned_by(self, m):
        return (m // self.maps) * self.uses + self.use[self.turn_of(m % self.maps)] + NT - 1

    def last_use(self, head):
        return max(self.use[t] + (NT if k == "full" else 1) - 1
                   for t, (k, a, _) in enumerate(self.turns) if a == head)

    def scores_beside(self, n):
        t, kt = self.tiles[n]
        kind, _, m = self.turns[t]
        if kind == "cmp":
            return []
        if self.bufs > self.ahead:
            return [(m + self.ahead, kt)]
        if kt < LOOK:
            return []
        step = self.maps_per_turn
        flat = [(m + self.ahead + s, qt) for s in range(step) for qt in range(NT)]
        share = len(flat) // (NT - LOOK)
        return flat[share * (kt - LOOK):share * (kt - LOOK + 1)]

    def first_turn(self, t):
        return self.turns[t][0] == "full" and (t == 0 or self.turns[t - 1][:2] != self.turns[t][:2])

    def head_end(self, a):
        return self.last_use(a) + 1

    def high_index(self, t):
        return NT * sum(kind == "full" for kind, _, _ in self.turns[:t])


NORMS = [("pre0", ((0, D),), KC, 0), ("post0", ((0, D),), 0, 1), ("pre1", ((0, D),), KC, 2),
         ("post1", ((0, D),), 0, 3), ("na", ((0, D),), KC, 4), ("ple0", ((0, D),), KC, 5),
         ("mla", ((0, D),), KC, 6), ("latent", ((0, Q_RANK), (Q_RANK, Q_RANK + KV_RANK)), 5, 7),
         ("ple1", ((0, D),), KC, 8), ("final", ((0, D),), 0, 9)]


def norm_base(k):
    seg = sum(len(n[1]) for n in NORMS[:k])
    banks = sum((2 * NT if n[2] else 0) for n in NORMS[:k])
    return seg, k, banks


def _program(nc, A, out):
    with ExitStack() as ctx:
        def sb(name, cols, dt=F32):
            return ctx.enter_context(nc.sbuf_tensor(name, [P, cols], dt))

        def sem(name):
            return ctx.enter_context(nc.semaphore(name))

        x = sb("x", NT * D)
        u_hi, u_lo = sb("u_hi", KC * T, F32R), sb("u_lo", KC * T, F32R)
        stage = [sb(f"stage{b}", UNIT) for b in range(2)]
        w_hi = [sb(f"w_hi{b}", UNIT, F32R) for b in range(2)]
        w_lo = [sb(f"w_lo{b}", UNIT, F32R) for b in range(2)]
        gain = [sb(f"gain{b}", D) for b in range(2)]
        ident = sb("ident", P)
        ss = sb("ss", 2 * NT)
        ms = sb("ms", 2 * NT)
        half_exp = sb("half_exp", 1)
        neg_max = sb("neg_max", 4 * NT)
        row_sum = sb("row_sum", 4 * NT)
        inv = sb("inv", 4 * NT)
        zero = sb("zero", 1)
        neg_lam = sb("neg_lam", 4)
        gate = sb("gate", NT * 48)
        subln = sb("subln", DIFF_HEADS)
        spare_r = sb("spare_r", 2 * T, F32R)
        ARENA = 25096
        arena = sb("arena", ARENA)
        psum = ctx.enter_context(nc.psum_tensor("psum", [P, 8, 512], F32))

        def bank(n, width=512):
            return psum[:, n, 0:width]

        def at(off, width=512, lo=0, hi=P):
            return arena[lo:hi, bass.ds(off, width)] if not isinstance(off, int) else arena[lo:hi, off:off + width]

        QT, KT, V, Z = 0, 4096, 8192, 12288
        TAIL = 16384
        N_CK, N_VC, N_PC = TAIL, TAIL + 64, TAIL + 64 + 4 * P
        N_P = N_PC + HEADS * NT * CMP
        N_CB = ARENA - HEADS * NT * CMP
        bias_rows = nc.dram_tensor("bias_rows", (P, HEADS * SPAN), F32, kind="Internal").ap()
        rpb_rows = nc.dram_tensor("rpb_rows", (GRID_W, RPB_LEN), F32, kind="Internal").ap()

        w_loaded = [sem(f"w_loaded{b}") for b in range(2)]
        w_high, w_ready = sem("w_high"), sem("w_ready")
        w_used = sem("w_used")
        bank_done = sem("bank_done")
        bank_free = {"act": sem("bank_free_act"), "dve": sem("bank_free_dve")}
        stage_end, held = sem("stage_end"), sem("held")
        x_in, const_in, small_in = [sem(f"x_in{t}") for t in range(NT)], sem("const_in"), sem("small_in")
        sq_act, x_added = sem("sq_act"), sem("x_added")
        gain_in = [sem("gain_in0"), sem("gain_in1")]
        out_written = sem("out_written")
        rows_made, rows_out = sem("rows_made"), sem("rows_out")
        strip_in, strip_used = [sem("strip_in0"), sem("strip_in1")], sem("strip_used")
        sq_done, ms_done, rstd_done, xn_done = sem("sq_done"), sem("ms_done"), sem("rstd_done"), sem("xn_done")
        turned, u_hi_done, u_lo_done = sem("turned"), sem("u_hi_done"), sem("u_lo_done")
        dve_step, act_step, pool_step, pe_step = sem("dve_step"), sem("act_step"), sem("pool_step"), sem("pe_step")
        own = {"dve": [dve_step, 0], "act": [act_step, 0], "pool": [pool_step, 0], "pe": [pe_step, 0]}

        def done(who, ins):
            own[who][1] += 1
            ins.then_inc(own[who][0], 1)

        def settle(who, eng):
            eng.wait_ge(own[who][0], own[who][1])

        stages = {"pe": 0, "act": 0, "dve": 0}

        def finish(who, eng, meanwhile=None):
            stages[who] += 1
            eng.drain().then_inc(stage_end, 1)
            if meanwhile:
                split_after(eng, meanwhile)
            eng.wait_ge(stage_end, 3 * stages[who])

        def hold(eng):
            eng.sem_inc(held, 1)

        block = ctx.enter_context(nc.Block())

        @block.sync
        def _(sp):
            def unit(n, b):
                sp.dma_start(stage[b][:], A["weights"][n]).then_inc(w_loaded[b], 16)

            for t in range(NT):
                sp.dma_start(x[:, t * D:(t + 1) * D], A["x"][t * P:(t + 1) * P]).then_inc(x_in[t], 16)
            sp.wait_ge(x_in[NT - 1], 16)
            unit(0, 0)
            unit(1, 1)
            assert N_UNITS % 2 == 0
            with sp.Fori(1, N_UNITS // 2) as i:
                for b in range(2):
                    sp.wait_ge(w_ready, 2 * i + b - 1)
                    sp.dma_start(stage[b][:], A["weights"][bass.ds(2 * i + b, 1)].rearrange("o p n -> p (o n)"))\
                        .then_inc(w_loaded[b], 16)
            sp.wait_ge(out_written, 16 * NT)

        def split_high(act, n, b, arrivals):
            act.wait_ge(w_loaded[b], 16 * arrivals)
            nc.scalar.activation(w_hi[b][:], stage[b][:], ACT.Copy).then_inc(w_high, 1)

        def split_low(pool, n, b):
            pool.wait_ge(w_high, n + 1)
            nc.gpsimd.tensor_tensor(w_lo[b][:], stage[b][:], w_hi[b][:].bitcast(F32), ALU.subtract)\
                .then_inc(w_ready, 1)

        def pairs_before(run):
            return sum(r["blocks"] for r in RUNS.values() if r["unit"] < run["unit"] and len(r["nks"]) == 2)

        def blocks_of(eng, run):
            if len(run["nks"]) == 2 and run["name"] != "ple1_gate" and run["blocks"] > 1:
                with eng.Fori(0, run["blocks"]) as i:
                    yield i
            else:
                yield from range(run["blocks"])

        def next_unit(run, i, a):
            u = len(run["nks"])
            b = (run["unit"] + a + (0 if u == 2 else i)) % 2
            n = run["unit"] + u * i + a + 2
            if u == 2:
                return n, b, (run["unit"] + a) // 2 + i + 2
            return n, b, n // 2 + 1

        def exists(n):
            return not isinstance(n, int) or n < N_UNITS

        def wait_used(eng, run, i, a):
            if a + 1 < len(run["nks"]):
                eng.wait_ge(w_used, pairs_before(run) + i + 1)
            else:
                eng.wait_ge(bank_done, 4 * (run["block"] + i) + 4)

        def wait_bank(pe, run, i, j):
            other = "dve" if run["taker"] == "act" else "act"
            pe.wait_ge(bank_free[run["taker"]], run["taken"] + 4 * i + j + 1)
            pe.wait_ge(bank_free[other], run["others"] + j + 1)

        out_hi, out_low = sem("out_hi"), sem("out_low")

        def project_tensor(pe, name, banks=4, nth_output=None):
            run = RUNS[name]
            w = run["width"]
            for i in blocks_of(pe, run):
                k0 = run["k0"]
                for a, nk in enumerate(run["nks"]):
                    u = len(run["nks"])
                    b = (run["unit"] + a + (0 if u == 2 else i)) % 2
                    pe.wait_ge(w_ready, run["unit"] + u * i + a + 1)
                    for j in range(banks):
                        if a == 0:
                            wait_bank(pe, run, i, j if banks == 4 else 3)
                        for k in range(nk):
                            if nth_output is not None and j == 0 and k % 2 == 0:
                                pe.wait_ge(out_low, 4 * nth_output + (k0 + k) // 2 + 1)
                            for wl, ul in ((0, 1), (1, 0), (0, 0)):
                                ww = (w_lo if wl else w_hi)[b]
                                uu = u_lo if ul else u_hi
                                at_u = (k0 + k) * T
                                if run["mode"] == "features":
                                    lhs, rhs = ww[:, k * w + j * P:k * w + (j + 1) * P], uu[:, at_u:at_u + T]
                                    dst = bank(j)
                                else:
                                    lhs, rhs = uu[:, at_u + j * P:at_u + (j + 1) * P], ww[:, k * w:(k + 1) * w]
                                    dst = bank(j, w)
                                mm = nc.tensor.matmul(dst, lhs, rhs, start=(a == 0 and k == 0 and (wl, ul) == (0, 1)),
                                                      stop=(a + 1 == u and k + 1 == nk and (wl, ul) == (0, 0)))
                        if a + 1 == u:
                            mm.then_inc(bank_done, 4 // banks)
                    if a + 1 < u:
                        mm.then_inc(w_used, 1)
                    k0 += nk

        def project_pool(pool, name):
            run = RUNS[name]
            for i in blocks_of(pool, run):
                for a in range(len(run["nks"])):
                    n, b, _ = next_unit(run, i, a)
                    if exists(n):
                        split_low(pool, n, b)

        def split_after(act, name):
            run = RUNS[name]
            i, a = run["blocks"] - 1, len(run["nks"]) - 1
            n, b, arrivals = next_unit(run, i, a)
            wait_used(act, run, i, a)
            split_high(act, n, b, arrivals)

        def project_scalar(act, name, take=None, banks=4, ends=False):
            run = RUNS[name]
            for i in (range(run["blocks"]) if ends else blocks_of(act, run)):
                for a in range(len(run["nks"])):
                    if a + 1 == len(run["nks"]) and take:
                        for j in range(banks):
                            act.wait_ge(bank_done, 4 * (run["block"] + i) + (j + 1 if banks == 4 else 4))
                            take(i, j).then_inc(bank_free["act"], 4 // banks)
                    n, b, arrivals = next_unit(run, i, a)
                    if exists(n) and not (ends and i == run["blocks"] - 1 and a == len(run["nks"]) - 1):
                        wait_used(act, run, i, a)
                        split_high(act, n, b, arrivals)

        def project_vector(dve, name, take, banks=4):
            run = RUNS[name]
            for i in blocks_of(dve, run):
                for j in range(banks):
                    dve.wait_ge(bank_done, 4 * (run["block"] + i) + (j + 1 if banks == 4 else 4))
                    take(i, j).then_inc(bank_free["dve"], 4 // banks)

        def to_features(place, scale=1.0):
            def take(i, j):
                return nc.vector.tensor_scalar(at(place + j * T + i * 4 * T), bank(j), scale, None, ALU.mult)
            return take

        def to_tokens(place, row, width=512):
            def take(i, j):
                return nc.vector.tensor_scalar(at(place + j * row + i * 512, width), bank(j, width), 1.0, None, ALU.mult)
            return take

        def silu_features(place):
            def take(i, j):
                return nc.scalar.activation(at(place + j * T + i * 4 * T), bank(j), ACT.Silu)
            return take

        def add_residual(i, j):
            dst = x[:, bass.ds(j * D + i * 512, 512)] if not isinstance(i, int) else x[:, j * D + i * 512:j * D + i * 512 + 512]
            return nc.vector.tensor_tensor(dst, bank(j), dst, ALU.add)

        def squares_of(k, who):
            if k in (2, 4):
                return range(NT) if who == "act" else ()
            if len(NORMS[k][1]) > 1:
                return range(NT) if who == "dve" else ()
            return range(2) if who == "dve" else range(2, NT)

        def seg_gain(k, s):
            lo, hi = NORMS[k][1][s]
            return gain[k % 2][:, lo:hi]

        def load_gain(act, k):
            act.dma_start(gain[k % 2][:], bass.AP(A["gains"].tensor, k * D, [[0, P], [1, D]])).then_inc(gain_in[k % 2], 16)

        def norm_vector(dve, k, src, xn, row):
            norm_sums(dve, k, src, xn, row)
            norm_scale(dve, k, src, xn, row)
            norm_low(dve, k)

        def norm_sums(dve, k, src, xn, row):
            seg0, segs = norm_base(k)[0], NORMS[k][1]
            for s, (lo, hi) in enumerate(segs):
                for t in squares_of(k, "dve"):
                    if k == 0:
                        dve.wait_ge(x_in[t], 16)
                    nc.vector.tensor_tensor_reduce(
                        out=at(xn + t * row + lo, hi - lo), in0=src(t, lo, hi), in1=src(t, lo, hi), scale=1.0,
                        scalar=0.0, op0=ALU.mult, op1=ALU.add,
                        accum_out=ss[:, s * NT + t:s * NT + t + 1]).then_inc(sq_done, 1)
                own_sq = sum(len(n[1]) * len(squares_of(j, "dve")) for j, n in enumerate(NORMS[:k]))
                if squares_of(k, "dve"):
                    dve.wait_ge(sq_done, own_sq + len(squares_of(k, "dve")) * (s + 1))
                if squares_of(k, "act"):
                    dve.wait_ge(sq_act, sum(len(squares_of(j, "act")) for j in range(k + 1)))
                nc.vector.tensor_scalar(ms[:, s * NT:(s + 1) * NT], ss[:, s * NT:(s + 1) * NT], 1.0 / (hi - lo), EPS,
                                        ALU.mult, ALU.add).then_inc(ms_done, 1)
            if k == 0:
                setup_rows_vector(dve)

        def norm_scale(dve, k, src, xn, row):
            seg0, segs = norm_base(k)[0], NORMS[k][1]
            dve.wait_ge(gain_in[k % 2], 16 * (k // 2 + 1))
            dve.wait_ge(rstd_done, seg0 + len(segs))
            for t in range(NT):
                for s, (lo, hi) in enumerate(segs):
                    ins = nc.vector.scalar_tensor_tensor(
                        out=at(xn + t * row + lo, hi - lo), in0=src(t, lo, hi), scalar=ss[:, s * NT + t:s * NT + t + 1],
                        in1=seg_gain(k, s), op0=ALU.mult, op1=ALU.mult)
                    ins.then_inc(xn_done, 1)

        def norm_low(dve, k):
            bank0 = norm_base(k)[2]
            if NORMS[k][2]:
                for b in range(2 * NT):
                    dve.wait_ge(u_hi_done, bank0 + b + 1)
                    d, n = turned_place(k, b)
                    nc.vector.tensor_tensor(d(u_lo), turned_bank(b, n), d(u_hi).bitcast(F32), ALU.subtract)\
                        .then_inc(u_lo_done, 1)

        def turned_place(k, b):
            t, h = b // 2, b % 2
            n = min(4, NORMS[k][2] - 4 * h)

            def d(u):
                return u[:].rearrange("p (c t) -> p c t", c=KC)[:, 4 * h:4 * h + n, t * P:(t + 1) * P]
            return d, n

        def turned_bank(b, n):
            return psum[:, b, 0:n * P].rearrange("p (c t) -> p c t", c=n)

        def norm_pool(pool, k):
            seg0 = norm_base(k)[0]
            for s in range(len(NORMS[k][1])):
                pool.wait_ge(ms_done, seg0 + s + 1)
                nc.gpsimd.tensor_tensor(ss[:, s * NT:(s + 1) * NT], ms[:, s * NT:(s + 1) * NT],
                                        half_exp[:, 0:1].to_broadcast([P, NT]), ALU.pow).then_inc(rstd_done, 1)

        def wait_normed(pe, k):
            pe.wait_ge(u_lo_done, norm_base(k)[2] + 2 * NT)

        def norm_tensor(pe, k, xn, row):
            segs = NORMS[k][1]
            xn0 = NT * norm_base(k)[0]
            if k == 0:
                pe.wait_ge(rows_made, 3)
            for b in range(2 * NT):
                t, h = b // 2, b % 2
                n = min(4, NORMS[k][2] - 4 * h)
                pe.wait_ge(xn_done, xn0 + len(segs) * (t + 1))
                for c in range(n):
                    tr = nc.tensor.transpose(psum[:, b, c * P:(c + 1) * P], at(xn + t * row + (4 * h + c) * P, P), ident[:])
                tr.then_inc(turned, 1)

        def squares_scalar(act, k, src, xn, row):
            lo, hi = NORMS[k][1][0]
            for t in squares_of(k, "act"):
                if k == 0:
                    act.wait_ge(x_in[t], 16)
                elif k in (2, 4):
                    act.wait_ge(x_added, NT * (k // 2 - 1) + t + 1)
                nc.scalar.activation(at(xn + t * row + lo, hi - lo), src(t, lo, hi), ACT.Square,
                                     accum_out=ss[:, t:t + 1]).then_inc(sq_act, 1)

        def norm_scalar(act, k, src, xn=0, row=D):
            bank0 = norm_base(k)[2]
            if k not in (5, 8):
                squares_scalar(act, k, src, xn, row)
            if k == 0:
                setup_rows_scalar(act)
            if k + 1 < len(NORMS):
                if k >= 1:
                    act.wait_ge(xn_done, NT * norm_base(k)[0])
                load_gain(act, k + 1)
            if NORMS[k][2]:
                for b in range(2 * NT):
                    act.wait_ge(turned, bank0 + b + 1)
                    d, n = turned_place(k, b)
                    nc.scalar.activation(d(u_hi), turned_bank(b, n), ACT.Copy).then_inc(u_hi_done, 1)
            if k == 0:
                setup_high(act)

        def x_tile(t, lo, hi):
            return x[:, t * D + lo:t * D + hi]


        def split_output_scalar(act, src, nth):
            for c in range(0, KC, 2):
                if nth == 1:
                    act.wait_ge(sub_out, c + 2)
                nc.scalar.activation(u_hi[:, c * T:(c + 2) * T], at(src + c * T, 2 * T), ACT.Copy).then_inc(out_hi, 1)

        def split_output_vector(dve, src, nth):
            for c in range(0, KC, 2):
                dve.wait_ge(out_hi, 4 * nth + c // 2 + 1)
                nc.vector.tensor_tensor(u_lo[:, c * T:(c + 2) * T], at(src + c * T, 2 * T),
                                        u_hi[:, c * T:(c + 2) * T].bitcast(F32), ALU.subtract).then_inc(out_low, 1)

        class Stage(Attention):

            def __init__(self, *args, **kw):
                super().__init__(*args, **kw)
                n = self.name
                self.s_ready, self.s_free = sem(f"{n}_scores"), sem(f"{n}_scores_taken")
                self.exp_done = sem(f"{n}_exp")
                self.p_ready = sem(f"{n}_probs")
                self.pt_ready, self.pt_high = sem(f"{n}_turned"), sem(f"{n}_turned_high")
                self.pt_free = sem(f"{n}_turned_taken")
                self.pv_done, self.o_free, self.summed = sem(f"{n}_pv"), sem(f"{n}_out_taken"), sem(f"{n}_summed")
                self.qk_high, self.q_staged = sem(f"{n}_qk_high"), sem(f"{n}_q_staged")
                self.low_out = sem(f"{n}_low_out")
                self.v_high, self.v_staged = sem(f"{n}_v_high"), sem(f"{n}_v_staged")
                self.fixed_high, self.fixed_k, self.fixed_v = sem(f"{n}_fixed_high"), sem(f"{n}_fixed_k"), sem(f"{n}_fixed_v")
                self.bias_in = [sem(f"{n}_bias0"), sem(f"{n}_bias1")]
                self.diag = gain[1 if self.mla else 0]
                self.diag_done = sem(f"{n}_diag") if self.diff else None
                self.masked = sem(f"{n}_masked") if self.name == "na" else None
                self.vec = sem(f"{n}_vec")
                self.nsa = self.name == "nsa"
                self.pt_banks = 3 if self.nsa else 4
                assert self.uses % self.pt_banks == 0
                place = N_P if self.nsa else TAIL
                if self.mla:
                    self.KR = self.LOWV = TAIL + 8 * T
                    place = self.KR + T
                self.P0 = place
                place += self.bufs * self.p_size()
                if self.nsa:
                    self.BIAS, self.LOWV, self.PCS, self.PTC = V + 2048, V + 3072, V + 3584, place
                    place += T
                else:
                    self.BIAS = place
                    place += 0 if self.mla else 2 * (T if self.causal else STRIP)
                    self.MASK = place
                    place += GRID_W if self.name == "na" else 0
                    if self.name == "na":
                        self.LOWV = place
                        place += T
                assert place <= ARENA, (n, place)
                first = 3 if self.causal else 4
                slots = [(u, c * T) for u in (u_hi, u_lo) for c in range(first, KC)] + [(spare_r, 0), (spare_r, T)]

                def take(count):
                    return [slots.pop(0) for _ in range(count)]
                if self.diff or self.mla:
                    self.QH, self.QL, self.KH, self.KL = take(2), take(2), take(2), take(2)
                    self.VH = take(2)
                    self.VL = take(2) if self.diff else None
                else:
                    self.QS = take(2)
                    self.KH = take(4 if self.nsa else 2)
                    self.KL = take(2 if self.nsa else 1)
                    self.VH = take(4 if self.nsa else 2)

            def rows(self, head):
                return 64 * head, 64 * head + 64

            def rope_rows(self, head):
                return ((64, 96), (0, 32))[head]

            def score_products(self, m, qt, n):
                head = m // self.per_head
                q = slice(qt * P, qt * P + P)
                if self.diff or self.mla:
                    lo, hi = self.rows(m % 2) if self.diff else ((0, 96), (0, P))[head]
                    pairs = ((self.QL, self.KH), (self.QH, self.KL), (self.QH, self.KH))
                    return [(slot(a[head], q, lo, hi), slot(b[head], slice(0, n), lo, hi)) for a, b in pairs]
                lo, hi = self.rows(head)
                if self.nsa:
                    kh, kl = self.KH[2 * (m % 2) + head], self.KL[m % 2]
                else:
                    kh, kl = self.KH[head], self.KL[0]
                return [(slot(self.QS[head], q, lo, hi), slot(kl, slice(0, n), lo, hi)),
                        (slot(self.QS[head], q), slot(kh, slice(0, n)))]

            def value_products(self, t, kt, turned_cols):
                kind, head, m = self.turns[t]
                high, low = u_hi[:, turned_cols], u_lo[:, turned_cols]
                k = slice(kt * P, kt * P + P)
                if self.diff:
                    vh, vl = slot(self.VH[head], k), slot(self.VL[head], k)
                    return [(vl, high), (vh, low), (vh, high)]
                v = slot(self.VH[2 * (m % 2) + head if self.nsa else head], k)
                return [(v, low), (v, high)]

            def bias_of(self, m, qt):
                n = self.length(qt)
                if self.mla:
                    return zero[:, 0:1].to_broadcast([P, n])
                if self.name == "na":
                    return at(self.BIAS + m * STRIP + (6 - 2 * qt) * GRID_W, n)
                b = m % 2 if self.diff else m // 2
                return at(self.BIAS + b * T + T - n, n)

            def p_tile(self, m, qt):
                return at(self.P0 + (m % self.bufs) * self.p_size() + self.p_at(qt), self.length(qt))

            def turned_cols(self, kt):
                return slice(self.pt_at(kt), self.pt_at(kt) + T - self.first_q(kt) * P)

            def diag_tile(self, m, qt):
                b = (m // 2 if self.diff else m) % 2
                return self.diag[:, (b * NT + qt) * P:(b * NT + qt + 1) * P]

            def stat(self, buf, m, qt=None):
                b = m % self.bufs
                return buf[:, b * NT:(b + 1) * NT] if qt is None else buf[:, b * NT + qt:b * NT + qt + 1]

            def each_pass(self, eng, base, body):
                n = self.passes
                body(base, 2, True)
                with repeat(eng, 1, n - 2) as i:
                    body(i + base, 2)
                body(base + n - 2, 1)
                body(base + n - 1, 0)

            def turned_bank(self, n):
                return 2 + n % self.pt_banks

        def slot(place, cols=slice(0, T), lo=0, hi=P):
            buf, c = place
            return buf[lo:hi, c + cols.start:c + cols.stop]

        def by_tile(place, lo, width):
            return slot(place).rearrange("p (t c) -> p t c", t=NT)[:, :, lo:lo + width]

        def values_of(row, col, width):
            v = arena[:, V:V + NT * row].rearrange("p (t c) -> p t c", t=NT)
            return v[:, :, bass.ds(col, width)] if not isinstance(col, int) else v[:, :, col:col + width]

        def place_of(att, I, left, m):
            if m < att.maps:
                return I, m
            return (I + 1, m - att.maps) if left else None

        def tile_at(att, I, left, n):
            if n < att.uses:
                return I, n
            return (I + 1, n - att.uses) if left else None

        def next_v(att, I, left, a):
            if a == 0:
                return I, 1
            return (I + 1, 0) if left else None

        def next_qk(att, I, left, a):
            if att.nsa:
                return (I + 1, a) if left else None
            if a == 0:
                return (I + 1, 1) if left else None
            return (I + 2, 0) if left == 2 else None

        def head_before(I, first, a):
            if a == 1:
                return I, 0
            return None if first else (I - 1, 1)

        def qk_parts(att, I, a):
            lo, hi = att.rows(a)
            other = (64 - lo, 128 - lo)
            if att.diff:
                return [(slot(att.QH[a]), slot(att.QL[a]), at(QT + (2 * I + a) * T)),
                        (slot(att.KH[a]), slot(att.KL[a]), at(KT + (2 * I + a) * T))]
            every = slice(0, T)
            if att.mla:
                rope = att.rope_rows(a)
                return [(slot(att.QH[a], every, lo, hi), slot(att.QL[a], every, lo, hi), at(QT + I * T, T, lo, hi)),
                        (slot(att.KH[a], every, lo, hi), slot(att.KL[a], every, lo, hi), at(KT + I * T, T, lo, hi)),
                        (slot(att.QH[a], every, *rope), slot(att.QL[a], every, *rope), at(TAIL + I * T, T, *rope))]
            out = [(slot(att.QS[a], every, lo, hi), slot(att.QS[a], every, *other), at(QT + I * T, T, lo, hi))]
            if att.name == "na":
                k = at(KT + I * T, T, lo, hi)
                out.append((slot(att.KH[a], every, lo, hi), slot(att.KL[0], every, lo, hi), k))
                out.append((slot(att.KH[a], every, *other), None, k))
            return out

        def v_parts(att, I, a):
            if att.diff:
                return (slot(att.VH[a]).rearrange("p (t c) -> p t c", t=NT),
                        slot(att.VL[a]).rearrange("p (t c) -> p t c", t=NT), values_of(D, (2 * I + a) * P, P))
            return by_tile(att.VH[a], 0, 64), by_tile(att.VH[a], 64, 64), values_of(D, (2 * I + a) * 64, 64)

        def fixed_k_parts(att, g):
            every, out = slice(0, T), []
            for a in range(2):
                lo, hi = att.rows(a)
                if att.nsa:
                    for branch in range(2):
                        k = at(KT + ((6, 4)[branch] + g) * T, T, lo, hi)
                        kh = att.KH[2 * branch + a]
                        out.append((slot(kh, every, lo, hi), slot(att.KL[branch], every, lo, hi), k))
                        out.append((slot(kh, every, 64 - lo, 128 - lo), None, k))
                else:
                    rope = att.rope_rows(a)
                    out.append((slot(att.KH[a], every, *rope), slot(att.KL[a], every, *rope), at(att.KR, T, *rope)))
            if att.mla:
                nothing = zero[32:64, 0:1].to_broadcast([32, T])
                out += [(slot(x_[1], every, 32, 64), None, nothing) for x_ in (att.KH, att.KL, att.QH, att.QL)]
            return out

        def fixed_v_parts(att, g):
            return [(by_tile(att.VH[2 * branch + a], 0, 64), by_tile(att.VH[2 * branch + a], 64, 64),
                     values_of(T, (256, 0)[branch] + (2 * g + a) * 64, 64)) for branch in range(2) for a in range(2)]

        def attend_tensor(pe, att, g=0, first=True):
            base = g * att.passes
            if first:
                pe.sem_inc(att.pt_ready, att.credit)
                pe.sem_inc(att.pv_done, att.credit)

            def score(I, m, qt):
                if qt == 0:
                    pe.wait_ge(att.q_staged, 2 * I + m // att.per_head + 1)
                n = max(att.length(qt), 256)
                pe.wait_ge(att.s_free, 4 * (att.maps * I + m) + qt + 1)
                pairs = att.score_products(m, qt, n)
                for nth, (lhs, rhs) in enumerate(pairs):
                    mm = nc.tensor.matmul(bank(qt % 2, n), lhs, rhs, start=(nth == 0), stop=(nth == len(pairs) - 1))
                mm.then_inc(att.s_ready, 1)

            def turn_tile(I, n):
                t, kt = att.tiles[n]
                kind, head, m = att.turns[t]
                if kind == "cmp":
                    pe.wait_ge(att.v_staged, 2 * I + head + 1)
                pe.wait_ge(att.pt_free, att.uses * I + n + 1)
                b = att.turned_bank(n)
                if kind == "cmp":
                    for qt in range(NT):
                        tr = nc.tensor.transpose(psum[0:CMP, b, qt * P:(qt + 1) * P],
                                                 at(att.PCS + head * NT * CMP + qt * CMP, CMP), ident[:])
                else:
                    q0 = att.first_q(kt)
                    for qt in range(q0, NT):
                        if kt == 0:
                            pe.wait_ge(att.p_ready, 4 * (2 * I + head if att.diff else att.maps * I + m) + qt + 1)
                        tr = nc.tensor.matmul(psum[:, b, (qt - q0) * P:(qt - q0 + 1) * P],
                                              att.p_tile(m, qt)[:, kt * P:(kt + 1) * P], att.diag_tile(m, qt),
                                              start=True, stop=True)
                tr.then_inc(att.pt_ready, 1)

            def value_tile(I, n):
                t, kt = att.tiles[n]
                kind, head, m = att.turns[t]
                starts = n == 0 or att.turns[att.tiles[n - 1][0]][1] != head
                ends = n + 1 == att.uses or att.turns[att.tiles[n + 1][0]][1] != head
                if starts:
                    pe.wait_ge(att.o_free, 2 * I + head + 1)
                    pe.wait_ge(att.v_staged, 2 * I + head + 1)
                pe.wait_ge(att.pt_free, att.uses * I + n + 1 + att.pt_banks)
                if kind == "cmp":
                    pairs = [(at(N_VC + (2 * g + head) * P, P, 0, CMP), at(att.PTC, T, 0, CMP))]
                    q0 = 0
                else:
                    q0 = att.first_q(kt)
                    pairs = att.value_products(t, kt, att.turned_cols(kt))
                for nth, (lhs, rhs) in enumerate(pairs):
                    mm = nc.tensor.matmul(psum[:, 6 + head, q0 * P:T], lhs, rhs, start=(starts and nth == 0),
                                          stop=(ends and nth == len(pairs) - 1))
                mm.then_inc(att.pv_done, 1)

            if att.nsa or att.mla:
                pe.wait_ge(att.fixed_k, g + 1)
            if att.nsa:
                pe.wait_ge(att.fixed_v, g + 1)
            for m in range(att.ahead):
                for qt in range(NT):
                    score(base, m, qt)
            for n in range(LOOK):
                turn_tile(base, n)

            def body(I, left, first=False):
                for n in range(att.uses):
                    ahead = tile_at(att, I, left, n + LOOK)
                    if ahead and not att.scores_first:
                        turn_tile(*ahead)
                    for m, qt in att.scores_beside(n):
                        where = place_of(att, I, left, m)
                        if where:
                            score(*where, qt)
                    if ahead and att.scores_first:
                        turn_tile(*ahead)
                    value_tile(I, n)
            att.each_pass(pe, base, body)

        def attend_vector(dve, att, g=0, first=True):
            base = g * att.passes
            if first:
                dve.sem_inc(att.s_free, 2)
                dve.sem_inc(att.o_free, 2)
                dve.sem_inc(att.pt_free, att.pt_banks)

            def score(I, m, qt):
                M = att.maps * I + m
                if qt == 0:
                    if att.nsa:
                        dve.wait_ge(att.bias_in[m // 2], 16 * (I + 1))
                    elif att.diff:
                        dve.wait_ge(att.bias_in[m % 2], 16 * (2 * I + m // 2 + 1))
                    elif att.name == "na":
                        dve.wait_ge(att.masked, M + 1)
                    dve.wait_ge(att.pt_ready, att.uses * I + (att.released(m) + 1 + att.credit))
                dve.wait_ge(att.s_ready, 4 * M + qt + 1)
                hold(dve)
                nc.vector.tensor_tensor_reduce(
                    out=att.p_tile(m, qt), in0=bank(qt % 2, att.length(qt)), in1=att.bias_of(m, qt), scale=-1.0,
                    scalar=BIG, op0=ALU.add, op1=ALU.min, accum_out=att.stat(neg_max, m, qt))\
                    .then_inc(att.s_free, 1)

            def low_parts(triples):
                for high, low, src in triples:
                    if low is not None:
                        ins = nc.vector.tensor_tensor(low, src, high.bitcast(F32), ALU.subtract)
                return ins

            def stage_qk(I, a):
                dve.wait_ge(att.qk_high, 2 * I + a + 1)
                low_parts(qk_parts(att, I, a)).then_inc(att.q_staged, 1)

            def stage_compressed(I, a):
                n = NT * CMP
                row = (2 * g + a) * 4 - base + I
                before = next(att.use[t] for t, (kind, h, _) in enumerate(att.turns) if kind == "cmp" and h == a)
                dve.wait_ge(att.pt_ready, att.uses * I + (before - att.uses + 1 + att.credit))
                nc.vector.tensor_scalar(at(att.PCS + a * n, n), at(N_PC + n * row, n), 1.0, None, ALU.mult)\
                    .then_inc(att.v_staged, 1)

            def counted(ins):
                ins.then_inc(att.vec, 1)

            def own_count(M, step, steps):
                dve.wait_ge(att.vec, steps * M + step)

            def make_ready(I, m):
                M = att.maps * I + m
                r = att.stat(inv, m)
                dve.wait_ge(att.exp_done, 4 * M + (8 if att.diff else 4))
                counted(nc.vector.reciprocal(r, att.stat(row_sum, m)))
                if att.diff:
                    head = 2 * I + m // 2
                    c = att.stat(inv, m + 1)
                    counted(nc.vector.reciprocal(c, att.stat(row_sum, m + 1)))
                    own_count(head, 2, 3)
                    counted(nc.vector.scalar_tensor_tensor(out=c, in0=c, scalar=neg_lam[:, 0:1],
                                                           in1=att.stat(row_sum, m), op0=ALU.mult, op1=ALU.mult))
                    own_count(head, 3, 3)
                elif att.nsa:
                    own_count(M, 1, 2)
                    head, branch = m // 2, 2 - m % 2
                    col = ((2 * g + head) * 4 - base) * 3 + branch + 3 * I
                    gates = gate[:].rearrange("p (t c) -> p t c", t=NT)
                    gates = gates[:, :, bass.ds(col, 1)] if not isinstance(col, int) else gates[:, :, col:col + 1]
                    r3 = r.rearrange("p (t o) -> p t o", o=1)
                    counted(nc.vector.tensor_tensor(r3, r3, gates, ALU.mult))
                    own_count(M, 2, 2)
                else:
                    own_count(M, 1, 1)
                dve.wait_ge(att.pt_ready, att.uses * I + (att.turned_by(m - att.maps_per_turn * 2) + 1 + att.credit))
                hold(dve)
                for qt in range(NT):
                    nc.vector.tensor_scalar(att.diag_tile(m, qt), ident[:], att.stat(inv, m, qt), None, ALU.mult)\
                        .then_inc(att.diag_done if att.diff else att.p_ready, 1)
                if att.diff:
                    for qt in range(NT):
                        nc.vector.scalar_tensor_tensor(
                            out=att.p_tile(m, qt), in0=att.p_tile(m + 1, qt), scalar=att.stat(inv, m + 1, qt),
                            in1=att.p_tile(m, qt), op0=ALU.mult, op1=ALU.add).then_inc(att.p_ready, 1)

            def take_turned(I, n):
                t, kt = att.tiles[n]
                kind = att.turns[t][0]
                b = att.turned_bank(n)
                if kind == "cmp":
                    dve.wait_ge(att.pt_ready, att.uses * I + att.use[t] + 1 + att.credit)
                    dve.wait_ge(att.pv_done, att.uses * I + (att.use[t] - att.uses // 2 + 1 + att.credit))
                    ins = nc.vector.tensor_scalar(at(att.PTC, T, 0, CMP), psum[0:CMP, b, :], 1.0, None, ALU.mult)
                else:
                    dve.wait_ge(att.pt_high, att.high_index(len(att.turns)) * I + att.high_index(t) + kt + 1)
                    cols = att.turned_cols(kt)
                    ins = nc.vector.tensor_tensor(u_lo[:, cols], bank(b, cols.stop - cols.start),
                                                  u_hi[:, cols].bitcast(F32), ALU.subtract)
                ins.then_inc(att.pt_free, 1)

            def take_head(I, head):
                dve.wait_ge(att.pv_done, att.uses * I + (att.last_use(head) + 1 + att.credit))
                o = psum[:, 6 + head, :]
                if att.diff:
                    ins = nc.vector.tensor_scalar(at(QT + (2 * I + head) * T), o, 1.0, None, ALU.mult)
                else:
                    z, part = at(Z + I * T, T, *att.rows(head)), at(att.LOWV, T, *att.rows(head))
                    dve.wait_ge(att.low_out, 2 * I + head + 1)
                    nc.vector.tensor_tensor(part, o[0:64], part, ALU.add).then_inc(att.summed, 1)
                    dve.wait_ge(att.summed, 2 * I + head + 1)
                    ins = nc.vector.tensor_tensor(z, part, z, ALU.mult)
                ins.then_inc(att.o_free, 1)

            def body(I, left, first=False):
                for n, (t, kt) in enumerate(att.tiles):
                    kind, a, m = att.turns[t]
                    for mm, qt in att.scores_beside(n):
                        where = place_of(att, I, left, mm)
                        if where:
                            score(*where, qt)
                    where = kt == 0 and kind != "cmp" and place_of(att, I, left, m + att.maps_per_turn)
                    if where:
                        make_ready(*where)
                    where = tile_at(att, I, left, n + LOOK)
                    if where:
                        take_turned(*where)
                    if kind == "cmp":
                        continue
                    if kt == 3 and att.first_turn(t) and next_qk(att, I, left, a):
                        stage_qk(*next_qk(att, I, left, a))
                    if kt == 2 and att.first_turn(t) and head_before(I, first, a):
                        take_head(*head_before(I, first, a))
                    if kt == 2 and att.first_turn(t) and att.nsa and next_v(att, I, left, a):
                        stage_compressed(*next_v(att, I, left, a))

            if att.nsa or att.mla:
                dve.wait_ge(att.fixed_high, g + 1)
                low_parts(fixed_k_parts(att, g)).then_inc(att.fixed_k, 1)
            stage_qk(base, 0)
            stage_qk(base, 1)
            if att.nsa:
                stage_compressed(base, 0)
            for m in range(att.ahead):
                for qt in range(NT):
                    score(base, m, qt)
            if not att.nsa:
                stage_qk(base + 1, 0)
            make_ready(base, 0)
            for n in range(LOOK):
                take_turned(base, n)
            att.each_pass(dve, base, body)
            take_head(base + att.passes - 1, 1)

        def attend_scalar(act, att, g=0):
            base = g * att.passes

            def load_bias(I, m):
                if att.name == "na":
                    for r2 in range(2):
                        first_at = RPB_PAD + 15 + (1 - r2) * RPB_ROW + m * RPB_HEAD + 2 * RPB_HEAD * I
                        act.dma_start(
                            arena[r2 * 64:r2 * 64 + 64, att.BIAS + m * STRIP:att.BIAS + (m + 1) * STRIP]
                            .rearrange("p (j c) -> p j c", c=GRID_W),
                            bass.AP(rpb_rows.tensor, first_at, [[RPB_LEN - 1, 64], [RPB_ROW, 14], [1, GRID_W]]))\
                            .then_inc(att.bias_in[m], 16)
                    return
                if att.diff:
                    b, row = m % 2, 4 * I + m
                else:
                    b, row = m // 2, (2 * g + m // 2) * 4 - base + I
                act.dma_start(at(att.BIAS + b * T), bass.AP(bias_rows.tensor, P - 1 + SPAN * row,
                                                            [[HEADS * SPAN - 1, P], [1, T]]))\
                    .then_inc(att.bias_in[b], 16)

            def score(I, m, qt):
                act.wait_ge(att.s_free, 4 * (att.maps * I + m) + qt + 3)
                nc.scalar.activation(att.p_tile(m, qt), att.p_tile(m, qt), ACT.Exp, scale=-1.0,
                                     bias=att.stat(neg_max, m, qt), accum_out=att.stat(row_sum, m, qt))\
                    .then_inc(att.exp_done, 1)

            def high_parts(triples):
                for high, _, src in triples:
                    ins = nc.scalar.activation(high, src, ACT.Copy)
                return ins

            def stage_v(I, a):
                act.wait_ge(att.pv_done, att.uses * I + (att.last_use(a) - att.uses + 1 + att.credit))
                high_parts([v_parts(att, I, a)]).then_inc(att.v_high, 1)

            def take_turned(I, n):
                t, kt = att.tiles[n]
                if att.turns[t][0] == "cmp":
                    return
                act.wait_ge(att.pt_ready, att.uses * I + (n + 1 + att.credit))
                full = [u for (k, _, _), u in zip(att.turns, att.use) if k == "full"]
                nth = full.index(att.use[t])
                before = full[nth - 1] - (att.uses if nth == 0 else 0)
                act.wait_ge(att.pv_done, att.uses * I + (before + kt + 1 + att.credit))
                cols = att.turned_cols(kt)
                nc.scalar.activation(u_hi[:, cols], bank(att.turned_bank(n), cols.stop - cols.start), ACT.Copy)\
                    .then_inc(att.pt_high, 1)

            def copy_low_out(I, head):
                act.wait_ge(att.pv_done, att.uses * I + (att.last_use(head) + 1 + att.credit))
                act.wait_ge(att.o_free, 2 * I + head + 1)
                nc.scalar.activation(at(att.LOWV, T, *att.rows(head)), psum[64:P, 6 + head, :], ACT.Copy)\
                    .then_inc(att.low_out, 1)

            def next_bias(I, left, a):
                if att.name == "na":
                    if left == 2:
                        load_bias(I + 2, a)
                elif not att.mla:
                    maps = (0, 1) if att.diff else (0,)
                    if a == 0 and (att.nsa or left):
                        if left:
                            for b in maps:
                                load_bias(I + 1, 2 + b)
                    elif a == 1 and left == 2:
                        for b in maps:
                            load_bias(I + 2, b)

            def body(I, left, first=False):
                for n, (t, kt) in enumerate(att.tiles):
                    kind, a, m = att.turns[t]
                    where = tile_at(att, I, left, n + LOOK)
                    if where:
                        take_turned(*where)
                    for mm, qt in att.scores_beside(n):
                        where = place_of(att, I, left, mm)
                        if where:
                            score(*where, qt)
                    if kind == "cmp":
                        continue
                    if kt == att.qk_at and att.first_turn(t) and next_qk(att, I, left, a):
                        high_parts(qk_parts(att, *next_qk(att, I, left, a))).then_inc(att.qk_high, 1)
                    if kt == att.low_out_at and att.first_turn(t) and head_before(I, first, a) and not att.diff:
                        copy_low_out(*head_before(I, first, a))
                    if kt == 1 and not att.nsa and next_v(att, I, left, a):
                        stage_v(*next_v(att, I, left, a))
                    if n + 1 == att.head_end(a):
                        next_bias(I, left, a)

            if att.nsa:
                load_bias(base, 0)
                load_bias(base, 2)
            elif not att.mla:
                load_bias(base, 0)
                load_bias(base, 1)
            if att.nsa or att.mla:
                if g:
                    act.wait_ge(att.pv_done, att.uses * base + att.credit)
                high_parts(fixed_k_parts(att, g) + (fixed_v_parts(att, g) if att.nsa else [])).then_inc(att.fixed_high, 1)
            for a in range(2):
                high_parts(qk_parts(att, base, a)).then_inc(att.qk_high, 1)
            if not att.nsa:
                stage_v(base, 0)
            for m in range(att.ahead):
                for qt in range(NT):
                    score(base, m, qt)
                if att.name == "na":
                    load_bias(base + 1, m)
                elif att.nsa and m == 1:
                    load_bias(base + 1, 0)
                elif att.diff:
                    load_bias(base + m // 2, (m + 2) % 4)
            if not att.nsa:
                high_parts(qk_parts(att, base + 1, 0)).then_inc(att.qk_high, 1)
            for n in range(LOOK):
                take_turned(base, n)
            att.each_pass(act, base, body)
            if not att.diff:
                copy_low_out(base + att.passes - 1, 1)

        def attend_pool(pool, att, g=0):
            def low_values(I, a):
                high, low, src = v_parts(att, I, a)
                pool.wait_ge(att.v_high, 2 * I + a + 1)
                hold(pool)
                nc.gpsimd.tensor_tensor(low, src, high.bitcast(F32), ALU.subtract).then_inc(att.v_staged, 1)

            def mask_strip(I, m):
                if att.name != "na":
                    return
                pool.wait_ge(att.bias_in[m], 32 * (I + 1))
                hold(pool)
                strip = at(att.BIAS + m * STRIP, STRIP).rearrange("p (j c) -> p j c", c=GRID_W)
                mask = at(att.MASK, GRID_W).unsqueeze(1).to_broadcast([P, STRIP // GRID_W, GRID_W])
                nc.gpsimd.tensor_tensor(strip, strip, mask, ALU.add).then_inc(att.masked, 1)

            if att.nsa:
                pool.wait_ge(att.fixed_high, g + 1)
                for high, low, src in fixed_v_parts(att, g):
                    ins = nc.gpsimd.tensor_tensor(low, src, high.bitcast(F32), ALU.subtract)
                ins.then_inc(att.fixed_v, 1)
                return
            mask_strip(0, 0)
            mask_strip(0, 1)
            low_values(0, 0)

            def body(I, left, first=False):
                for a in range(2):
                    if left:
                        mask_strip(I + 1, a)
                    if next_v(att, I, left, a):
                        low_values(*next_v(att, I, left, a))
            att.each_pass(pool, 0, body)

        nsa = Stage("nsa", passes=4, per_head=2, causal=True, ahead=2, bufs=4, cmp=True, low_out_at=0)
        diff = Stage("diff", passes=4, per_head=2, causal=True, ahead=4, bufs=4, scores_first=False)
        na = Stage("na", passes=8, per_head=1, causal=False, ahead=2, bufs=2, qk_at=2, low_out_at=0)
        mla = Stage("mla", passes=8, per_head=1, causal=False, ahead=2, bufs=2)

        pe_k, pe_v = at(N_CB - 64, 32), at(N_CB - 32, 32)
        w2_k, w2_v = at(N_CB - 256, P), at(N_CB - 128, 64)
        ONEHOT, TABLE, ROWMASK, ROWS, LAMBDAS = Z, Z + SPAN, Z + SPAN + HEADS, Z + 2 * SPAN + HEADS, Z + 3 * SPAN + HEADS
        lam_sum, lam_exp, rpb_out = sem("lam_sum"), sem("lam_exp"), sem("rpb_out")
        consts = [(at(ONEHOT, 2 * SPAN + HEADS, 0, BUCKETS), "bias"), (ident[:], "ident"), (subln[:], "subln"),
                  (at(N_CB - 256, 256), "compress")]

        def setup_scalar(act):
            for nth, (dst, name) in enumerate(consts):
                act.dma_start(dst, A[name]).then_inc(const_in, 16)
                if nth == 1:
                    load_gain(act, 0)
            act.dma_start(at(LAMBDAS, 256), bass.AP(A["lambdas"].tensor, 0, [[0, P], [1, 256]])).then_inc(const_in, 16)
            act.dma_start(rpb_rows, bass.AP(A["rpb"].tensor, 0, [[0, GRID_W], [1, RPB_LEN]])).then_inc(rpb_out, 16)

        def setup_rows_scalar(act):
            act.wait_ge(lam_sum, 2)
            nc.scalar.activation(neg_lam[:, 2:4], neg_lam[:, 0:2], ACT.Exp).then_inc(lam_exp, 1)
            act.wait_ge(rows_made, 3)
            act.dma_start(bass.AP(bias_rows.tensor, 0, [[SPAN, HEADS], [HEADS * SPAN, P], [1, SPAN]]),
                          at(ROWS, SPAN, 0, HEADS).unsqueeze(1).to_broadcast([HEADS, P, SPAN])).then_inc(rows_out, 16)

        def setup_high(act):
            for b in range(2):
                act.wait_ge(w_loaded[b], 16)
                nc.scalar.activation(w_hi[b][:], stage[b][:], ACT.Copy).then_inc(w_high, 1)

        def setup_pool(pool):
            for b in range(2):
                split_low(pool, b, b)

        def setup_tensor(pe):
            pe.wait_ge(const_in, 16 * (len(consts) + 1))
            for b in range(2):
                mm = nc.tensor.matmul(psum[0:HEADS, b, :], at(TABLE, HEADS, 0, BUCKETS),
                                      at(ONEHOT + b * 512, 512, 0, BUCKETS), start=True, stop=True)
            mm.then_inc(rows_made, 1)

        def setup_vector(dve):
            dve.sem_inc(bank_free["dve"], 4)
            dve.sem_inc(bank_free["act"], 4)
            nc.vector.memset(zero[:], 0.0)
            done("dve", nc.vector.memset(half_exp[:], -0.5))

        def setup_rows_vector(dve):
            dve.wait_ge(const_in, 16 * (len(consts) + 1))
            for k in range(2):
                nc.vector.tensor_tensor_reduce(
                    out=at(ROWS + k * 64, 64), in0=at(LAMBDAS + 128 * k, 64), in1=at(LAMBDAS + 128 * k + 64, 64),
                    scale=1.0, scalar=0.0, op0=ALU.mult, op1=ALU.add, accum_out=neg_lam[:, k:k + 1]).then_inc(lam_sum, 1)
            done("dve", nc.vector.tensor_scalar(subln[:], subln[:], 1.0 - LAMBDA_INIT, None, ALU.mult))
            dve.wait_ge(lam_exp, 1)
            done("dve", nc.vector.tensor_tensor(neg_lam[:, 0:1], neg_lam[:, 3:4], neg_lam[:, 2:3], ALU.subtract))
            settle("dve", dve)
            done("dve", nc.vector.tensor_scalar(neg_lam[:, 0:1], neg_lam[:, 0:1], -LAMBDA_INIT, None, ALU.add))
            dve.wait_ge(rows_made, 1)
            for b in range(2):
                nc.vector.tensor_tensor(at(ROWS + b * 512, 512, 0, HEADS), psum[0:HEADS, b, :],
                                        at(ROWMASK + b * 512, 512, 0, HEADS), ALU.add).then_inc(rows_made, 1)
        def load_strips(act, r):
            if r == 0:
                act.wait_ge(rows_out, 16)
            if r >= 2:
                act.wait_ge(strip_used, 4 * (r - 1))
            act.dma_start(at((Z, TAIL)[r % 2], 4 * STRIP).rearrange("p (h j) -> p h j", h=4),
                          bass.AP(bias_rows.tensor, P - 1 + 4 * SPAN * r,
                                  [[HEADS * SPAN - 1, P], [SPAN, 4], [1, STRIP]])).then_inc(strip_in[r % 2], 16)

        def cut_strips(dve, r):
            dve.wait_ge(strip_in[r % 2], 16 * (r // 2 + 1))
            strips = at((Z, TAIL)[r % 2], 4 * STRIP).rearrange("p (h j) -> p h j", h=4)
            for qt in range(NT):
                j = 415 - P * qt
                dst = at(N_CB + 4 * r * NT * CMP, 4 * NT * CMP).rearrange("p (h t c) -> p h t c", h=4, t=NT)
                nc.vector.tensor_copy(dst[:, :, qt, :], strips[:, :, j:j + 16 * (CMP - 1) + 1:16]).then_inc(strip_used, 1)

        X, HID = N_PC, N_PC + 32 * 4 * CMP
        MX, LSUM = HID + 8 * CMP, HID + 8 * CMP + 64
        assert LSUM + 64 <= N_CB - 256
        cmp_sum = sem("cmp_sum")
        cmp_x, cmp_hi, cmp_lo = sem("cmp_x"), sem("cmp_hi"), sem("cmp_lo")
        cmp_kv, cmp_kv_taken, cmp_s = sem("cmp_kv"), sem("cmp_kv_taken"), sem("cmp_s")
        cmp_shifted, cmp_exp = sem("cmp_shifted"), sem("cmp_exp")
        XQ, PART, WIDE = 32 * 4 * CMP // 4, 4 * CMP, 256

        def x_part(q, low):
            u = (u_hi, u_lo)[q // 2][:, 8 * (q % 2) * 2 * PART:8 * (q % 2 + 1) * 2 * PART]
            return u.rearrange("p (o b c) -> p o b c", o=8, b=2)[:, :, low, :]

        def x_quarter(q):
            return at(X + q * XQ, XQ).rearrange("p (o c) -> p o c", o=8)


        def compress_vector(dve):
            n = 0
            for side, pos in ((0, pe_k), (1, pe_v)):
                for half in range(2):
                    for gp in range(2):
                        src = at(KT + (2 * side + gp) * T, T, 64 * half, 64 * half + 64)
                        src = bass.AP(src.tensor, src.offset, [src.ap[0], [1, 32], [16, CMP]])
                        dst = at(X, 32 * 4 * CMP, 64 * side, 64 * side + 64).rearrange("p (o q c) -> p o q c", o=32, q=4)
                        nc.vector.tensor_tensor(
                            dst[:, :, 2 * half + gp, :], src,
                            pos[64 * half:64 * half + 64, :].unsqueeze(2).to_broadcast([64, 32, CMP]),
                            ALU.add).then_inc(cmp_x, 1)
            for q in range(4):
                dve.wait_ge(cmp_hi, q + 1)
                nc.vector.tensor_tensor(x_part(q, 1), x_quarter(q), x_part(q, 0).bitcast(F32), ALU.subtract)\
                    .then_inc(cmp_lo, 1)
            dve.wait_ge(bank_done, 4 * RUNS["nsa_cmp"]["block"] + 4)
            for side in range(2):
                done("dve", nc.vector.tensor_copy(at(HID + side * PART, PART), bank(side)[:, PART:2 * PART]))
            settle("dve", dve)
            for side in range(2):
                ins = nc.vector.tensor_tensor(at(HID + side * PART, PART), bank(side, PART), at(HID + side * PART, PART), ALU.add)
            ins.then_inc(cmp_sum, 1)
            dve.wait_ge(cmp_kv, 1)
            for half in range(2):
                nc.vector.tensor_copy(at(N_CK, 2 * CMP, 64 * half, 64 * half + 64),
                                      psum[64 * half:64 * half + 64, 2, 2 * CMP * half:2 * CMP * (half + 1)])\
                    .then_inc(cmp_kv_taken, 1)
            vc = at(N_VC, 4 * P, 0, CMP).rearrange("p (g c) -> p g c", g=4)
            nc.vector.memset(vc[:, :, 64:P], 0.0)
            nc.vector.tensor_copy(vc[:, :, 0:64], psum[0:CMP, 3, 0:256].rearrange("p (g c) -> p g c", g=4))\
                .then_inc(cmp_kv_taken, 1)
            n = 4 * NT * CMP
            for g in range(4):
                dve.wait_ge(cmp_s, g + 1)
                done("dve", nc.vector.tensor_tensor(at(N_PC + g * n, n), bank(4 + g, n), at(N_CB + g * n, n), ALU.add))
            settle("dve", dve)
            pc = at(N_PC, HEADS * NT * CMP).rearrange("p (h c) -> p h c", c=CMP)

            def spread(off):
                return at(off, 64).unsqueeze(2).to_broadcast([P, 64, CMP])
            done("dve", nc.vector.tensor_reduce(at(MX, 64), pc, AX, ALU.max))
            settle("dve", dve)
            nc.vector.tensor_tensor(pc, pc, spread(MX), ALU.subtract).then_inc(cmp_shifted, 1)
            dve.wait_ge(cmp_exp, 1)
            done("dve", nc.vector.tensor_reduce(at(LSUM, 64), pc, AX, ALU.add))
            settle("dve", dve)
            done("dve", nc.vector.reciprocal(at(LSUM, 64), at(LSUM, 64)))
            settle("dve", dve)
            r = at(LSUM, 64).rearrange("p (h t) -> p h t", t=NT)
            g0 = gate[:].rearrange("p (t h b) -> p h t b", t=NT, b=3)[:, :, :, 0]
            done("dve", nc.vector.tensor_tensor(r, r, g0, ALU.mult))
            settle("dve", dve)
            done("dve", nc.vector.memset(r[0:CMP, :, 0:1], 0.0))
            settle("dve", dve)
            done("dve", nc.vector.tensor_tensor(pc, pc, spread(LSUM), ALU.mult))

        def compress_scalar(act):
            act.wait_ge(cmp_x, 8)
            for q in range(4):
                nc.scalar.activation(x_part(q, 0), x_quarter(q), ACT.Copy).then_inc(cmp_hi, 1)

            def hidden(i, j):
                act.wait_ge(cmp_sum, 1)
                return nc.scalar.activation(at(HID, 2 * PART), at(HID, 2 * PART), ACT.Silu)
            project_scalar(act, "nsa_cmp", hidden, banks=1)
            act.wait_ge(cmp_shifted, 1)
            pc = at(N_PC, HEADS * NT * CMP)
            nc.scalar.activation(pc, pc, ACT.Exp).then_inc(cmp_exp, 1)

        def compress_tensor(pe):
            run = RUNS["nsa_cmp"]
            n = 4 * CMP
            pe.wait_ge(cmp_lo, 4)
            wait_bank(pe, run, 0, 3)
            for a in range(2):
                b = (run["unit"] + a) % 2
                pe.wait_ge(w_ready, run["unit"] + a + 1)
                for o in range(16):
                    for side in range(2):
                        rows = slice(64 * side, 64 * side + 64)
                        for w in (w_lo, w_hi):
                            c = o * 2 * PART
                            mm = nc.tensor.matmul(
                                bank(side, WIDE), w[b][rows, o * P:(o + 1) * P], (u_hi, u_lo)[a][rows, c:c + WIDE],
                                start=(a == 0 and o == 0 and w is w_lo), stop=(a == 1 and o == 15 and w is w_hi))
                mm.then_inc(*((w_used, 1) if a == 0 else (bank_done, 4)))
            pe.wait_ge(bank_free["act"], run["taken"] + 8)
            nc.tensor.matmul(bank(2, n), w2_k, at(HID, n), start=True, stop=True)
            for half in range(2):
                for gp in range(2):
                    q = 2 * half + gp
                    mm = nc.tensor.matmul(psum[0:CMP, 3, (2 * gp + half) * 64:(2 * gp + half + 1) * 64],
                                          at(HID + n + q * CMP, CMP), w2_v, start=True, stop=True)
            mm.then_inc(cmp_kv, 1)
            pe.wait_ge(cmp_kv_taken, 3)
            for g in range(4):
                gp, half = g // 2, g % 2
                rows = (64 * half, 64 * half + 64)
                for j in range(4):
                    for qt in range(NT):
                        c = (j * NT + qt) * CMP
                        mm = nc.tensor.matmul(psum[:, 4 + g, c:c + CMP], at(QT + (4 * gp + j) * T + qt * P, P, *rows),
                                              at(N_CK + gp * CMP, CMP, *rows), start=True, stop=True)
                mm.then_inc(cmp_s, 1)

        SQ, ONES, RSTD, ROWS_R = TAIL, TAIL + DIFF_HEADS * T, TAIL + DIFF_HEADS * T + 1, TAIL + DIFF_HEADS * T + 64
        NR = DIFF_HEADS * NT
        sub_sq, sub_sum, sub_in, sub_pow, sub_ones = (sem(f"sub_{n}") for n in ("sq", "sum", "in", "pow", "ones"))
        sub_turned, sub_rows, sub_spread, sub_scaled, sub_out = \
            (sem(f"sub_{n}") for n in ("turned", "rows", "spread", "scaled", "out"))

        def subln_scalar(act):
            for u in range(DIFF_HEADS):
                nc.scalar.activation(at(SQ + u * T), at(QT + u * T), ACT.Square).then_inc(sub_sq, 1)

        def subln_tensor(pe):
            pe.wait_ge(sub_ones, 1)
            for u in range(DIFF_HEADS):
                pe.wait_ge(sub_sq, u + 1)
                for t in range(NT):
                    r = u * NT + t
                    mm = nc.tensor.matmul(psum[:, 0, r:r + 1], at(SQ + u * T + t * P, P), at(ONES, 1), start=True, stop=True)
            mm.then_inc(sub_sum, 1)
            pe.wait_ge(sub_pow, 1)
            nc.tensor.transpose(psum[0:NR, 1, 0:P], at(RSTD, NR), ident[:]).then_inc(sub_turned, 1)
            pe.wait_ge(sub_rows, 1)
            for u in range(DIFF_HEADS):
                for t in range(NT):
                    r = u * NT + t
                    mm = nc.tensor.matmul(bank(u)[:, t * P:(t + 1) * P], ident[0:NR, r:r + 1].to_broadcast([NR, P]),
                                          at(ROWS_R, P, 0, NR), start=True, stop=True)
                mm.then_inc(sub_spread, 1)

        def subln_vector(dve):
            nc.vector.memset(at(ONES, 1), 1.0 / P).then_inc(sub_ones, 1)
            dve.wait_ge(sub_sum, 1)
            nc.vector.tensor_scalar(at(RSTD, NR), psum[:, 0, 0:NR], EPS, None, ALU.add).then_inc(sub_in, 1)
            dve.wait_ge(sub_turned, 1)
            nc.vector.tensor_copy(at(ROWS_R, P, 0, NR), psum[0:NR, 1, 0:P]).then_inc(sub_rows, 1)
            for u in range(DIFF_HEADS):
                dve.wait_ge(sub_spread, u + 1)
                nc.vector.scalar_tensor_tensor(out=at(QT + u * T), in0=bank(u), scalar=subln[:, u:u + 1],
                                               in1=at(QT + u * T), op0=ALU.mult, op1=ALU.mult).then_inc(sub_scaled, 1)
                dve.wait_ge(sub_scaled, u + 1)
                nc.vector.tensor_tensor(at(Z + u * T), at(Z + u * T), at(QT + u * T), ALU.mult).then_inc(sub_out, 1)

        def subln_pool(pool):
            pool.wait_ge(sub_in, 1)
            nc.gpsimd.tensor_tensor(at(RSTD, NR), at(RSTD, NR), half_exp[:, 0:1].to_broadcast([P, NR]), ALU.pow)\
                .then_inc(sub_pow, 1)

        PP, PIN, E = 4096, V, Z
        p_in, p_turned, p_hi = sem("p_in"), sem("p_turned"), sem("p_hi")
        e_used, e_mul = sem("e_used"), sem("e_mul")

        def p_place(u, t):
            return u[:].rearrange("p (c t) -> p c t", c=KC)[:, 0:2, t * P:(t + 1) * P]

        def p_bank(t):
            return psum[:, t, 0:2 * P].rearrange("p (c t) -> p c t", c=2)

        def ple_tensor(pe, nth):
            pe.wait_ge(p_in, 16 * (nth + 1))
            for t in range(NT):
                for c in range(2):
                    tr = nc.tensor.transpose(psum[:, t, c * P:(c + 1) * P], at(PIN + t * PLE + c * P, P), ident[:])
                tr.then_inc(p_turned, 1)

        def ple_scalar(act, nth):
            act.dma_start(at(PIN, NT * PLE).rearrange("p (t c) -> p t c", t=NT),
                          A["p"][nth].rearrange("(t p) c -> p t c", p=P)).then_inc(p_in, 16)
            squares_scalar(act, (5, 8)[nth], x_tile, 0, D)
            for t in range(NT):
                act.wait_ge(p_turned, NT * nth + t + 1)
                nc.scalar.activation(p_place(u_hi, t), p_bank(t), ACT.Copy).then_inc(p_hi, 1)

        def ple_vector(dve, nth):
            for t in range(NT):
                dve.wait_ge(p_hi, NT * nth + t + 1)
                nc.vector.tensor_tensor(p_place(u_lo, t), p_bank(t), p_place(u_hi, t).bitcast(F32), ALU.subtract)

        def gate_scalar(act, nth):
            def take(i, j):
                act.wait_ge(e_used, 8 * nth + 4 * i + j + 1)
                return nc.scalar.activation(at(E + j * 512), bank(j), ACT.Sigmoid)
            project_scalar(act, f"ple{nth}_gate", take, ends=nth == 0)

        def gate_vector(dve, nth):
            if nth == 0:
                dve.sem_inc(e_used, 4)
            run = RUNS[f"ple{nth}_gate"]
            for i in blocks_of(dve, run):
                for j in range(4):
                    dve.wait_ge(bank_free["act"], run["taken"] + 4 * i + j + 5)
                    nc.vector.tensor_tensor(at(E + j * 512), at(E + j * 512), at(PP + j * D + i * 512), ALU.mult)\
                        .then_inc(e_mul, 1)
                    dve.wait_ge(e_mul, 8 * nth + 4 * i + j + 1)
                    dst = x[:, bass.ds(j * D + i * 512, 512)] if not isinstance(i, int) else \
                        x[:, j * D + i * 512:j * D + i * 512 + 512]
                    nc.vector.tensor_tensor(dst, dst, at(E + j * 512), ALU.add).then_inc(e_used, 1)

        CQ, LXN, ROPE_K, ROPE_Q = mla.P0, V, mla.P0 + NT * 640, mla.P0 + NT * 640 + T
        assert ROPE_Q + T <= ARENA
        rope_in = sem("rope_in")
        MLA_SCALE = (64 + ROPE) ** -0.5

        def rotate(dve, b, table, tmp, dst):
            done("dve", nc.vector.tensor_tensor(at(tmp, T, 64, 96), psum[64:96, b, :], at(table, T, 64, 96), ALU.mult))
            done("dve", nc.vector.tensor_tensor(at(tmp + T, T, 64, 96), psum[96:128, b, :], at(table, T, 96, 128), ALU.mult))
            settle("dve", dve)
            return nc.vector.tensor_tensor(dst, at(tmp, T, 64, 96), at(tmp + T, T, 64, 96), ALU.add)

        def load_rope(act):
            act.dma_start(at(ROPE_K, 2 * T), A["rope"]).then_inc(rope_in, 16)

        def rope_vector(dve):
            dve.wait_ge(rope_in, 16)
            def take(i, j):
                done("dve", rotate(dve, 0, ROPE_K, QT, at(mla.KR, T, 64, 96)))
                settle("dve", dve)
                return nc.vector.tensor_copy(at(mla.KR, T, 0, 32), at(mla.KR, T, 64, 96))
            project_vector(dve, "mla_rope", take, banks=1)

        def mla_q_vector(dve):
            def take(i, j):
                h = 4 * i + j
                u, half = h // 2, h % 2
                nc.vector.tensor_scalar(at(QT + u * T, T, 64 * half, 64 * half + 64), psum[0:64, j, :], MLA_SCALE, None, ALU.mult)
                return rotate(dve, j, ROPE_Q, CQ + 2 * T * (h % 2), at(TAIL + u * T, T, *mla.rope_rows(half)))
            project_vector(dve, "mla_q", take)

        def y_tile(t, lo, hi):
            return at(KT + t * D + lo, hi - lo)

        def cq_tile(t, lo, hi):
            return at(CQ + t * 640 + lo, hi - lo)

        @block.tensor
        def _(pe):
            setup_tensor(pe)
            norm_tensor(pe, 0, 0, D)
            wait_normed(pe, 0)
            for name in ("nsa_q", "nsa_k", "nsa_v"):
                project_tensor(pe, name)
            project_tensor(pe, "nsa_gate")
            project_tensor(pe, "nsa_z")
            finish("pe", pe)
            compress_tensor(pe)
            finish("pe", pe)
            attend_tensor(pe, nsa, 0)
            attend_tensor(pe, nsa, 1, first=False)
            finish("pe", pe)
            project_tensor(pe, "nsa_out", nth_output=0)
            finish("pe", pe)
            norm_tensor(pe, 2, 0, D)
            wait_normed(pe, 2)
            for name in ("diff_q", "diff_k", "diff_v", "diff_z"):
                project_tensor(pe, name)
            finish("pe", pe)
            attend_tensor(pe, diff)
            finish("pe", pe)
            subln_tensor(pe)
            project_tensor(pe, "diff_out", nth_output=1)
            finish("pe", pe)
            norm_tensor(pe, 4, 0, D)
            wait_normed(pe, 4)
            for name in ("na_q", "na_k", "na_v", "na_z"):
                project_tensor(pe, name)
            finish("pe", pe)
            attend_tensor(pe, na)
            finish("pe", pe)
            project_tensor(pe, "na_out", nth_output=2)
            finish("pe", pe)
            ple_tensor(pe, 0)
            finish("pe", pe)
            project_tensor(pe, "ple0_proj")
            finish("pe", pe)
            norm_tensor(pe, 5, 0, D)
            wait_normed(pe, 5)
            project_tensor(pe, "ple0_gate")
            finish("pe", pe)
            norm_tensor(pe, 6, 0, D)
            wait_normed(pe, 6)
            project_tensor(pe, "mla_cq")
            project_tensor(pe, "mla_ckv")
            project_tensor(pe, "mla_rope", banks=1)
            project_tensor(pe, "mla_z")
            finish("pe", pe)
            norm_tensor(pe, 7, LXN, 640)
            wait_normed(pe, 7)
            for name in ("mla_q", "mla_k", "mla_v"):
                project_tensor(pe, name)
            finish("pe", pe)
            attend_tensor(pe, mla)
            finish("pe", pe)
            project_tensor(pe, "mla_out", nth_output=3)
            finish("pe", pe)
            ple_tensor(pe, 1)
            finish("pe", pe)
            project_tensor(pe, "ple1_proj")
            finish("pe", pe)
            norm_tensor(pe, 8, 0, D)
            wait_normed(pe, 8)
            project_tensor(pe, "ple1_gate")
            finish("pe", pe)

        @block.scalar
        def _(act):
            setup_scalar(act)
            norm_scalar(act, 0, x_tile)
            load_strips(act, 0)
            load_strips(act, 1)
            project_scalar(act, "nsa_q")
            load_strips(act, 2)
            load_strips(act, 3)
            project_scalar(act, "nsa_k")
            project_scalar(act, "nsa_v")
            project_scalar(act, "nsa_gate", lambda i, j: nc.scalar.activation(
                gate[:, j * 48:(j + 1) * 48], bank(j, 48), ACT.Sigmoid))
            act.wait_ge(strip_used, 4 * 4)
            project_scalar(act, "nsa_z", silu_features(Z), ends=True)
            finish("act", act, "nsa_z")
            compress_scalar(act)
            finish("act", act)
            attend_scalar(act, nsa, 0)
            attend_scalar(act, nsa, 1)
            finish("act", act)
            split_output_scalar(act, Z, 0)
            project_scalar(act, "nsa_out", ends=True)
            finish("act", act, "nsa_out")
            norm_scalar(act, 1, y_tile)
            norm_scalar(act, 2, x_tile)
            for name in ("diff_q", "diff_k", "diff_v"):
                project_scalar(act, name)
            project_scalar(act, "diff_z", silu_features(Z), ends=True)
            finish("act", act, "diff_z")
            attend_scalar(act, diff)
            finish("act", act)
            subln_scalar(act)
            split_output_scalar(act, Z, 1)
            project_scalar(act, "diff_out", ends=True)
            finish("act", act, "diff_out")
            norm_scalar(act, 3, y_tile)
            norm_scalar(act, 4, x_tile)
            act.wait_ge(rpb_out, 16)
            act.dma_start(at(na.MASK, GRID_W), A["colmask"]).then_inc(small_in, 16)
            for name in ("na_q", "na_k", "na_v"):
                project_scalar(act, name)
            project_scalar(act, "na_z", silu_features(Z), ends=True)
            finish("act", act, "na_z")
            attend_scalar(act, na)
            finish("act", act)
            split_output_scalar(act, Z, 2)
            project_scalar(act, "na_out", ends=True)
            finish("act", act, "na_out")
            ple_scalar(act, 0)
            finish("act", act)
            project_scalar(act, "ple0_proj", ends=True)
            finish("act", act, "ple0_proj")
            norm_scalar(act, 5, x_tile)
            gate_scalar(act, 0)
            finish("act", act, "ple0_gate")
            norm_scalar(act, 6, x_tile)
            load_rope(act)
            for name in ("mla_cq", "mla_ckv", "mla_rope"):
                project_scalar(act, name)
            project_scalar(act, "mla_z", silu_features(Z), ends=True)
            finish("act", act, "mla_z")
            norm_scalar(act, 7, cq_tile, LXN, 640)
            for name in ("mla_q", "mla_k", "mla_v"):
                project_scalar(act, name)
            finish("act", act)
            attend_scalar(act, mla)
            finish("act", act)
            split_output_scalar(act, Z, 3)
            project_scalar(act, "mla_out", ends=True)
            finish("act", act, "mla_out")
            ple_scalar(act, 1)
            finish("act", act)
            project_scalar(act, "ple1_proj", ends=True)
            finish("act", act, "ple1_proj")
            norm_scalar(act, 8, x_tile)
            gate_scalar(act, 1)
            finish("act", act)
            squares_scalar(act, 9, x_tile, 0, D)
            xn0 = NT * norm_base(9)[0]
            for t in range(NT):
                act.wait_ge(xn_done, xn0 + t + 1)
                act.dma_start(out[t * P:(t + 1) * P, :], at(t * D, D)).then_inc(out_written, 16)
            act.wait_ge(out_written, 16 * NT)

        @block.gpsimd
        def _(pool):
            norm_pool(pool, 0)
            setup_pool(pool)
            for name in ("nsa_q", "nsa_k", "nsa_v", "nsa_gate", "nsa_z"):
                project_pool(pool, name)
            project_pool(pool, "nsa_cmp")
            attend_pool(pool, nsa, 0)
            attend_pool(pool, nsa, 1)
            project_pool(pool, "nsa_out")
            norm_pool(pool, 1)
            norm_pool(pool, 2)
            for name in ("diff_q", "diff_k", "diff_v", "diff_z"):
                project_pool(pool, name)
            attend_pool(pool, diff)
            subln_pool(pool)
            project_pool(pool, "diff_out")
            norm_pool(pool, 3)
            norm_pool(pool, 4)
            for name in ("na_q", "na_k", "na_v", "na_z"):
                project_pool(pool, name)
            attend_pool(pool, na)
            project_pool(pool, "na_out")
            norm_pool(pool, 5)
            project_pool(pool, "ple0_proj")
            project_pool(pool, "ple0_gate")
            norm_pool(pool, 6)
            for name in ("mla_cq", "mla_ckv", "mla_rope", "mla_z"):
                project_pool(pool, name)
            norm_pool(pool, 7)
            for name in ("mla_q", "mla_k", "mla_v"):
                project_pool(pool, name)
            attend_pool(pool, mla)
            project_pool(pool, "mla_out")
            norm_pool(pool, 8)
            project_pool(pool, "ple1_proj")
            project_pool(pool, "ple1_gate")
            norm_pool(pool, 9)

        def post_norm(dve, k):
            norm_vector(dve, k, y_tile, 0, D)
            dve.wait_ge(xn_done, NT * norm_base(k + 1)[0])
            for t in range(NT):
                nc.vector.tensor_tensor(x_tile(t, 0, D), x_tile(t, 0, D), at(t * D, D), ALU.add).then_inc(x_added, 1)
            dve.wait_ge(x_added, NT * (k + 1) // 2)

        @block.vector
        def _(dve):
            setup_vector(dve)
            norm_vector(dve, 0, x_tile, 0, D)
            project_vector(dve, "nsa_q", to_features(QT, 0.125))
            cut_strips(dve, 0)
            cut_strips(dve, 1)
            project_vector(dve, "nsa_k", to_features(KT))
            cut_strips(dve, 2)
            cut_strips(dve, 3)
            project_vector(dve, "nsa_v", to_tokens(V, 512))
            finish("dve", dve)
            compress_vector(dve)
            finish("dve", dve)
            attend_vector(dve, nsa, 0)
            attend_vector(dve, nsa, 1, first=False)
            finish("dve", dve)
            split_output_vector(dve, Z, 0)
            project_vector(dve, "nsa_out", to_tokens(KT, D))
            finish("dve", dve)
            post_norm(dve, 1)
            norm_vector(dve, 2, x_tile, 0, D)
            project_vector(dve, "diff_q", to_features(QT, 0.125))
            project_vector(dve, "diff_k", to_features(KT))
            project_vector(dve, "diff_v", to_tokens(V, D))
            finish("dve", dve)
            attend_vector(dve, diff)
            finish("dve", dve)
            subln_vector(dve)
            split_output_vector(dve, Z, 1)
            project_vector(dve, "diff_out", to_tokens(KT, D))
            finish("dve", dve)
            post_norm(dve, 3)
            norm_vector(dve, 4, x_tile, 0, D)
            project_vector(dve, "na_q", to_features(QT, 0.125))
            project_vector(dve, "na_k", to_features(KT))
            project_vector(dve, "na_v", to_tokens(V, D))
            dve.wait_ge(small_in, 16)
            finish("dve", dve)
            attend_vector(dve, na)
            finish("dve", dve)
            split_output_vector(dve, Z, 2)
            project_vector(dve, "na_out", add_residual)
            finish("dve", dve)
            norm_sums(dve, 5, x_tile, 0, D)
            ple_vector(dve, 0)
            finish("dve", dve)
            norm_scale(dve, 5, x_tile, 0, D)
            project_vector(dve, "ple0_proj", to_tokens(PP, D))
            finish("dve", dve)
            norm_low(dve, 5)
            gate_vector(dve, 0)
            finish("dve", dve)
            norm_vector(dve, 6, x_tile, 0, D)
            project_vector(dve, "mla_cq", to_tokens(CQ, 640, Q_RANK))
            project_vector(dve, "mla_ckv", to_tokens(CQ + Q_RANK, 640, KV_RANK))
            rope_vector(dve)
            finish("dve", dve)
            norm_vector(dve, 7, cq_tile, LXN, 640)
            mla_q_vector(dve)
            project_vector(dve, "mla_k", to_features(KT))
            project_vector(dve, "mla_v", to_tokens(V, D))
            finish("dve", dve)
            attend_vector(dve, mla)
            finish("dve", dve)
            split_output_vector(dve, Z, 3)
            project_vector(dve, "mla_out", add_residual)
            finish("dve", dve)
            norm_sums(dve, 8, x_tile, 0, D)
            ple_vector(dve, 1)
            finish("dve", dve)
            norm_scale(dve, 8, x_tile, 0, D)
            project_vector(dve, "ple1_proj", to_tokens(PP, D))
            finish("dve", dve)
            norm_low(dve, 8)
            gate_vector(dve, 1)
            finish("dve", dve)
            norm_vector(dve, 9, x_tile, 0, D)


def _constants():
    n = np.arange(SPAN)
    dist = np.maximum(511 - n, 0)
    exact = BUCKETS // 2
    nf = np.maximum(dist, 1).astype(np.float32)
    large = exact + (np.log(nf / np.float32(exact)) / np.float32(np.log(128 / exact))
                     * np.float32(BUCKETS - exact)).astype(np.int32)
    bucket = np.where(dist < exact, dist, np.minimum(large, BUCKETS - 1))
    onehot = (np.arange(BUCKETS)[:, None] == bucket[None, :]).astype(np.float32)
    rowmask = np.tile(np.where(511 - n >= 0, 0.0, MASKED).astype(np.float32), (BUCKETS, 1))
    col = np.arange(GRID_W)
    start = np.clip(col - 8, 0, GRID_W - 16)
    inside = (col[None, :] >= start[:, None]) & (col[None, :] < start[:, None] + 16)
    colmask = np.tile(np.where(inside, 0.0, MASKED).astype(np.float32), (2, 1))
    inv = (1.0 / (np.float32(10000.0) ** (np.arange(0, ROPE, 2, dtype=np.float32) / np.float32(ROPE)))).astype(np.float32)
    ang = np.arange(T, dtype=np.float32)[None, :] * inv[:, None]
    cos, sin = np.cos(ang), np.sin(ang)
    rope = np.zeros((P, T), np.float32)
    rope[64:96] = np.concatenate([cos, cos])
    rope[96:128] = np.concatenate([-sin, sin])
    rope = np.concatenate([rope, rope * np.float32((64 + ROPE) ** -0.5)], axis=1)
    return dict(onehot=onehot, rowmask=rowmask, colmask=colmask, rope=rope, ident=np.eye(P, dtype=np.float32))


def _units(w, run):
    units = []
    for i in range(run["blocks"]):
        k = 0
        for nk in run["nks"]:
            part = w[k * P:(k + nk) * P, i * run["width"]:(i + 1) * run["width"]]
            u = np.zeros((P, UNIT), w.dtype)
            u[:, :nk * run["width"]] = part.reshape(nk, P, run["width"]).transpose(1, 0, 2).reshape(P, -1)
            units.append(u)
            k += nk
    return units


def _layout(inputs):
    f = {k: np.asarray(v) for k, v in inputs.items()}
    w = f["nsa_w_in"][0]
    kv = [w[:, D + 256 * n:D + 256 * (n + 1)] for n in range(6)]
    slots = np.array([(2 * gp + half) * 4 + j for gp in range(2) for j in range(4) for half in range(2)])
    cols = (slots[:, None] * 64 + np.arange(64)).reshape(-1)
    mats = {"nsa_q": w[:, :D][:, cols], "nsa_k": np.concatenate([kv[0], kv[1], kv[2], kv[4]], 1),
            "nsa_v": np.concatenate([kv[3], kv[5]], 1), "nsa_gate": w[:, 2560:2608], "nsa_z": w[:, 2608:][:, cols],
            "nsa_out": f["nsa_w_out"][0][cols]}
    for n, name in enumerate(("q", "k", "v", "z")):
        mats[f"diff_{name}"] = f["diff_w_in"][0][:, n * D:(n + 1) * D]
        mats[f"na_{name}"] = f["na_w_in_2"][0][:, n * D:(n + 1) * D]
    mats["diff_out"], mats["na_out"], mats["mla_out"] = f["diff_w_out"][0], f["na_w_out_2"][0], f["mla_w_out_2"][0]
    w = f["mla_w_in_2"][0]
    mats["mla_cq"], mats["mla_ckv"] = w[:, :Q_RANK], w[:, Q_RANK:Q_RANK + KV_RANK]
    r = w[:, Q_RANK + KV_RANK:Q_RANK + KV_RANK + ROPE]
    swapped = np.concatenate([r[:, 16:], r[:, :16]], 1)
    mats["mla_rope"] = np.concatenate([r, swapped, r, swapped], 1)
    mats["mla_z"] = w[:, Q_RANK + KV_RANK + ROPE:]
    q = f["mla_w_qb_2"][0].reshape(Q_RANK, HEADS, 96)
    mats["mla_q"] = np.concatenate([q, q[:, :, 80:96], q[:, :, 64:80]], 2).reshape(Q_RANK, HEADS * P)
    k = f["mla_w_kvb_2"][0].reshape(KV_RANK, HEADS, P)
    mats["mla_k"], mats["mla_v"] = k[:, :, :64].reshape(KV_RANK, D), k[:, :, 64:].reshape(KV_RANK, D)
    for i in range(2):
        mats[f"ple{i}_gate"], mats[f"ple{i}_proj"] = f["ple_w_gate_2"][i], f["ple_w_proj_2"][i]
    units = []
    for name, run in RUNS.items():
        if name == "nsa_cmp":
            w1 = [f[n][0].reshape(32, 64, P).transpose(1, 0, 2).reshape(64, 32 * P) for n in ("nsa_cmp_w1_k", "nsa_cmp_w1_v")]
            w1 = np.concatenate(w1, 0)
            units += [w1[:, :UNIT], w1[:, UNIT:]]
        else:
            units += _units(mats[name], run)
    latent = np.zeros(D, np.float32)
    latent[:Q_RANK], latent[Q_RANK:Q_RANK + KV_RANK] = f["mla_q_norm_2"][0], f["mla_kv_norm_2"][0]
    gains = [f["norm_pre"][0], f["norm_post"][0], f["norm_pre"][1], f["norm_post"][1], f["norm_g_2"][0],
             f["ple_norm_2"][0], f["norm_g_2"][1], latent, f["ple_norm_2"][1], f["final_norm_2"]]
    rpb = np.zeros((1, RPB_LEN), np.float32)
    rpb[0, RPB_PAD:-RPB_PAD] = f["na_rpb_2"][0].reshape(-1)
    twice = lambda a: np.concatenate([a, a], 0)
    data = dict(
        x=f["x"][0], weights=np.stack(units), gains=np.stack(gains),
        subln=f["diff_subln"][0].reshape(DIFF_HEADS, P).T,
        compress=np.concatenate([twice(f["nsa_cmp_w2_k"][0].T).T, f["nsa_cmp_w2_v"][0],
                                 twice(f["nsa_cmp_pe_k"][0].T), twice(f["nsa_cmp_pe_v"][0].T)], 1),
        lambdas=np.concatenate([f[f"diff_lambda_{n}"] for n in ("q1", "k1", "q2", "k2")], 1), rpb=rpb, p=f["p_2"][:, 0])
    data.update(_constants())
    data["bias"] = np.concatenate([data.pop("onehot"), f["rel_bias_table"], data.pop("rowmask")], 1)
    return {k: np.ascontiguousarray(v) for k, v in data.items()}


def kernel(**inputs):
    import concourse.bacc as bacc
    from concourse.bass_utils import run_bass_kernel_spmd

    data = _layout(inputs)
    nc = bacc.Bacc("TRN2", target_bir_lowering=False, num_devices=1)
    aps = {k: nc.dram_tensor(f"in_{k}", v.shape, F32, kind="ExternalInput").ap() for k, v in data.items()}
    out = nc.dram_tensor("out_x", (T, D), F32, kind="ExternalOutput").ap()
    _program(nc, aps, out)
    r = run_bass_kernel_spmd(nc, [{f"in_{k}": v for k, v in data.items()}], core_ids=[0])
    return r.results[0]["out_x"].reshape(1, T, D)
```
